# Optimizing a Trainium2 kernel written in Bass

```python
import jax, jax.numpy as jnp
from jax import lax
import numpy as np

D_MODEL = 1024
BATCH = 1
SEQ = 512
DEPTH = 2

N_A_LAYERS = DEPTH // 2
N_B_LAYERS = DEPTH - N_A_LAYERS
EPS = 1e-6

CHUNK = 128
A_WIDTH = 2 * D_MODEL
A_GROUP_WIDTH = 256
A_GROUPS = A_WIDTH // A_GROUP_WIDTH

HEAD_DIM = 128
DILATED_GROUPS = ((128, 1), (512, 4), (2048, 16))
N_GROUPS = len(DILATED_GROUPS)
Q_HEADS_PER_GROUP = D_MODEL // HEAD_DIM
KV_HEADS_PER_GROUP = 2
Q_PER_KV = Q_HEADS_PER_GROUP // KV_HEADS_PER_GROUP
N_Q_HEADS = N_GROUPS * Q_HEADS_PER_GROUP
N_KV_HEADS = N_GROUPS * KV_HEADS_PER_GROUP
B_WIDTH = Q_HEADS_PER_GROUP * HEAD_DIM
BAND = 128


def rms_norm(x, g):
    xf = x.astype(jnp.float32)
    y = xf * lax.rsqrt(jnp.mean(xf * xf, axis=-1, keepdims=True) + EPS)
    return (y * g.astype(jnp.float32)).astype(x.dtype)

def ada_mod(c, w, b, n):
    h = jax.nn.silu(c) @ w + b
    return jnp.split(h[:, None, :], n, axis=-1)

def alibi_slopes():
    h = jnp.arange(1, N_Q_HEADS + 1, dtype=jnp.float32)
    return jnp.exp2(-8.0 * h / N_Q_HEADS)

def to_dilated(t, d):
    b, s = t.shape[:2]
    rest = t.shape[2:]
    span = d * BAND
    sp = -(-s // span) * span
    t = jnp.pad(t, [(0, 0), (0, sp - s)] + [(0, 0)] * len(rest))
    t = t.reshape((b, sp // d, d) + rest)
    t = jnp.swapaxes(t, 1, 2)
    return t.reshape((b, d, sp // span, BAND) + rest)

def from_dilated(t, s):
    b, d, nb = t.shape[:3]
    rest = t.shape[4:]
    t = t.reshape((b, d, nb * BAND) + rest)
    t = jnp.swapaxes(t, 1, 2)
    return t.reshape((b, nb * BAND * d) + rest)[:, :s]

def band_keys(t):
    prev = jnp.pad(t[:, :, :-1], [(0, 0), (0, 0), (1, 0)] + [(0, 0)] * 3)
    return jnp.concatenate([prev, t], axis=3)

def gmlp_layer(x, c, ada_w, ada_b, norm_g, w_in, sgu_g, w_s, b_s, w_out):
    bsz, s, _ = x.shape
    shift, scale, gate = ada_mod(c, ada_w, ada_b, 3)
    h = rms_norm(x, norm_g) * (1 + scale) + shift
    u, v, z = jnp.split(h @ w_in, 3, axis=-1)
    u = jax.nn.gelu(u)
    v = rms_norm(jax.nn.gelu(v), sgu_g)
    v = v.reshape(bsz, s // CHUNK, CHUNK, A_GROUPS, A_GROUP_WIDTH)
    w_causal = jnp.tril(w_s)
    mixed = jnp.einsum('gts,bcsge->bctge', w_causal, v) + b_s.T[None, None, :, :, None]
    y = u * mixed.reshape(bsz, s, A_WIDTH) * jax.nn.silu(z)
    return x + gate * (y @ w_out)

def shared_kv(x, c, ada_w, ada_b, norm_g, w_kv, k_norm_g):
    bsz, s, _ = x.shape
    shift, scale = ada_mod(c, ada_w, ada_b, 2)
    h = rms_norm(x, norm_g) * (1 + scale) + shift
    k, v = jnp.split(h @ w_kv, 2, axis=-1)
    k = rms_norm(k.reshape(bsz, s, N_KV_HEADS, HEAD_DIM), k_norm_g)
    v = v.reshape(bsz, s, N_KV_HEADS, HEAD_DIM)
    groups = []
    for g, (window, d) in enumerate(DILATED_GROUPS):
        hs = slice(g * KV_HEADS_PER_GROUP, (g + 1) * KV_HEADS_PER_GROUP)
        groups.append((band_keys(to_dilated(k[:, :, hs], d)),
                       band_keys(to_dilated(v[:, :, hs], d))))
    return groups

def dilated_group_attn(q, kb, vb, slopes, window, d):
    s = q.shape[1]
    ql = to_dilated(q, d)
    bsz, _, nb = ql.shape[:3]
    ql = ql.reshape(bsz, d, nb, BAND, KV_HEADS_PER_GROUP, Q_PER_KV, HEAD_DIM)
    sc = jnp.einsum('brnikgh,brnjkh->brnkgij', ql, kb, preferred_element_type=jnp.float32)
    i = jnp.arange(BAND)[:, None]
    j = jnp.arange(2 * BAND)[None, :]
    dq = BAND + i - j
    key_idx = (jnp.arange(nb)[:, None, None] - 1) * BAND + j
    valid = (dq >= 0) & (dq <= window // d) & (key_idx >= 0)
    bias = -slopes.astype(jnp.float32).reshape(KV_HEADS_PER_GROUP, Q_PER_KV)[:, :, None, None] \
        * (d * dq).astype(jnp.float32)
    sc = jnp.where(valid[:, None, None], sc + bias, -jnp.inf)
    m = jnp.max(sc, axis=-1, keepdims=True)
    p = jnp.exp(sc - m)
    l = jnp.sum(p, axis=-1, keepdims=True)
    o = jnp.einsum('brnkgij,brnjkh->brnikgh', p / l, vb.astype(jnp.float32))
    lse = jnp.moveaxis((m + jnp.log(l))[..., 0], -1, 3)
    o = from_dilated(o.reshape(bsz, d, nb, BAND, Q_HEADS_PER_GROUP, HEAD_DIM), s)
    lse = from_dilated(lse.reshape(bsz, d, nb, BAND, Q_HEADS_PER_GROUP), s)
    return o, lse

def dilated_layer(x, c, kv_groups, ada_w, ada_b, norm_g, w_in, q_norm_g, w_out):
    bsz, s, _ = x.shape
    shift, scale, gate = ada_mod(c, ada_w, ada_b, 3)
    h = rms_norm(x, norm_g) * (1 + scale) + shift
    qz = h @ w_in
    q = qz[..., :N_Q_HEADS * HEAD_DIM].reshape(bsz, s, N_Q_HEADS, HEAD_DIM)
    z = qz[..., N_Q_HEADS * HEAD_DIM:]
    q = rms_norm(q, q_norm_g) * (HEAD_DIM ** -0.5)
    slopes = alibi_slopes()
    outs, lses = [], []
    for g, (window, d) in enumerate(DILATED_GROUPS):
        hs = slice(g * Q_HEADS_PER_GROUP, (g + 1) * Q_HEADS_PER_GROUP)
        kb, vb = kv_groups[g]
        o, lse = dilated_group_attn(q[:, :, hs], kb, vb, slopes[hs], window, d)
        outs.append(o)
        lses.append(lse)
    alpha = jax.nn.softmax(jnp.stack(lses), axis=0)
    o = jnp.sum(alpha[..., None] * jnp.stack(outs), axis=0).astype(x.dtype)
    y = o.reshape(bsz, s, B_WIDTH) * jax.nn.silu(z)
    return x + gate * (y @ w_out)

def first_inputs(seed: int = 0) -> dict:
    key = jax.random.key(seed)
    ks = jax.random.split(key, 24)
    nrm = lambda k, shape, sc: jax.random.normal(k, shape, jnp.float32) * sc
    D = D_MODEL
    return {
        "x": nrm(ks[0], (BATCH, SEQ, D), 1.0),
        "c": nrm(ks[1], (BATCH, D), 1.0),
        "a_ada_w": nrm(ks[2], (N_A_LAYERS, D, 3 * D), 0.5 * D ** -0.5),
        "a_ada_b": nrm(ks[3], (N_A_LAYERS, 3 * D), 0.01),
        "a_norm_g": 1.0 + nrm(ks[4], (N_A_LAYERS, D), 0.05),
        "a_w_in": nrm(ks[5], (N_A_LAYERS, D, 3 * A_WIDTH), D ** -0.5),
        "a_sgu_g": 1.0 + nrm(ks[6], (N_A_LAYERS, A_WIDTH), 0.05),
        "a_w_spatial": nrm(ks[7], (N_A_LAYERS, A_GROUPS, CHUNK, CHUNK), 0.5 * CHUNK ** -0.5),
        "a_b_spatial": 1.0 + nrm(ks[8], (N_A_LAYERS, A_GROUPS, CHUNK), 0.01),
        "a_w_out": nrm(ks[9], (N_A_LAYERS, A_WIDTH, D), A_WIDTH ** -0.5),
        "kv_ada_w": nrm(ks[10], (D, 2 * D), 0.5 * D ** -0.5),
        "kv_ada_b": nrm(ks[11], (2 * D,), 0.01),
        "kv_norm_g": 1.0 + nrm(ks[12], (D,), 0.05),
        "w_kv": nrm(ks[13], (D, 2 * N_KV_HEADS * HEAD_DIM), D ** -0.5),
        "k_norm_g": 1.0 + nrm(ks[14], (HEAD_DIM,), 0.05),
        "b_ada_w": nrm(ks[15], (N_B_LAYERS, D, 3 * D), 0.5 * D ** -0.5),
        "b_ada_b": nrm(ks[16], (N_B_LAYERS, 3 * D), 0.01),
        "b_norm_g": 1.0 + nrm(ks[17], (N_B_LAYERS, D), 0.05),
        "b_w_in": nrm(ks[18], (N_B_LAYERS, D, N_Q_HEADS * HEAD_DIM + B_WIDTH), D ** -0.5),
        "b_q_norm_g": 1.0 + nrm(ks[19], (N_B_LAYERS, HEAD_DIM), 0.05),
        "b_w_out": nrm(ks[20], (N_B_LAYERS, B_WIDTH, D), B_WIDTH ** -0.5),
    }

def first_block(x, c, a_ada_w, a_ada_b, a_norm_g, a_w_in, a_sgu_g, a_w_spatial, a_b_spatial,
              a_w_out, kv_ada_w, kv_ada_b, kv_norm_g, w_kv, k_norm_g, b_ada_w, b_ada_b,
              b_norm_g, b_w_in, b_q_norm_g, b_w_out):
    kv_groups = None
    for layer in range(DEPTH):
        if layer < N_A_LAYERS:
            x = gmlp_layer(x, c, a_ada_w[layer], a_ada_b[layer], a_norm_g[layer], a_w_in[layer],
                           a_sgu_g[layer], a_w_spatial[layer], a_b_spatial[layer], a_w_out[layer])
        else:
            if layer == N_A_LAYERS:
                kv_groups = shared_kv(x, c, kv_ada_w, kv_ada_b, kv_norm_g, w_kv, k_norm_g)
            lb = layer - N_A_LAYERS
            x = dilated_layer(x, c, kv_groups, b_ada_w[lb], b_ada_b[lb], b_norm_g[lb], b_w_in[lb],
                              b_q_norm_g[lb], b_w_out[lb])
    return x


DEPTH_2 = 1

CHUNK_2 = 64
LEFT_CHUNKS = 8
BAND_2 = (LEFT_CHUNKS + 1) * CHUNK_2
N_HEADS = 8
HEAD_DIM_2 = 64
D_ATTN = N_HEADS * HEAD_DIM_2
REL_CLIP = 128
D_CONV = 512
CONV_WIDTH = 31
N_BRANCH = 2
D_IN = 3 * D_ATTN + 2 * D_CONV + N_BRANCH * D_MODEL
D_FF = 2816


def rms_norm_2(x, g):
    xf = x.astype(jnp.float32)
    y = xf * lax.rsqrt(jnp.mean(xf * xf, axis=-1, keepdims=True) + EPS)
    return (y * g.astype(jnp.float32)).astype(x.dtype)

def layer_norm(x, g, b):
    xf = x.astype(jnp.float32)
    mu = jnp.mean(xf, axis=-1, keepdims=True)
    var = jnp.mean(jnp.square(xf - mu), axis=-1, keepdims=True)
    y = (xf - mu) * lax.rsqrt(var + EPS)
    return (y * g.astype(jnp.float32) + b.astype(jnp.float32)).astype(x.dtype)

def swiglu(x, w_gate, w_up, w_down):
    return (jax.nn.silu(x @ w_gate) * (x @ w_up)) @ w_down

def chunked_attention(q, k, v, rel_table):
    B, S, H, Dh = q.shape
    nc = S // CHUNK_2
    qc = q.reshape(B, nc, CHUNK_2, H, Dh)
    pad = ((0, 0), (LEFT_CHUNKS, 0), (0, 0), (0, 0), (0, 0))
    kp = jnp.pad(k.reshape(B, nc, CHUNK_2, H, Dh), pad)
    vp = jnp.pad(v.reshape(B, nc, CHUNK_2, H, Dh), pad)
    k_band = jnp.concatenate([kp[:, j:j + nc] for j in range(LEFT_CHUNKS + 1)], axis=2)
    v_band = jnp.concatenate([vp[:, j:j + nc] for j in range(LEFT_CHUNKS + 1)], axis=2)
    scores = jnp.einsum('bnqhd,bnkhd->bnhqk', qc, k_band).astype(jnp.float32) * (HEAD_DIM_2 ** -0.5)
    qi = jnp.arange(CHUNK_2)[:, None]
    kj = jnp.arange(BAND_2)[None, :]
    dist = qi + LEFT_CHUNKS * CHUNK_2 - kj
    idx = jnp.clip(dist, -REL_CLIP, REL_CLIP) + REL_CLIP
    bias = rel_table.astype(jnp.float32)[:, idx]
    scores = scores + bias[None, None]
    key_chunk = jnp.arange(nc)[:, None] + (jnp.arange(BAND_2) // CHUNK_2)[None, :] - LEFT_CHUNKS
    valid = (key_chunk >= 0)[None, :, None, None, :]
    scores = jnp.where(valid, scores, jnp.float32(-1e30))
    p = jax.nn.softmax(scores, axis=-1).astype(v.dtype)
    out = jnp.einsum('bnhqk,bnkhd->bnqhd', p, v_band)
    return out.reshape(B, S, H * Dh)

def conv_module(c_in, glu_bias, dw_w, dw_b, ln_g, ln_b, w_out):
    c = c_in + glu_bias
    c = c[..., :D_CONV] * jax.nn.sigmoid(c[..., D_CONV:])
    c = lax.conv_general_dilated(
        c, dw_w.astype(c.dtype), window_strides=(1,), padding=((CONV_WIDTH - 1, 0),),
        dimension_numbers=('NWC', 'WIO', 'NWC'), feature_group_count=D_CONV) + dw_b
    c = jax.nn.silu(layer_norm(c, ln_g, ln_b))
    return c @ w_out

def hybrid_mixer(u, w_in, gate_bias, rel_table, w_attn_out, conv_glu_bias, conv_dw_w,
                 conv_dw_b, conv_ln_g, conv_ln_b, conv_w_out, w_out):
    B, S, _ = u.shape
    proj = u @ w_in
    q, k, v, c_in, g = jnp.split(
        proj, [D_ATTN, 2 * D_ATTN, 3 * D_ATTN, 3 * D_ATTN + 2 * D_CONV], axis=-1)
    shp = (B, S, N_HEADS, HEAD_DIM_2)
    y_a = chunked_attention(q.reshape(shp), k.reshape(shp), v.reshape(shp), rel_table) @ w_attn_out
    y_b = conv_module(c_in, conv_glu_bias, conv_dw_w, conv_dw_b, conv_ln_g, conv_ln_b, conv_w_out)
    gates = jax.nn.sigmoid(g + gate_bias)
    merged = gates[..., :D_MODEL] * y_a + gates[..., D_MODEL:] * y_b
    return merged @ w_out

def second_inputs(seed: int = 0) -> dict:
    key = jax.random.key(seed)
    ks = jax.random.split(key, 32)
    L, D = DEPTH_2, D_MODEL

    def w(k, shape, fan_in):
        return jax.random.normal(k, shape, jnp.float32) * (fan_in ** -0.5)

    def gain(k, shape):
        return 1.0 + 0.05 * jax.random.normal(k, shape, jnp.float32)

    def small(k, shape, s=0.02):
        return s * jax.random.normal(k, shape, jnp.float32)

    return {
        "x": jax.random.normal(ks[0], (BATCH, SEQ, D), jnp.float32),
        "ffn1_norm_pre": gain(ks[1], (L, D)),
        "ffn1_w_gate": w(ks[2], (L, D, D_FF), D),
        "ffn1_w_up": w(ks[3], (L, D, D_FF), D),
        "ffn1_w_down": w(ks[4], (L, D_FF, D), D_FF),
        "ffn1_norm_post": gain(ks[5], (L, D)),
        "mix_norm_pre": gain(ks[6], (L, D)),
        "w_in": w(ks[7], (L, D, D_IN), D),
        "gate_bias": small(ks[8], (L, N_BRANCH * D), 0.1),
        "rel_table": small(ks[9], (L, N_HEADS, 2 * REL_CLIP + 1), 0.5),
        "w_attn_out": w(ks[10], (L, D_ATTN, D), D_ATTN),
        "conv_glu_bias": small(ks[11], (L, 2 * D_CONV)),
        "conv_dw_w": w(ks[12], (L, CONV_WIDTH, 1, D_CONV), CONV_WIDTH),
        "conv_dw_b": small(ks[13], (L, D_CONV)),
        "conv_ln_g": gain(ks[14], (L, D_CONV)),
        "conv_ln_b": small(ks[15], (L, D_CONV)),
        "conv_w_out": w(ks[16], (L, D_CONV, D), D_CONV),
        "w_out": w(ks[17], (L, D, D), D),
        "mix_norm_post": gain(ks[18], (L, D)),
        "ffn2_norm_pre": gain(ks[19], (L, D)),
        "ffn2_w_gate": w(ks[20], (L, D, D_FF), D),
        "ffn2_w_up": w(ks[21], (L, D, D_FF), D),
        "ffn2_w_down": w(ks[22], (L, D_FF, D), D_FF),
        "ffn2_norm_post": gain(ks[23], (L, D)),
    }

def second_block(x, ffn1_norm_pre, ffn1_w_gate, ffn1_w_up, ffn1_w_down, ffn1_norm_post,
              mix_norm_pre, w_in, gate_bias, rel_table, w_attn_out, conv_glu_bias,
              conv_dw_w, conv_dw_b, conv_ln_g, conv_ln_b, conv_w_out, w_out, mix_norm_post,
              ffn2_norm_pre, ffn2_w_gate, ffn2_w_up, ffn2_w_down, ffn2_norm_post):
    h = x
    for l in range(DEPTH_2):
        f = swiglu(rms_norm_2(h, ffn1_norm_pre[l]), ffn1_w_gate[l], ffn1_w_up[l], ffn1_w_down[l])
        h = h + 0.5 * rms_norm_2(f, ffn1_norm_post[l])
        m = hybrid_mixer(rms_norm_2(h, mix_norm_pre[l]), w_in[l], gate_bias[l], rel_table[l],
                         w_attn_out[l], conv_glu_bias[l], conv_dw_w[l], conv_dw_b[l],
                         conv_ln_g[l], conv_ln_b[l], conv_w_out[l], w_out[l])
        h = h + rms_norm_2(m, mix_norm_post[l])
        f = swiglu(rms_norm_2(h, ffn2_norm_pre[l]), ffn2_w_gate[l], ffn2_w_up[l], ffn2_w_down[l])
        h = h + 0.5 * rms_norm_2(f, ffn2_norm_post[l])
    return h


def setup_inputs(seed=0):
    out = dict(first_inputs(seed))
    for name, value in second_inputs(seed + 1).items():
        if name != "x":
            out[name + "_2"] = value
    return out


def reference(
    x, c, a_ada_w, a_ada_b, a_norm_g, a_w_in, a_sgu_g, a_w_spatial, a_b_spatial, a_w_out,
    kv_ada_w, kv_ada_b, kv_norm_g, w_kv, k_norm_g, b_ada_w, b_ada_b, b_norm_g, b_w_in,
    b_q_norm_g, b_w_out, ffn1_norm_pre_2, ffn1_w_gate_2, ffn1_w_up_2, ffn1_w_down_2,
    ffn1_norm_post_2, mix_norm_pre_2, w_in_2, gate_bias_2, rel_table_2, w_attn_out_2,
    conv_glu_bias_2, conv_dw_w_2, conv_dw_b_2, conv_ln_g_2, conv_ln_b_2, conv_w_out_2, w_out_2,
    mix_norm_post_2, ffn2_norm_pre_2, ffn2_w_gate_2, ffn2_w_up_2, ffn2_w_down_2,
    ffn2_norm_post_2,
):
    x = first_block(
        x, c, a_ada_w, a_ada_b, a_norm_g, a_w_in, a_sgu_g, a_w_spatial, a_b_spatial, a_w_out,
        kv_ada_w, kv_ada_b, kv_norm_g, w_kv, k_norm_g, b_ada_w, b_ada_b, b_norm_g, b_w_in,
        b_q_norm_g, b_w_out,
    )
    return second_block(
        x, ffn1_norm_pre_2, ffn1_w_gate_2, ffn1_w_up_2, ffn1_w_down_2, ffn1_norm_post_2,
        mix_norm_pre_2, w_in_2, gate_bias_2, rel_table_2, w_attn_out_2, conv_glu_bias_2,
        conv_dw_w_2, conv_dw_b_2, conv_ln_g_2, conv_ln_b_2, conv_w_out_2, w_out_2,
        mix_norm_post_2, ffn2_norm_pre_2, ffn2_w_gate_2, ffn2_w_up_2, ffn2_w_down_2,
        ffn2_norm_post_2,
    )


_drawn_inputs = setup_inputs


def setup_inputs(seed=0):
    import zlib

    import numpy as np

    out = dict(_drawn_inputs(seed))
    spreads = {}
    factors = {'a_ada_b': 7.431,
     'a_norm_g': 3.946,
     'a_sgu_g': 8.0,
     'a_b_spatial': 8.0,
     'kv_ada_b': 8.0,
     'kv_norm_g': 8.0,
     'k_norm_g': 8.0,
     'b_ada_b': 8.0,
     'b_norm_g': 8.0,
     'b_q_norm_g': 8.0,
     'conv_glu_bias_2': 200.0,
     'conv_ln_b_2': 200.0,
     'ffn2_norm_post_2': 29.016,
     'ffn1_norm_pre_2': 8.0,
     'ffn1_w_gate_2': 3.333,
     'ffn1_w_up_2': 3.123,
     'ffn1_w_down_2': 3.135,
     'ffn1_norm_post_2': 8.0,
     'mix_norm_pre_2': 8.0,
     'gate_bias_2': 8.0,
     'rel_table_2': 8.0,
     'w_attn_out_2': 3.715,
     'conv_dw_b_2': 64.0,
     'conv_ln_g_2': 64.0,
     'mix_norm_post_2': 29.482,
     'ffn2_norm_pre_2': 8.0}
    for name, (base, spread) in spreads.items():
        noise = np.random.default_rng([zlib.crc32(name.encode()), seed]).standard_normal(out[name].shape)
        drawn = base * np.exp(spread * noise) if base else spread * noise
        out[name] = __import__('jax').numpy.asarray(drawn.astype(out[name].dtype))
    for name, factor in factors.items():
        out[name] = (out[name] * factor).astype(out[name].dtype)
    return out
```

```python
from contextlib import ExitStack

import numpy as np

import concourse.bass as bass
from concourse import mybir

ALU = mybir.AluOpType
ACT = mybir.ActivationFunctionType
AX = mybir.AxisListType.X
F32 = mybir.dt.float32
F32R = mybir.dt.float32r

P = 128
D = 1024
KD = D // P
T = 512
TT = T // P
EPS = 1e-6
AW = 2048
AG = 8
AN = AW // P
NQ = 8
NKV = 2
GROUPS = 3
DILATION = (1, 4, 16)
KVH = GROUPS * NKV
FFA, FFB = 12, 10
FF = (FFA + FFB) * P
H2, HD2 = 8, 64
CH2 = 64
CONV = 31
CT = 4
REL = 257
SLOT = 16 * P
MASKED = -1e30

PHASES = [("v", 8, 16), ("uz", 16, 32), ("ao", 8, 8), ("kv", 6, 12), ("qz", 16, 32), ("bo", 4, 8),
          ("gu1a", FFA, 2 * FFA), ("dn1a", 8, 8), ("gu1b", FFB, 2 * FFB), ("dn1b", 8, 8),
          ("mix", 10, 20), ("gates", 8, 16), ("outs", 4, 16), ("wo", 4, 8),
          ("gu2a", FFA, 2 * FFA), ("dn2a", 8, 8), ("gu2b", FFB, 2 * FFB), ("dn2b", 8, 8)]
C0, T0 = {}, {}
_c = _t = 0
for _name, _nc, _nt in PHASES:
    C0[_name], T0[_name] = _c, _t
    _c, _t = _c + _nc, _t + _nt
TILES_END = {name: T0[name] + nt for name, _, nt in PHASES}

ROWS_A = [("a_ada_b", 24), ("kv_ada_b", 16), ("b_ada_b", 24), ("a_norm_g", 8), ("a_sgu_g", 16),
          ("kv_norm_g", 8), ("b_norm_g", 8), ("k_norm_g", 1), ("b_q_norm_g", 1)]
ROWS_B = [("ffn1_norm_pre_2", 8), ("ffn1_norm_post_2", 8), ("mix_norm_pre_2", 8), ("gate_bias_2", 16),
          ("conv_glu_bias_2", 8), ("conv_dw_b_2", 4), ("conv_ln_g_2", 4), ("conv_ln_b_2", 4),
          ("mix_norm_post_2", 8), ("ffn2_norm_pre_2", 8), ("ffn2_norm_post_2", 8)]
COL = {}
for _rows, _base in ((ROWS_A, 0), (ROWS_B, P)):
    for _name, _n in _rows:
        COL[_name] = _base
        _base += _n
COL["conv_dw_w_2"] = 2 * P


class Chain:

    def __init__(self, eng, sem):
        self.eng, self.sem, self.base, self.n, self.i, self.per = eng, sem, 0, 0, None, 0

    def done(self, ins):
        ins.then_inc(self.sem, 1)
        self.n += 1
        at = self.base + self.n
        self.eng.wait_ge(self.sem, at if self.i is None else self.i * self.per + at)

    def enter(self, i, per):
        self.base, self.n, self.i, self.per = self.base + self.n, 0, i, per

    def leave(self, count):
        assert self.n == self.per, (self.n, self.per)
        self.base, self.n, self.i = self.base + count * self.per, 0, None


DIST_AT, DIST_W = (0, 256, 768), (256, T, T)
PE_NORMS = (0, 4, 6)


def stats_before(n):
    return sum(m not in PE_NORMS for m in range(n))


ROW_DMAS = len(ROWS_A) + len(ROWS_B) + 1
ROW_COUNTS = (sum(n for _, n in ROWS_A), sum(n for _, n in ROWS_B), CONV * CT)


def seg(t, start, n):
    if isinstance(start, int):
        return t[:, start:start + n]
    return t[:, bass.ds(start, n)]


def build(nc, x, c, a_ada_w, a_ada_b, a_norm_g, a_w_in, a_sgu_g, a_w_spatial, a_b_spatial, a_w_out,
          kv_ada_w, kv_ada_b, kv_norm_g, w_kv, k_norm_g, b_ada_w, b_ada_b, b_norm_g, b_w_in,
          b_q_norm_g, b_w_out, ffn1_norm_pre_2, ffn1_w_gate_2, ffn1_w_up_2, ffn1_w_down_2,
          ffn1_norm_post_2, mix_norm_pre_2, w_in_2, gate_bias_2, rel_table_2, w_attn_out_2,
          conv_glu_bias_2, conv_dw_w_2, conv_dw_b_2, conv_ln_g_2, conv_ln_b_2, conv_w_out_2, w_out_2,
          mix_norm_post_2, ffn2_norm_pre_2, ffn2_w_gate_2, ffn2_w_up_2, ffn2_w_down_2,
          ffn2_norm_post_2, out):
    vectors = {"c": c, "a_ada_b": a_ada_b, "kv_ada_b": kv_ada_b, "b_ada_b": b_ada_b, "a_norm_g": a_norm_g,
               "a_sgu_g": a_sgu_g, "kv_norm_g": kv_norm_g, "b_norm_g": b_norm_g, "k_norm_g": k_norm_g,
               "b_q_norm_g": b_q_norm_g, "ffn1_norm_pre_2": ffn1_norm_pre_2,
               "ffn1_norm_post_2": ffn1_norm_post_2, "mix_norm_pre_2": mix_norm_pre_2,
               "gate_bias_2": gate_bias_2, "conv_glu_bias_2": conv_glu_bias_2,
               "conv_dw_b_2": conv_dw_b_2, "conv_ln_g_2": conv_ln_g_2, "conv_ln_b_2": conv_ln_b_2,
               "mix_norm_post_2": mix_norm_post_2, "ffn2_norm_pre_2": ffn2_norm_pre_2,
               "ffn2_norm_post_2": ffn2_norm_post_2}
    ctx = ExitStack()
    with ctx:
        KB = 1024
        BASE = 16512
        W0, X0, HH, HL, BH, BL, U = (BASE + k * KB for k in (0, 48, 64, 80, 96, 128, 160))
        END = 229360
        SMALL = END - 3584 - (END - 3584) % 32
        TMP = SMALL - 16 * KB
        TILE = 4 * T

        def at(name, offset, cols, dt=F32, rows=P):
            return nc.alloc_sbuf_tensor_at("s_" + name, [rows, cols], dt, offset=offset)

        raw = at("raw", W0, 2 * SLOT)
        w_high = at("w_high", W0 + 16 * KB, 2 * SLOT, F32R)
        w_low = at("w_low", W0 + 32 * KB, 2 * SLOT, F32R)
        xT = at("xT", X0, KD * T)
        h_high = at("h_high", HH, KD * T, F32R)
        h_low = at("h_low", HL, KD * T, F32R)
        b_high = at("b_high", BH, 16 * T, F32R)
        b_low = at("b_low", BL, 16 * T, F32R)
        ident = at("ident", SMALL, P)
        ones = at("ones", SMALL + 512, P)
        cols = at("cols", SMALL + 1024, 3 * P)
        ada = at("ada", SMALL + 2560, 64)
        derived = at("derived", SMALL + 2816, 64)
        slopes = at("slopes", SMALL + 3072, 24)
        tiny = at("tiny", SMALL + 3168, 96)
        acc_sq = at("acc_sq", TMP, T)
        rstd = at("rstd", TMP + TILE, T)
        sq = [at(f"sq{j}", TMP + (2 + j) * TILE, T) for j in range(2)]
        n1 = [at(f"n1{j}", TMP + (4 + j) * TILE, T) for j in range(2)]
        n2 = [at(f"n2{j}", TMP + (6 + j) * TILE, T) for j in range(2)]
        xin = at("xin", BH, TT * D)
        ada_w = [at(f"ada_w{j}", BH + 16 * KB + 4 * KB * j, D) for j in range(4)]
        ada_acc = [at(f"ada_acc{j}", U + 8 * KB + 4 * KB * j, D) for j in range(2)]
        rows = [at(f"rows{j}", BL + 512 * j, P) for j in range(3)]
        c_row = at("c_row", BL + 2 * KB, P, rows=KD)
        wsp = at("wsp", BL + 4 * KB, AG * P)
        relrow = at("relrow", BL + 8 * KB, 3 * P, rows=H2)
        junk = [at(f"junk{j}", BH + 8 * KB * j, AW) for j in range(4)]
        v_tok = at("v_tok", BL, AN * T)
        wsT = at("wsT", U, AG * P)
        bsb = at("bsb", U + 4 * KB, AG * P)
        ug = [at(f"ug{j}", U + 8 * KB + j * TILE, T) for j in range(2)]
        zs = [at(f"zs{j}", U + 12 * KB + j * TILE, T) for j in range(2)]
        y32 = [at(f"y32{j}", U + 16 * KB + j * TILE, T) for j in range(2)]
        vs = [at(f"vs{j}", U + 20 * KB + j * TILE, T) for j in range(2)]
        v_gel = [at(f"v_gel{j}", U + 16 * KB + j * TILE, T) for j in range(2)]
        ws = at("ws", U + 24 * KB, P)
        ada2_w = [at(f"ada2_w{j}", U + 4 * KB * j, D) for j in range(4)]
        ada2_acc = at("ada2_acc", U + 16 * KB, D)
        ada3_w = [at(f"ada3_w{j}", o, D) for j, o in enumerate((U + 24 * KB, TMP + 2 * TILE, BL + 24 * KB, BL + 28 * KB))]
        ada3_acc = at("ada3_acc", BL + 20 * KB, D)
        kT = at("kT", U, KVH * T)
        v1 = at("v1", U + 12 * KB, TT * KVH * P)
        k_raw = [at(f"k_raw{j}", BH + 16 * KB + j * TILE, T) for j in range(2)]
        k_sq = [at(f"k_sq{j}", BH + 20 * KB + j * TILE, T) for j in range(2)]
        k_ms = [at(f"k_ms{j}", BH + 24 * KB + j * TILE, T) for j in range(2)]
        k_rt = [at(f"k_rt{j}", BH + 28 * KB + j * TILE, T) for j in range(2)]
        v_raw = [at(f"v_raw{j}", BL + 16 * KB + j * TILE, T) for j in range(2)]
        yb = at("yb", BH, KD * T)
        pT = at("pT", BH + 16 * KB, 4 * 256 + 8 * T)
        s_row = [at(f"s_row{j}", BH + 36 * KB + j * 5 * KB, 1280) for j in range(2)]
        qT = [[at(f"qT{j}{g}", BH + 46 * KB + (3 * j + g) * TILE, T) for g in range(GROUPS)] for j in range(2)]
        bias = at("bias", BH + 58 * KB, 1280)
        q_sq = [at(f"q_sq{g}", TMP + g * TILE, T) for g in range(GROUPS)]
        zb = [at(f"zb{j}", TMP + (3 + j) * TILE, T) for j in range(2)]
        dist = at("dist", TMP + 5 * TILE, 1280)
        f = at("f", U, KD * T)
        sg = [at(f"sg{j}", U + 16 * KB + j * TILE, T) for j in range(2)]
        hd = [at(f"hd{j}", U + 20 * KB + j * TILE, T) for j in range(2)]
        q2 = at("q2", U, 4 * T)
        k2 = at("k2", U + 8 * KB, 4 * T)
        v2 = at("v2", U + 16 * KB, 4 * T)
        c_sig = [at(f"c_sig{j}", U + 24 * KB + j * TILE, T) for j in range(2)]
        PAD = CONV - 1
        GW = T + PAD
        glu = at("glu", BH + 16 * KB, CT * GW)
        s2_row = [at(f"s2_row{j}", TMP + 8448 + j * TILE, T) for j in range(2)]
        p2T = at("p2T", BH + 8 * KB, 4 * T)
        cy = at("cy", BL + 8 * KB, CT * T)
        gates = [at(f"gates{j}", o + 16 * KB, KD * T) for j, o in enumerate((BH, BL))]
        v2_raw = [at(f"v2_raw{j}", BH + j * TILE, T) for j in range(2)]
        toep = at("toep", TMP, H2 * REL)
        ln = [at(f"ln{j}", TMP + 8448 + j * TILE, T) for j in range(3)]
        branch = [at(f"branch{j}", U + j * TILE, T) for j in range(2)]
        m32 = at("m32", U + 4 * TILE, T)
        o_tok = [at(f"o_tok{j}", BH + j * 4 * KB, D) for j in range(2)]

        rel_ext = nc.dram_tensor("rel_ext", [H2, 3 * P], F32).ap()

        def bank(name):
            return ctx.enter_context(nc.psum_tensor(name, [P, 512], F32))

        acc = [bank("acc0"), bank("acc1")]
        misc = bank("misc")
        sc = [bank("sc0"), bank("sc1"), bank("sc2")]
        tr = [bank("tr"), misc]
        xb = [sc[1], sc[2], tr[0]]
        ob = bank("ob")

        def sem(name):
            return ctx.enter_context(nc.semaphore(name))

        w_landed = [sem("w_landed0"), sem("w_landed1")]
        w_high_ready, w_ready = sem("w_high_ready"), sem("w_ready")
        tile_ready = sem("tile_ready")
        evac = [sem("evac0"), sem("evac1")]
        dve_own, pool_own = sem("dve_own"), sem("pool_own")
        x_landed, rows_landed, wsp_landed, rel_landed = sem("x_landed"), sem("rows_landed"), sem("wsp_landed"), sem("rel_landed")
        rel_padded, rel_stored, toep_landed = sem("rel_padded"), sem("rel_stored"), sem("toep_landed")
        toep_free = sem("toep_free")
        bsb_landed = sem("bsb_landed")
        ada_landed = [sem(f"ada_landed{j}") for j in range(4)]
        ada_used, ada_read, ada_cols = sem("ada_used"), sem("ada_read"), sem("ada_cols")
        consts_ready = sem("consts_ready")
        rows_turned, cols_ready, c_ready = sem("rows_turned"), sem("cols_ready"), sem("c_ready")
        c_landed, c_turned = sem("c_landed"), sem("c_turned")
        x_turned, x_stored = sem("x_turned"), sem("x_stored")
        wsp_ready, wsp_turned, wsT_ready = sem("wsp_ready"), sem("wsp_turned"), sem("wsT_ready")
        sq_ready, sq_added = sem("sq_ready"), sem("sq_added")
        stat_ready, ms_ready, root_ready = sem("stat_ready"), sem("ms_ready"), sem("root_ready")
        h32_ready, h_high_ready, h_ready = sem("h32_ready"), sem("h_high_ready"), sem("h_ready")
        x_updated = sem("x_updated")
        v_turned, v_stored = sem("v_turned"), sem("v_stored")
        v_sq, v_ms, v_root = sem("v_sq"), sem("v_ms"), sem("v_root")
        vs_ready, ws_ready, mix_ready, mix_taken = sem("vs_ready"), sem("ws_ready"), sem("mix_ready"), sem("mix_taken")
        y32_ready, y_high_ready, y_ready = sem("y32_ready"), sem("y_high_ready"), sem("y_ready")
        k_stat, k_ms_ready, k_root, k_done = sem("k_stat"), sem("k_ms_ready"), sem("k_root"), sem("k_done")
        v1_turned, v1_stored = sem("v1_turned"), sem("v1_stored")
        dist_ready, bias_ready = sem("dist_ready"), sem("bias_ready")
        scores_ready, scores_taken, top_ready = sem("scores_ready"), sem("scores_taken"), sem("top_ready")
        p_ready, p_scaled, p_turned = sem("p_ready"), sem("p_scaled"), sem("p_turned")
        p_stored = [sem("p_stored0"), sem("p_stored1")]
        pv_ready, o_taken = sem("pv_ready"), sem("o_taken")
        qsq_summed, qms_ready, q_root = sem("qsq_summed"), sem("qms_ready"), sem("q_root")
        qr_ready = sem("qr_ready")
        hid_high_ready, hid_ready = sem("hid_high_ready"), sem("hid_ready")
        conv_step, gates_ready = sem("conv_step"), sem("gates_ready")
        ln_sum, ln_mean_ready, ln_sq_ready, ln_sq_summed, ln_ms, ln_root = (
            sem(n) for n in ("ln_sum", "ln_mean_ready", "ln_sq_ready", "ln_sq_summed", "ln_ms", "ln_root"))
        ln_out, conv_silu, conv_high, conv_ready = sem("ln_out"), sem("conv_silu"), sem("conv_high"), sem("conv_ready")
        v2_turned, v2_stored = sem("v2_turned"), sem("v2_stored")
        s2_ready, s2_taken, top2_ready, p2_ready, p2_scaled = (
            sem(n) for n in ("s2_ready", "s2_taken", "top2_ready", "p2_ready", "p2_scaled"))
        p2_turned, p2_stored, pv2_ready, o2_high, o2_ready = (
            sem(n) for n in ("p2_turned", "p2_stored", "pv2_ready", "o2_high", "o2_ready"))
        m32_ready, m_high, m_ready = sem("m32_ready"), sem("m_high"), sem("m_ready")
        dist_int, dist_thinned = sem("dist_int"), sem("dist_thinned")
        out_turned, out_copied = sem("out_turned"), sem("out_copied")
        out_stored = [sem(f"out_stored{b}") for b in range(2)]

        A_A, A_KV, A_B, SC_K, HG1, HG2 = 0, 8, 16, 24, 25, 33
        V_SS, V_MS, V_RT, V_R = 0, 4, 8, 12
        MX, NM, LS, LI = 16, 18, 20, 22
        Q_MS, Q_RT, Q_R = 24, 36, 48
        SHIFT_A, GATE_A, SHIFT_KV, SHIFT_B, GATE_B = 0, 16, 24, 40, 56

        def col(name, n=0):
            if isinstance(n, int):
                return cols[:, COL[name] + n:COL[name] + n + 1]
            return cols[:, bass.ds(n + COL[name], 1)]

        def kview(w):
            return w.rearrange("(k p) n -> p k n", p=P)

        W = {"a_in": kview(a_w_in[0]), "a_out": kview(a_w_out[0]), "kv": kview(w_kv), "b_in": kview(b_w_in[0]),
             "b_out": kview(b_w_out[0]), "in2": kview(w_in_2[0]), "attn": kview(w_attn_out_2[0]),
             "conv": kview(conv_w_out_2[0]), "out2": kview(w_out_2[0]),
             "g1": kview(ffn1_w_gate_2[0]), "u1": kview(ffn1_w_up_2[0]), "d1": kview(ffn1_w_down_2[0]),
             "g2": kview(ffn2_w_gate_2[0]), "u2": kview(ffn2_w_up_2[0]), "d2": kview(ffn2_w_down_2[0])}

        def wide(k, t):
            return k * 2 * P + t * P

        def paired(k, t):
            return t * 8 * P + k * P

        def tall(k, t):
            return k * P

        block = ctx.enter_context(nc.Block())

        @block.sync
        def _(sp):
            def wait_slot(q, s):
                if not isinstance(q, int) or q > 0:
                    sp.wait_ge(x_landed, 16 * TT)
                    sp.wait_ge(w_ready, 2 * q + s - 1)

            def column(n0):
                return n0 if isinstance(n0, int) else sp.snap(n0)

            def put(s, off, w, k0, nk, n0, n):
                dst = raw[:, s * SLOT + off:s * SLOT + off + nk * n].rearrange("p (k n) -> p k n", k=nk)
                src = w[:, k0:k0 + nk, n0:n0 + n] if isinstance(n0, int) else w[:, k0:k0 + nk, bass.ds(n0, n)]
                sp.dma_start(dst, src).then_inc(w_landed[s], 16)

            def chunk_wide(q, s, w, n0):
                n0 = column(n0)
                wait_slot(q, s)
                put(s, 0, w, 0, 4, n0, 2 * P)
                put(s, 8 * P, w, 4, 4, n0, 2 * P)

            def chunk_paired(q, s, wa, na, wb, nb):
                na, nb = column(na), column(nb)
                wait_slot(q, s)
                put(s, 0, wa, 0, 8, na, P)
                put(s, 8 * P, wb, 0, 8, nb, P)

            def chunk_tall(q, s, w, k0, nk, n0):
                half = nk // 2
                n0 = column(n0)
                wait_slot(q, s)
                put(s, 0, w, k0, half, n0, P)
                put(s, half * P, w, k0 + half, half, n0, P)

            def chunk_outs(q, s, n0):
                n0 = column(n0)
                wait_slot(q, s)
                put(s, 0, W["attn"], 0, 4, n0, 2 * P)
                put(s, 8 * P, W["conv"], 0, 4, n0, 2 * P)

            sp.dma_start(c_row[:, :], c[0].rearrange("(k p) -> k p", p=P)).then_inc(c_landed, 16)
            for t in range(TT):
                sp.dma_start(xin[:, t * D:(t + 1) * D], x[0, t * P:(t + 1) * P, :]).then_inc(x_landed, 16)
            for s in range(2):
                chunk_wide(0, s, W["a_in"], AW + s * 2 * P)
            n = 0
            for table, names in ((0, ROWS_A), (1, ROWS_B)):
                r = 0
                for name, k in names:
                    v = vectors[name]
                    if len(v.shape) == 2:
                        v = v[0]
                    sp.dma_start(rows[table][r:r + k, :], v.rearrange("(k p) -> k p", p=P)).then_inc(rows_landed, 16)
                    r += k
                    n += 1
            sp.dma_start(rows[2][0:CONV * CT, :],
                           conv_dw_w_2[0, :, 0, :].rearrange("t (k p) -> (t k) p", p=P)).then_inc(rows_landed, 16)
            assert n + 1 == ROW_DMAS
            sp.dma_start(wsp[:, :].rearrange("t (g s) -> t g s", g=AG),
                         a_w_spatial[0].rearrange("g t s -> t g s")).then_inc(wsp_landed, 16)
            sp.dma_start(relrow[:, 0:REL], rel_table_2[0]).then_inc(rel_landed, 16)
            sp.dma_start(bsb[:, :].rearrange("p (g t) -> p g t", g=AG),
                         a_b_spatial[0][None, :, :].broadcast_to([P, AG, P])).then_inc(bsb_landed, 16)
            sp.wait_ge(rel_padded, 1)
            sp.dma_start(rel_ext, relrow[:, :]).then_inc(rel_stored, 16)

            with sp.Fori(1, 4) as i:
                for s in range(2):
                    chunk_wide(i, s, W["a_in"], i * 512 + (AW + s * 2 * P))
            q0 = C0["uz"] // 2
            with sp.Fori(0, 8) as i:
                for s in range(2):
                    chunk_paired(i + q0, s, W["a_in"], i * 256 + s * P, W["a_in"], i * 256 + (2 * AW + s * P))
            q0 = C0["ao"] // 2
            with sp.Fori(0, 4) as i:
                for s in range(2):
                    chunk_tall(i + q0, s, W["a_out"], 0, 16, i * 256 + s * P)
            q0 = C0["kv"] // 2
            with sp.Fori(0, 3) as i:
                for s in range(2):
                    chunk_wide(i + q0, s, W["kv"], i * 512 + s * 2 * P)
            q0 = C0["qz"] // 2
            with sp.Fori(0, 8) as i:
                for s in range(2):
                    chunk_paired(i + q0, s, W["b_in"], i * P + 2 * s * D, W["b_in"], i * P + (2 * s + 1) * D)
            q0 = C0["bo"] // 2
            with sp.Fori(0, 2) as i:
                for s in range(2):
                    chunk_wide(i + q0, s, W["b_out"], i * 512 + s * 2 * P)

            def ffn(l):
                for part, k0, nk in (("a", 0, FFA), ("b", FFA, FFB)):
                    q0 = C0[f"gu{l}{part}"] // 2
                    with sp.Fori(0, nk // 2) as i:
                        for s in range(2):
                            n0 = i * 256 + (k0 + s) * P
                            chunk_paired(i + q0, s, W[f"g{l}"], n0, W[f"u{l}"], n0)
                    q0 = C0[f"dn{l}{part}"] // 2
                    with sp.Fori(0, 4) as i:
                        for s in range(2):
                            chunk_tall(i + q0, s, W[f"d{l}"], k0, nk, i * 256 + s * P)

            ffn(1)
            q0 = C0["mix"] // 2
            with sp.Fori(0, 2) as i:
                for s in range(2):
                    n0 = i * 256 + (1536 + s * P)
                    chunk_paired(i + q0, s, W["in2"], n0, W["in2"], n0 + 512)
            with sp.Fori(0, 3) as i:
                for s in range(2):
                    chunk_wide(i + (q0 + 2), s, W["in2"], i * 512 + s * 2 * P)
            sp.wait_ge(rel_stored, 16)
            sp.wait_ge(toep_free, 1)
            for h in range(H2):
                src = bass.AP(tensor=rel_ext.tensor, offset=h * 3 * P, ap=[[1, P], [1, REL]])
                sp.dma_start(toep[:, h * REL:(h + 1) * REL], src).then_inc(toep_landed, 16)
            q0 = C0["gates"] // 2
            with sp.Fori(0, 4) as i:
                for s in range(2):
                    n0 = i * 256 + (2560 + s * P)
                    chunk_paired(i + q0, s, W["in2"], n0, W["in2"], n0 + D)
            q0 = C0["outs"] // 2
            with sp.Fori(0, 2) as i:
                for s in range(2):
                    chunk_outs(i + q0, s, i * 512 + s * 2 * P)
            q0 = C0["wo"] // 2
            with sp.Fori(0, 2) as i:
                for s in range(2):
                    chunk_wide(i + q0, s, W["out2"], i * 512 + s * 2 * P)
            ffn(2)
            for t in range(TT):
                sp.wait_ge(out_copied, 2 * t + 2)
                sp.dma_start(out[0, t * P:(t + 1) * P, :], o_tok[t % 2][:, :]).then_inc(out_stored[t % 2], 16)
            for s in range(2):
                sp.wait_ge(out_stored[s], 16 * TT // 2)
            sp.wait_ge(toep_landed, 16 * H2)

        @block.gpsimd
        def _(pool):
            own = Chain(pool, pool_own)
            own.done(pool.memset(ident[:, :], 0.0))
            pool.memset(ones[:, :], 1.0).then_inc(consts_ready, 1)
            pool.affine_select(out=ident[:, :], in_=ident[:, :], compare_op=ALU.not_equal, fill=1.0, base=0,
                               pattern=[[-1, P]], channel_multiplier=1).then_inc(consts_ready, 1)
            aw = a_ada_w[0].rearrange("(k p) n -> p k n", p=P)

            def load_block(b):
                for k in range(KD):
                    m = b * KD + k
                    if m >= 4:
                        pool.wait_ge(ada_used, m - 3)
                    pool.dma_start(ada_w[m % 4][:, :], aw[:, k, b * D:(b + 1) * D]).then_inc(ada_landed[m % 4], 16)

            load_block(0)
            load_block(1)

            pool.wait_ge(wsp_landed, 16)
            pool.affine_select(out=wsp[:, :].rearrange("t (g s) -> t g s", g=AG),
                               in_=wsp[:, :].rearrange("t (g s) -> t g s", g=AG), compare_op=ALU.is_ge, fill=0.0,
                               base=0, pattern=[[0, AG], [-1, P]], channel_multiplier=1).then_inc(wsp_ready, 1)

            load_block(2)
            for g in range(GROUPS):
                for h in range(NQ):
                    n = g * NQ + h
                    own.done(pool.memset(slopes[:, n:n + 1], float(np.exp2(np.float32(-8.0 * (n + 1) / (GROUPS * NQ))))))

            pool.wait_ge(y_ready, AN)
            for w, blocks, b0 in ((kv_ada_w, 2, 3), (b_ada_w[0], 2, 5)):
                wv = w.rearrange("(k p) n -> p k n", p=P)
                with pool.Fori(0, blocks) as i:
                    for k in range(KD):
                        pool.wait_ge(ada_used, (i + b0) * KD + (k - 3))
                        pool.dma_start(ada2_w[k % 4][:, :], wv[:, k, bass.ds(i * D, D)]).then_inc(ada_landed[k % 4], 16)

            pool.wait_ge(tile_ready, TILES_END["ao"])
            pool.wait_ge(sq_added, 2 * KD)
            for k in range(KD):
                pool.wait_ge(ada_used, 7 * KD + k - 3)
                pool.dma_start(ada3_w[k % 4][:, :], wv[:, k, 2 * D:3 * D]).then_inc(ada_landed[k % 4], 16)

            pool.wait_ge(ada_used, 8 * KD)
            for g in range(GROUPS):
                off, w = DIST_AT[g], DIST_W[g]
                part = dist[:, off:off + w]
                if g == 0:
                    pool.wait_ge(h_ready, 3 * KD)
                    own.done(pool.iota(part, pattern=[[1, w]], base=P - w, channel_multiplier=-1,
                                       allow_small_or_imprecise_dtypes=True))
                    own.done(pool.affine_select(out=part, in_=part, compare_op=ALU.is_ge, fill=MASKED, base=0,
                                                pattern=[[1, w]], channel_multiplier=-1))
                else:
                    pool.iota(bias[:, off:off + w].bitcast(mybir.dt.int32), pattern=[[-1, w]], base=w - P,
                              channel_multiplier=1).then_inc(dist_int, 1)
            for g in range(GROUPS):
                off, w = DIST_AT[g], DIST_W[g]
                part = dist[:, off:off + w]
                if g == 1:
                    pool.wait_ge(dist_thinned, 2)
                pool.affine_select(out=part, in_=part, compare_op=ALU.is_ge, fill=MASKED, base=w - P,
                                   pattern=[[-1, w]], channel_multiplier=1).then_inc(dist_ready, 1)

        @block.tensor
        def _(pe):
            def product(b, tq, s, where, t, high, low, k0, nk, ready=None, base=0):
                if not isinstance(tq, int) or tq > 0:
                    pe.wait_ge(evac[b], tq)
                for k in range(nk):
                    if ready is not None:
                        pe.wait_ge(ready, base + k + 1)
                    o = s * SLOT + where(k, t)
                    hi = high[:, (k0 + k) * T:(k0 + k + 1) * T]
                    lo = low[:, (k0 + k) * T:(k0 + k + 1) * T]
                    pe.matmul(acc[b][:, :], w_high[:, o:o + P], hi, start=(k == 0), stop=False)
                    pe.matmul(acc[b][:, :], w_high[:, o:o + P], lo, start=False, stop=False)
                    mm = pe.matmul(acc[b][:, :], w_low[:, o:o + P], hi, start=False, stop=(k == nk - 1))
                mm.then_inc(tile_ready, 1)

            def chunk(c):
                pe.wait_ge(w_ready, c + 1)

            def sum_square(n, k):
                pe.wait_ge(sq_ready, KD * n + k + 1)
                pe.matmul(misc[:, :], ones[:, :], sq[k % 2][:, :], start=(k == 0), stop=(k == KD - 1))\
                  .then_inc(sq_added, 1)

            def sums(n):
                if n > 0:
                    pe.wait_ge(ms_ready, n)
                if n in PE_NORMS:
                    for k in range(KD):
                        sum_square(n, k)
                else:
                    pe.wait_ge(sq_added, KD * (n + 1))
                    pe.matmul(misc[:, :], ones[:, :], acc_sq[:, :], start=True, stop=True).then_inc(stat_ready, 1)

            def ada_sum(table, b):
                pe.wait_ge(ada_used, b * KD + KD)
                for n in range(KD):
                    o = ob[:, KD * b + n:KD * b + n + 1] if isinstance(b, int) else ob[:, bass.ds(b * KD + n, 1)]
                    mm = pe.matmul(o, table[:, n * P:(n + 1) * P], ones[:, 0:1], start=True, stop=True)
                mm.then_inc(ada_read, 1)

            pe.wait_ge(consts_ready, 2)
            pe.wait_ge(c_landed, 16)
            pe.transpose(sc[0][:, 0:KD], c_row[:, :], ident[0:KD, 0:KD]).then_inc(c_turned, 1)
            pe.wait_ge(x_landed, 16 * TT)
            for k in range(KD):
                if k >= 3:
                    pe.wait_ge(x_stored, k - 2)
                for t in range(TT):
                    mm = pe.transpose(xb[k % 3][:, t * P:(t + 1) * P], xin[:, t * D + k * P:t * D + (k + 1) * P], ident[:, :])
                mm.then_inc(x_turned, 1)
                if k >= 2:
                    sum_square(0, k - 2)
            sum_square(0, KD - 2)
            sum_square(0, KD - 1)
            pe.wait_ge(rows_landed, 16 * ROW_DMAS)
            pe.wait_ge(c_ready, 1)
            for j, n in enumerate(ROW_COUNTS):
                mm = pe.transpose(sc[0][:, j * P:j * P + n], rows[j][0:n, :], ident[0:n, 0:n])
            mm.then_inc(rows_turned, 1)
            for b in range(2):
                ada_sum(ada_acc[b], b)
            pe.wait_ge(wsp_ready, 1)
            pe.wait_ge(x_stored, KD)
            for g in range(AG):
                mm = pe.transpose(sc[1 + g // 4][:, g % 4 * P:(g % 4 + 1) * P], wsp[:, g * P:(g + 1) * P], ident[:, :])
            mm.then_inc(wsp_turned, 1)

            def v_turn(n, j, tq):
                pe.wait_ge(evac[j], tq + 1)
                if not isinstance(n, int) or n >= 2:
                    pe.wait_ge(v_stored, n - 1)
                else:
                    pe.wait_ge(wsT_ready, 1)
                for t in range(TT):
                    mm = pe.transpose(sc[1 + j][:, t * P:(t + 1) * P], v_gel[j][:, t * P:(t + 1) * P], ident[:, :])
                mm.then_inc(v_turned, 1)

            def v_pair(i, first, ready=None):
                for s in range(2):
                    chunk(2 * i + s)
                    for t in range(2):
                        product(t, 2 * i + s, s, wide, t, h_high, h_low, 0, KD,
                                *((h_ready, 0) if first and s == t == 0 else ()))
                        if not (first and s == t == 0):
                            v_turn(4 * i + 2 * s + t - 1, 1 - t, 2 * i + s - (1 - t))

            v_pair(0, True)
            with pe.Fori(1, 4) as i:
                v_pair(i, False)
            v_turn(15, 1, 7)
            ada_sum(ada_acc[0], 2)

            q0, t0 = C0["uz"], T0["uz"] // 2
            with pe.Fori(0, 8) as i:
                for j in range(2):
                    chunk(2 * i + (q0 + j))
                    product(0, 2 * i + (t0 + j), j, paired, 0, h_high, h_low, 0, KD)
                    pe.wait_ge(vs_ready, 2 * i + (j + 1))
                    pe.wait_ge(ws_ready, i + 1)
                    if j == 0:
                        pe.wait_ge(v_stored, 2 * AG)
                    pe.wait_ge(mix_taken, 2 * i + j)
                    for t in range(TT):
                        mm = pe.matmul(sc[1 + j][:, t * P:(t + 1) * P], vs[j][:, t * P:(t + 1) * P], ws[:, :],
                                       start=True, stop=True)
                    mm.then_inc(mix_ready, 1)
                    product(1, 2 * i + (t0 + j), j, paired, 1, h_high, h_low, 0, KD)

            q0, t0 = C0["ao"], T0["ao"] // 2
            pe.wait_ge(y_ready, AN)
            with pe.Fori(0, 4) as i:
                for s in range(2):
                    chunk(2 * i + (q0 + s))
                    product(s, i + t0, s, tall, 0, b_high, b_low, 0, AN)
                ada_sum(ada2_acc, i + 3)
            sums(1)

            def kv_after(m):
                if m < 3:
                    pe.wait_ge(evac[1], T0["kv"] // 2 + m + 1)
                    if m > 0:
                        pe.wait_ge(k_ms_ready, 2 * m)
                    else:
                        pe.wait_ge(ms_ready, 2)
                    for j in range(2):
                        pe.matmul((misc, tr[0])[j][:, :], ones[:, :], k_sq[j][:, :], start=True, stop=True)\
                            .then_inc(k_stat, 1)
                else:
                    for j in range(2):
                        n = 2 * (m - 3) + j
                        pe.wait_ge(evac[j], T0["kv"] // 2 + m + 1)
                        if n >= 2:
                            pe.wait_ge(v1_stored, n - 1)
                        for t in range(TT):
                            mm = pe.transpose(sc[1 + j][:, t * P:(t + 1) * P], v_raw[j][:, t * P:(t + 1) * P], ident[:, :])
                        mm.then_inc(v1_turned, 1)

            for m in range(6):
                chunk(C0["kv"] + m)
                product(0, T0["kv"] // 2 + m, m % 2, wide, 0, b_high, b_low, 0, KD,
                        *((h_ready, KD) if m == 0 else ()))
                if m > 0:
                    kv_after(m - 1)
                product(1, T0["kv"] // 2 + m, m % 2, wide, 1, b_high, b_low, 0, KD)
            kv_after(5)
            ada_sum(ada3_acc, 7)

            TQ = T0["qz"] // 2

            def q_product(s, j, n, first):
                if n % 2 == 0:
                    chunk(2 * s + (C0["qz"] + n // 2))
                product(n % 2, 2 * s + (TQ + n // 2), n // 2, paired, n % 2, h_high, h_low, 0, KD,
                        *((h_ready, 2 * KD) if first and n == 0 else ()))

            def scores(a, j, kv, r):
                qt = TT - 1 - r
                if r == 0:
                    pe.wait_ge(qr_ready, a + 1)
                if not isinstance(a, int) or 4 * a + r > 0:
                    pe.wait_ge(scores_taken, 4 * a + r)
                for g in range(GROUPS):
                    w = (min(2, qt + 1) if g == 0 else qt + 1) * P
                    k = (g * NKV + kv) * T
                    mm = pe.matmul(sc[g][:, DIST_W[g] - w:DIST_W[g]], qT[j][g][:, qt * P:(qt + 1) * P],
                                   kT[:, k + (qt + 1) * P - w:k + (qt + 1) * P], start=True, stop=True)
                mm.then_inc(scores_ready, 1)

            def turn(a, r):
                qt = TT - 1 - r
                pe.wait_ge(p_scaled, 4 * a + (r + 1))
                at_ = 0
                for g in range(GROUPS):
                    e = 3 * r + g
                    if not isinstance(a, int) or 6 * a + e // 2 > 0:
                        pe.wait_ge(p_stored[e % 2], 6 * a + e // 2)
                    for m in range(min(2, qt + 1) if g == 0 else qt + 1):
                        mm = pe.transpose(tr[e % 2][:, m * P:(m + 1) * P], s_row[r % 2][:, at_:at_ + P], ident[:, :])
                        at_ += P
                    mm.then_inc(p_turned, 1)

            def square_sums(s):
                if not isinstance(s, int) or s > 1:
                    pe.wait_ge(o_taken, s - 1)
                pe.wait_ge(evac[0], 2 * s + (TQ + 2))
                for g in range(GROUPS):
                    for t in range(TT):
                        mm = pe.matmul(ob[:, 480 + g * TT + t:481 + g * TT + t], q_sq[g][:, t * P:(t + 1) * P],
                                       ones[:, 0:1], start=True, stop=True)
                mm.then_inc(qsq_summed, 1)

            def weighted(a, kv, last=False):
                for b in range(2):
                    pe.wait_ge(p_stored[b], 6 * a + 6)
                if last:
                    pe.wait_ge(o_taken, a)
                else:
                    pe.wait_ge(qms_ready, a + 2)
                order = [(1, k) for k in range(TT)] + [(2, k) for k in range(TT)] + [(0, k) for k in range(TT)]
                for n, (g, k) in enumerate(order):
                    end = min(k + 2, TT) if g == 0 else TT
                    src = k * 256 if g == 0 else D + (g - 1) * 4 * T + k * T + k * P
                    v = k * KVH * P + (g * NKV + kv) * P
                    mm = pe.matmul(ob[:, k * P:end * P], v1[:, v:v + P], pT[:, src:src + (end - k) * P],
                                   start=(n == 0), stop=(n == len(order) - 1), skip_group_check=True)
                mm.then_inc(pv_ready, 1)

            def head_step(s, j, kv, first=False, last=False):
                for n in range(4):
                    if not last:
                        q_product(s, j, n, first)
                    if not first:
                        if n > 0:
                            turn(s - 1, n - 1)
                        scores(s - 1, 1 - j, kv, n)
                if not last:
                    square_sums(s)
                if not first:
                    turn(s - 1, 3)
                    weighted(s - 1, kv, last)

            pe.wait_ge(v1_stored, KVH)
            pe.wait_ge(k_done, KVH)
            pe.wait_ge(ada_cols, 4)
            head_step(0, 0, 0, first=True)
            with pe.Fori(0, 2) as i:
                head_step(2 * i + 1, 1, 0)
                head_step(2 * i + 2, 0, 0)
            head_step(5, 1, 1)
            head_step(6, 0, 1)
            head_step(7, 1, 1)
            head_step(8, 0, 1, last=True)

            def out_wide(name, high, low, k0, ready=None, base=0):
                q0, t0 = C0[name], T0[name] // 2
                for s in range(2):
                    chunk(q0 + s)
                    for t in range(2):
                        product(t, t0 + s, s, wide, t, high, low, k0, KD,
                                *((ready, base) if ready is not None and s == t == 0 else ()))
                for s in range(2):
                    chunk(q0 + 2 + s)
                    for t in range(2):
                        product(t, t0 + 2 + s, s, wide, t, high, low, k0, KD)

            out_wide("bo", h_high, h_low, 0, h_ready, 3 * KD)
            sums(2)

            def ffn(l, hb, nb):
                for part, nk in (("a", FFA), ("b", FFB)):
                    q0, t0 = C0[f"gu{l}{part}"], T0[f"gu{l}{part}"] // 2
                    for s in range(2):
                        chunk(q0 + s)
                        for t in range(2):
                            product(t, t0 + s, s, paired, t, h_high, h_low, 0, KD,
                                    *((h_ready, hb) if part == "a" and s == t == 0 else ()))
                    with pe.Fori(1, nk // 2) as i:
                        for s in range(2):
                            chunk(2 * i + (q0 + s))
                            for t in range(2):
                                product(t, 2 * i + (t0 + s), s, paired, t, h_high, h_low, 0, KD)
                    q0, t0 = C0[f"dn{l}{part}"], T0[f"dn{l}{part}"] // 2
                    pe.wait_ge(hid_ready, (l - 1) * (FFA + FFB) + (FFA if part == "a" else FFA + FFB))
                    with pe.Fori(0, 4) as i:
                        for s in range(2):
                            chunk(2 * i + (q0 + s))
                            product(s, i + t0, s, tall, 0, b_high, b_low, 0, nk)
                sums(nb)
                if l == 1:
                    sums(nb + 1)

            ffn(1, 4 * KD, 3)

            q0, t0 = C0["mix"], T0["mix"] // 2
            for m in range(4):
                chunk(q0 + m)
                for t in range(2):
                    product(t, t0 + m, m % 2, paired, t, h_high, h_low, 0, KD,
                            *((h_ready, 5 * KD) if m == t == 0 else ()))

            def v2_turn(n):
                pe.wait_ge(evac[n % 2], t0 + 8 + n // 2 + 1)
                if n >= 2:
                    pe.wait_ge(v2_stored, n - 1)
                for t in range(TT):
                    mm = pe.transpose(sc[1 + n % 2][:, t * P:(t + 1) * P], v2_raw[n % 2][:, t * P:(t + 1) * P], ident[:, :])
                mm.then_inc(v2_turned, 1)

            for m in range(6):
                chunk(q0 + 4 + m)
                for t in range(2):
                    product(t, t0 + 4 + m, m % 2, wide, t, h_high, h_low, 0, KD)
                    if m == 5 and t == 0:
                        v2_turn(0)
                        v2_turn(1)
            v2_turn(2)
            v2_turn(3)

            def scores2(n):
                h, qt = n // TT, n % TT
                r0 = h % 2 * HD2
                if n >= 2:
                    pe.wait_ge(s2_taken, n - 1)
                w = (qt + 1) * P
                pe.matmul(sc[n % 2][:, 0:w], q2[r0:r0 + HD2, h // 2 * T + qt * P:h // 2 * T + (qt + 1) * P],
                          k2[r0:r0 + HD2, h // 2 * T:h // 2 * T + w], start=True, stop=True).then_inc(s2_ready, 1)

            def turn2(n):
                h, qt = n // TT, n % TT
                pe.wait_ge(p2_scaled, n + 1)
                if n >= 2:
                    pe.wait_ge(p2_stored, n - 1)
                for k in range(qt + 1):
                    mm = pe.transpose(tr[n % 2][:, k * P:(k + 1) * P], s2_row[n % 2][:, k * P:(k + 1) * P], ident[:, :])
                mm.then_inc(p2_turned, 1)

            def weighted2(h):
                pe.wait_ge(p2_stored, TT * (h + 1))
                r0 = h % 2 * HD2
                bank2 = (ob, sc[2])[h // 2 % 2]
                if h >= 4:
                    pe.wait_ge(o2_ready, h // 2 - 1)
                for k in range(TT):
                    mm = pe.matmul(bank2[r0:r0 + HD2, k * P:T], v2[:, k * T + h * HD2:k * T + (h + 1) * HD2],
                                   p2T[:, k * T + k * P:(k + 1) * T], start=(k == 0), stop=(k == TT - 1),
                                   skip_group_check=True)
                mm.then_inc(pv2_ready, 1)

            for b in range(2):
                pe.wait_ge(evac[b], t0 + 8)
            pe.wait_ge(v2_stored, 4)
            q0, t0 = C0["gates"], T0["gates"] // 2

            def gate_half(n):
                p = n // 2
                m, b = p // 2, p % 2
                if n % 4 == 0:
                    chunk(q0 + m)
                if n % 2 == 0:
                    pe.wait_ge(evac[b], t0 + m)
                for k in range(n % 2 * 4, n % 2 * 4 + 4):
                    o = m % 2 * SLOT + paired(k, b)
                    hi, lo = h_high[:, k * T:(k + 1) * T], h_low[:, k * T:(k + 1) * T]
                    pe.matmul(acc[b][:, :], w_high[:, o:o + P], hi, start=(k == 0), stop=False, skip_group_check=True)
                    pe.matmul(acc[b][:, :], w_high[:, o:o + P], lo, start=False, stop=False, skip_group_check=True)
                    mm = pe.matmul(acc[b][:, :], w_low[:, o:o + P], hi, start=False, stop=(k == KD - 1),
                                   skip_group_check=True)
                if n % 2 == 1:
                    mm.then_inc(tile_ready, 1)

            for n in range(H2 * TT):
                scores2(n)
                gate_half(n)
                if n >= 1:
                    turn2(n - 1)
                if n % TT == 0 and n > 0:
                    weighted2(n // TT - 1)
            turn2(H2 * TT - 1)
            weighted2(H2 - 1)

            pe.wait_ge(conv_step, CONV * CT)
            pe.wait_ge(p2_stored, H2 * TT)
            for n in range(CT):
                mm = pe.matmul(misc[:, :], ones[:, :], cy[:, n * T:(n + 1) * T], start=(n == 0), stop=(n == CT - 1))
            mm.then_inc(ln_sum, 1)
            for n in range(CT):
                pe.wait_ge(ln_sq_ready, n + 1)
                pe.matmul(tr[0][:, :], ones[:, :], ln[n % 2][:, :], start=(n == 0), stop=(n == CT - 1))\
                    .then_inc(ln_sq_summed, 1)

            q0, t0 = C0["outs"], T0["outs"] // 2
            pe.wait_ge(o2_ready, H2 // 2)
            pe.wait_ge(conv_ready, CT)
            with pe.Fori(0, 2) as i:
                for s in range(2):
                    chunk(2 * i + (q0 + s))
                    for j in range(2):
                        for t in range(2):
                            product(t, 4 * i + (t0 + 2 * s + j), s, lambda k, t, j=j: (8 * t + 2 * k + j) * P, t,
                                    b_high, b_low, 4 * t, 4)
            out_wide("wo", h_high, h_low, 0, m_ready, 0)
            sums(5)
            sums(6)
            ffn(2, 6 * KD, 7)

            pe.wait_ge(x_updated, 3 * KD)
            for t in range(TT):
                for b in range(2):
                    n = 2 * t + b
                    if n >= 2:
                        pe.wait_ge(out_copied, n - 1)
                    for m in range(4):
                        k = 4 * b + m
                        mm = pe.transpose(sc[b][:, m * P:(m + 1) * P], xT[:, k * T + t * P:k * T + (t + 1) * P], ident[:, :])
                    mm.then_inc(out_turned, 1)

        @block.scalar
        def _(act):
            def high_part(q, s, tiles):
                act.wait_ge(w_landed[s], 32 * q + 32)
                if not isinstance(tiles, int) or tiles > 0:
                    act.wait_ge(tile_ready, tiles)
                act.activation(w_high[:, s * SLOT:(s + 1) * SLOT], raw[:, s * SLOT:(s + 1) * SLOT], ACT.Copy)\
                   .then_inc(w_high_ready, 1)

            def next_high(q, s, tiles):
                if s == 0:
                    high_part(q, 1, tiles)
                else:
                    high_part(q + 1, 0, tiles)

            def root(n):
                act.wait_ge(ms_ready, n + 1)
                act.activation(n1[1][:, :], n1[0][:, :], ACT.Sqrt).then_inc(root_ready, 1)

            def square(src, j, n, m):
                if not isinstance(m, int) or KD * n + m >= 2:
                    act.wait_ge(sq_added, m + (KD * n - 1))
                act.activation(sq[j][:, :], src, ACT.Square).then_inc(sq_ready, 1)

            def high_of(src, dst, k, ready, at_least, done):
                act.wait_ge(ready, at_least)
                act.activation(seg(dst, k * T, T), src, ACT.Copy).then_inc(done, 1)


            act.wait_ge(c_turned, 1)
            act.activation(tiny[:, 64:72], sc[0][:, 0:KD], ACT.Silu).then_inc(c_ready, 1)

            for k in range(KD):
                act.wait_ge(x_turned, k + 1)
                act.activation(xT[:, k * T:(k + 1) * T], xb[k % 3][:, :], ACT.Copy).then_inc(x_stored, 1)
                act.wait_ge(x_stored, k + 1)
                square(xT[:, k * T:(k + 1) * T], k % 2, 0, k)
            act.wait_ge(cols_ready, 1)
            high_part(0, 0, 0)
            root(0)
            act.wait_ge(wsp_turned, 1)
            act.activation(wsT[:, 0:512], sc[1][:, :], ACT.Copy)
            act.activation(wsT[:, 512:1024], sc[2][:, :], ACT.Copy).then_inc(wsT_ready, 1)
            for k in range(KD):
                high_of(n2[k % 2][:, :], h_high, k, h32_ready, k + 1, h_high_ready)

            def v_pair(i, first):
                for s in range(2):
                    next_high(i, s, 4 * i + 2 * s)
                    for t in range(2):
                        act.wait_ge(tile_ready, 4 * i + (2 * s + t + 1))
                        if not (first and s == 0):
                            act.wait_ge(v_turned, 4 * i + (2 * s + t - 1))
                        act.activation(v_gel[t][:, :], acc[t][:, :], ACT.Gelu_apprx_tanh).then_inc(evac[t], 1)

            v_pair(0, True)
            with act.Fori(1, 4) as i:
                v_pair(i, False)
            act.wait_ge(v_stored, AN)
            act.wait_ge(ada_used, 3 * KD)
            for t in range(TT):
                ins = act.activation(junk[t][:, :].rearrange("p (n e) -> p n e", e=P),
                                     v_tok[:, :].rearrange("p (n c e) -> p n c e", c=TT, e=P)[:, :, t, :],
                                     ACT.Square, accum_out=tiny[:, V_SS + t:V_SS + t + 1])
            ins.then_inc(v_sq, 1)
            act.wait_ge(v_ms, 1)
            act.activation(tiny[:, V_RT:V_RT + 4], tiny[:, V_MS:V_MS + 4], ACT.Sqrt).then_inc(v_root, 1)

            q0, t0 = C0["uz"] // 2, T0["uz"]
            with act.Fori(0, 8) as i:
                for j in range(2):
                    next_high(i + q0, j, 4 * i + (t0 + 2 * j))
                    act.wait_ge(tile_ready, 4 * i + (t0 + 2 * j + 1))
                    act.activation(ug[j][:, :], acc[0][:, :], ACT.Gelu_apprx_tanh).then_inc(evac[0], 1)
                    act.wait_ge(tile_ready, 4 * i + (t0 + 2 * j + 2))
                    act.activation(zs[j][:, :], acc[1][:, :], ACT.Silu).then_inc(evac[1], 1)
                    high_of(y32[j][:, :], b_high, 2 * i + j, y32_ready, 2 * i + (j + 1), y_high_ready)

            q0, t0 = C0["ao"] // 2, T0["ao"]
            with act.Fori(0, 4) as i:
                for s in range(2):
                    next_high(i + q0, s, 2 * i + (t0 + s))
                    act.wait_ge(evac[s], i + (t0 // 2 + 1))
                    square(seg(xT, (2 * i + s) * T, T), s, 1, 2 * i + s)
            root(1)
            act.wait_ge(tile_ready, TILES_END["ao"])
            for k in range(KD):
                high_of(n2[k % 2][:, :], b_high, k, h32_ready, KD + k + 1, h_high_ready)

            for m in range(6):
                next_high(C0["kv"] // 2 + m // 2, m % 2, T0["kv"] + 2 * m)
                if 1 <= m <= 3:
                    for j in range(2):
                        act.wait_ge(k_ms_ready, 2 * (m - 1) + j + 1)
                        act.activation(k_rt[j][:, :], k_ms[j][:, :], ACT.Sqrt).then_inc(k_root, 1)
                for t in range(2):
                    act.wait_ge(tile_ready, T0["kv"] + 2 * m + t + 1)
                    if m < 3:
                        if m > 0:
                            act.wait_ge(k_done, 2 * (m - 1) + t + 1)
                        act.activation(k_raw[t][:, :], acc[t][:, :], ACT.Copy)
                        act.activation(k_sq[t][:, :], acc[t][:, :], ACT.Square).then_inc(evac[t], 1)
                    else:
                        n = 2 * (m - 3) + t
                        if n >= 2:
                            act.wait_ge(v1_turned, n - 1)
                        act.activation(v_raw[t][:, :], acc[t][:, :], ACT.Copy).then_inc(evac[t], 1)
                if m < 4:
                    for k in (2 * m, 2 * m + 1):
                        high_of(n2[k % 2][:, :], h_high, k, h32_ready, 2 * KD + k + 1, h_high_ready)

            q0, t0 = C0["qz"] // 2, T0["qz"]

            def head_bias(a):
                if not isinstance(a, int) or a > 0:
                    act.wait_ge(scores_taken, 4 * a)
                for g in range(GROUPS):
                    part = slice(DIST_AT[g], DIST_AT[g] + DIST_W[g])
                    ins = act.activation(bias[:, part], dist[:, part], ACT.Identity, scale=seg(slopes, a + g * NQ, 1))
                ins.then_inc(bias_ready, 1)

            def store_g2(a, r):
                qt = TT - 1 - r
                e = 3 * r + 2
                act.wait_ge(p_turned, 12 * a + (e + 1))
                if not isinstance(a, int) or a > 0:
                    act.wait_ge(pv_ready, a)
                dst = pT[:, D + 4 * T:D + 8 * T].rearrange("p (k i) -> p k i", i=T)[:, 0:qt + 1, qt * P:(qt + 1) * P]
                act.activation(dst, tr[e % 2][:, 0:(qt + 1) * P].rearrange("p (k i) -> p k i", i=P), ACT.Copy)\
                   .then_inc(p_stored[e % 2], 1)

            def head_step(s, j, first=False, last=False):
                for n in range(4):
                    if not last:
                        if n % 2 == 0:
                            next_high(s + q0, n // 2, 4 * s + (t0 + n))
                        act.wait_ge(tile_ready, 4 * s + (t0 + n + 1))
                        if n == 0 and not first:
                            act.wait_ge(scores_ready, 4 * s - 4)
                            act.wait_ge(qsq_summed, s)
                        if n < 3:
                            act.activation(qT[j][n][:, :], acc[n % 2][:, :], ACT.Copy)
                            act.activation(q_sq[n][:, :], acc[n % 2][:, :], ACT.Square).then_inc(evac[n % 2], 1)
                        else:
                            if not isinstance(s, int) or s > 1:
                                act.wait_ge(o_taken, s - 1)
                            act.activation(zb[j][:, :], acc[1][:, :], ACT.Silu).then_inc(evac[1], 1)
                    if not first:
                        a = s - 1
                        if n > 0:
                            store_g2(a, n - 1)
                        w = (min(2, TT - n) + 2 * (TT - n)) * P
                        act.wait_ge(top_ready, 4 * a + (n + 1))
                        act.activation(s_row[n % 2][:, 0:w], s_row[n % 2][:, 0:w], ACT.Exp,
                                       bias=tiny[:, NM + n % 2:NM + n % 2 + 1],
                                       accum_out=tiny[:, LS + n % 2:LS + n % 2 + 1]).then_inc(p_ready, 1)
                if not last:
                    act.wait_ge(qms_ready, s + 1)
                    act.activation(tiny[:, Q_RT:Q_RT + 12], tiny[:, Q_MS:Q_MS + 12], ACT.Sqrt).then_inc(q_root, 1)
                if not first:
                    store_g2(s - 1, 3)
                if not last:
                    if first:
                        act.wait_ge(dist_ready, GROUPS)
                    head_bias(s)

            head_step(0, 0, first=True)
            with act.Fori(0, 2) as i:
                head_step(2 * i + 1, 1)
                head_step(2 * i + 2, 0)
            for s in (5, 6, 7):
                head_step(s, s % 2)
            head_step(8, 0, last=True)
            for k in range(KD):
                high_of(yb[:, k * T:(k + 1) * T], h_high, k, o_taken, k + 1, h_high_ready)

            q0, t0 = C0["bo"] // 2, T0["bo"]
            for m in range(4):
                next_high(q0 + m // 2, m % 2, t0 + 2 * m)
                for t in range(2):
                    n = 2 * m + t
                    act.wait_ge(evac[t], t0 // 2 + m + 1)
                    square(xT[:, n * T:(n + 1) * T], t, 2, n)
            root(2)

            def apply(base, hbase):
                for k in range(KD):
                    high_of(n2[k % 2][:, :], h_high, k, h32_ready, base + k + 1, h_high_ready)

            def squares_of_x(n, base):
                for k in range(KD):
                    act.wait_ge(x_updated, base + k + 1)
                    square(xT[:, k * T:(k + 1) * T], k % 2, n, k)

            def ffn(l, nb):
                for part, nk in (("a", FFA), ("b", FFB)):
                    q0, t0 = C0[f"gu{l}{part}"] // 2, T0[f"gu{l}{part}"]
                    with act.Fori(0, nk // 2) as i:
                        for s in range(2):
                            next_high(i + q0, s, 4 * i + (t0 + 2 * s))
                            act.wait_ge(tile_ready, 4 * i + (t0 + 2 * s + 1))
                            act.activation(sg[s][:, :], acc[0][:, :], ACT.Silu).then_inc(evac[0], 1)
                            high_of(hd[s][:, :], b_high, 2 * i + s, evac[1], 2 * i + (t0 // 2 + s + 1), hid_high_ready)
                    q0, t0 = C0[f"dn{l}{part}"] // 2, T0[f"dn{l}{part}"]
                    if part == "a":
                        with act.Fori(0, 4) as i:
                            for s in range(2):
                                next_high(i + q0, s, 2 * i + (t0 + s))
                                act.wait_ge(tile_ready, 2 * i + (t0 + s + 1))
                                act.activation(seg(f, (2 * i + s) * T, T), acc[s][:, :], ACT.Copy).then_inc(evac[s], 1)

                def down(i, last=False):
                    for s in range(2):
                        if not (last and s == 1):
                            next_high(i + q0, s, 2 * i + (t0 + s))
                        act.wait_ge(evac[s], i + (t0 // 2 + 1))
                        square(seg(f, (2 * i + s) * T, T), s, nb, 2 * i + s)

                with act.Fori(0, 3) as i:
                    down(i)
                down(3, last=(l == 2))
                root(nb)

            apply(3 * KD, 4 * KD)
            ffn(1, 3)
            squares_of_x(4, 0)
            root(4)
            apply(4 * KD, 5 * KD)

            q0, t0 = C0["mix"] // 2, T0["mix"]
            for m in range(4):
                next_high(q0 + m // 2, m % 2, t0 + 2 * m)
                act.wait_ge(tile_ready, t0 + 2 * m + 2)
                if m >= 2:
                    act.wait_ge(evac[0], t0 // 2 + m - 1)
                act.activation(c_sig[m % 2][:, :], acc[1][:, :], ACT.Sigmoid, bias=col("conv_glu_bias_2", 4 + m))\
                   .then_inc(evac[1], 1)
            for m in range(6):
                next_high(q0 + 2 + m // 2, m % 2, t0 + 8 + 2 * m)
                for t in range(2):
                    act.wait_ge(tile_ready, t0 + 8 + 2 * m + t + 1)
                    n = 2 * m + t
                    if n < 8:
                        dst = (q2, k2)[n // 4][:, n % 4 * T:(n % 4 + 1) * T]
                    else:
                        dst = v2_raw[t][:, :]
                        if n >= 10:
                            act.wait_ge(v2_turned, n - 9)
                    act.activation(dst, acc[t][:, :], ACT.Copy).then_inc(evac[t], 1)

            def store2(n):
                h, qt = n // TT, n % TT
                act.wait_ge(p2_turned, n + 1)
                if h > 0:
                    act.wait_ge(pv2_ready, h)
                dst = p2T[:, :].rearrange("p (k i) -> p k i", i=T)[:, 0:qt + 1, qt * P:(qt + 1) * P]
                act.activation(dst, tr[n % 2][:, 0:(qt + 1) * P].rearrange("p (k i) -> p k i", i=P), ACT.Copy)\
                   .then_inc(p2_stored, 1)

            def output2(m):
                act.wait_ge(pv2_ready, 2 * m + 2)
                act.activation(b_high[:, m * T:(m + 1) * T], (ob, sc[2])[m % 2][:, :], ACT.Copy).then_inc(o2_high, 1)

            q0, t0 = C0["gates"] // 2, T0["gates"]

            def gate(p):
                act.wait_ge(tile_ready, t0 + p + 1)
                if p == 0:
                    act.wait_ge(conv_step, CONV * CT)
                act.activation(gates[p % 2][:, p // 2 * T:(p // 2 + 1) * T], acc[p % 2][:, :], ACT.Identity,
                               bias=col("gate_bias_2", p // 2 + 8 * (p % 2))).then_inc(evac[p % 2], 1)

            for n in range(H2 * TT):
                w = (n % TT + 1) * P
                act.wait_ge(top2_ready, n + 1)
                act.activation(s2_row[n % 2][:, 0:w], s2_row[n % 2][:, 0:w], ACT.Exp,
                               bias=tiny[:, NM + n % 2:NM + n % 2 + 1],
                               accum_out=tiny[:, LS + n % 2:LS + n % 2 + 1]).then_inc(p2_ready, 1)
                if n > 0:
                    store2(n - 1)
                if n > 8 and n % 8 == 1:
                    output2(n // 8 - 1)
                if n % 2 == 0 and n > 0:
                    gate(n // 2 - 1)
                if n % 4 == 0:
                    next_high(q0 + n // 8, n // 4 % 2, t0 + n // 2)
            store2(H2 * TT - 1)
            gate(15)
            output2(H2 // 2 - 1)

            for n in range(CT):
                act.wait_ge(ln_mean_ready, n + 1)
                if n >= 2:
                    act.wait_ge(ln_sq_summed, n - 1)
                act.activation(ln[n % 2][:, :], cy[:, n * T:(n + 1) * T], ACT.Square).then_inc(ln_sq_ready, 1)
            act.wait_ge(ln_ms, 1)
            act.activation(ln[0][:, :], ln[2][:, :], ACT.Sqrt).then_inc(ln_root, 1)
            for n in range(CT):
                act.wait_ge(ln_out, n + 1)
                cy_n = cy[:, n * T:(n + 1) * T]
                act.activation(cy_n, cy_n, ACT.Silu, bias=col("conv_ln_b_2", n)).then_inc(conv_silu, 1)
                high_of(cy_n, b_high, 4 + n, conv_silu, n + 1, conv_high)

            for b in range(2):
                act.wait_ge(evac[b], T0["gates"] // 2 + KD)
                act.activation(gates[b][:, :], gates[b][:, :], ACT.Sigmoid).then_inc(gates_ready, 1)
            q0, t0 = C0["outs"] // 2, T0["outs"]
            with act.Fori(0, 2) as i:
                for s in range(2):
                    next_high(i + q0, s, 8 * i + (t0 + 4 * s))
                    for j in range(2):
                        n = 4 * i + (2 * s + j)
                        high_of(m32[:, :], h_high, n, m32_ready, n + 1, m_high)

            q0, t0 = C0["wo"] // 2, T0["wo"]
            for m in range(4):
                next_high(q0 + m // 2, m % 2, t0 + 2 * m)
                for t in range(2):
                    n = 2 * m + t
                    act.wait_ge(tile_ready, t0 + n + 1)
                    square(acc[t][:, :], t, 5, n)
                    act.activation(f[:, n * T:(n + 1) * T], acc[t][:, :], ACT.Copy).then_inc(evac[t], 1)
            root(5)
            squares_of_x(6, KD)
            root(6)
            apply(5 * KD, 6 * KD)
            ffn(2, 7)

        @block.vector
        def _(dve):
            own = Chain(dve, dve_own)

            def low_part(q, s):
                dve.wait_ge(w_high_ready, 2 * q + (s + 1))
                w = slice(s * SLOT, (s + 1) * SLOT)
                dve.tensor_tensor(w_low[:, w], raw[:, w], w_high[:, w].bitcast(F32), ALU.subtract).then_inc(w_ready, 1)

            def next_low(q, s):
                if s == 0:
                    low_part(q, 1)
                else:
                    low_part(q + 1, 0)

            def low_of(src, high, low, k, ready, at_least, done):
                dve.wait_ge(ready, at_least)
                dve.tensor_tensor(seg(low, k * T, T), src, seg(high, k * T, T).bitcast(F32), ALU.subtract)\
                   .then_inc(done, 1)

            def clear_sum():
                own.done(dve.memset(acc_sq[:, :], 0.0))

            def add_square(n, m, j):
                dve.wait_ge(sq_ready, m + (KD * n + 1))
                if not isinstance(m, int) or KD * n + m > 0:
                    dve.wait_ge(sq_added, m + KD * n)
                dve.tensor_tensor(acc_sq[:, :], acc_sq[:, :], sq[j][:, :], ALU.add).then_inc(sq_added, 1)

            def reciprocal_root(n):
                if n in PE_NORMS:
                    dve.wait_ge(sq_added, KD * (n + 1))
                else:
                    dve.wait_ge(stat_ready, stats_before(n) + 1)
                dve.tensor_scalar(n1[0][:, :], misc[:, :], 1.0 / D, EPS, ALU.mult, ALU.add).then_inc(ms_ready, 1)
                dve.wait_ge(root_ready, n + 1)
                own.done(dve.reciprocal(rstd[:, :], n1[1][:, :]))

            def apply(hbase, scale, shift, high, low, tiles=range(KD)):
                for k in tiles:
                    if k >= 2:
                        dve.wait_ge(h_high_ready, hbase + k - 1)
                        dve.wait_ge(h_ready, hbase + k - 1)
                    x_k = xT[:, k * T:(k + 1) * T]
                    if shift is None:
                        dve.scalar_tensor_tensor(out=n2[k % 2][:, :], in0=x_k, scalar=scale(k), in1=rstd[:, :],
                                                 op0=ALU.mult, op1=ALU.mult).then_inc(h32_ready, 1)
                    else:
                        own.done(dve.scalar_tensor_tensor(out=n1[k % 2][:, :], in0=x_k, scalar=scale(k), in1=rstd[:, :],
                                                          op0=ALU.mult, op1=ALU.mult))
                        dve.tensor_scalar(n2[k % 2][:, :], n1[k % 2][:, :], shift(k), None, ALU.add).then_inc(h32_ready, 1)
                    if k > tiles[0]:
                        low_of(n2[(k - 1) % 2][:, :], high, low, k - 1, h_high_ready, hbase + k, h_ready)
                k = tiles[-1]
                low_of(n2[k % 2][:, :], high, low, k, h_high_ready, hbase + k + 1, h_ready)

            def ada_block(table, bufs, b, k0, nk, sums_taken=None):
                for k in range(k0, k0 + nk):
                    dve.wait_ge(ada_landed[k % 4], b * 32 + 16 * (k // 4 + 1))
                    ck = tiny[:, 64 + k:65 + k]
                    if k == 0:
                        if sums_taken is not None:
                            dve.wait_ge(ada_read, sums_taken)
                        dve.tensor_scalar(table[:, :], bufs[0][:, :], ck, None, ALU.mult).then_inc(ada_used, 1)
                    else:
                        dve.wait_ge(ada_used, b * KD + k)
                        dve.scalar_tensor_tensor(out=table[:, :], in0=bufs[k % 4][:, :], scalar=ck, in1=table[:, :],
                                                 op0=ALU.mult, op1=ALU.add).then_inc(ada_used, 1)

            def ada_columns(n0, n1_, read):
                dve.wait_ge(ada_read, read)
                b0 = COL["a_ada_b"]
                dve.tensor_tensor(ada[:, n0:n1_], ob[:, n0:n1_], cols[:, b0 + n0:b0 + n1_], ALU.add).then_inc(ada_cols, 1)

            def scale_columns(dst, scale0, norm):
                own.done(dve.scalar_tensor_tensor(out=derived[:, dst:dst + KD], in0=ada[:, scale0:scale0 + KD], scalar=1.0,
                                                  in1=cols[:, COL[norm]:COL[norm] + KD], op0=ALU.add, op1=ALU.mult))

            def derived_col(n):
                return derived[:, n:n + 1]

            def ada_col(n):
                return ada[:, n:n + 1]

            dve.wait_ge(c_ready, 1)
            ada_block(ada_acc[0], ada_w, 0, 0, KD)
            dve.wait_ge(rows_turned, 1)
            for j, n in enumerate(ROW_COUNTS):
                ins = dve.tensor_copy(cols[:, j * P:j * P + n], sc[0][:, j * P:j * P + n])
            ins.then_inc(cols_ready, 1)
            dve.wait_ge(rel_landed, 16)
            dve.tensor_copy(relrow[:, REL:3 * P], relrow[:, REL - 1:REL].broadcast_to([H2, 3 * P - REL])).then_inc(rel_padded, 1)
            dve.wait_ge(cols_ready, 1)
            own.done(dve.scalar_tensor_tensor(out=derived[:, SC_K:SC_K + 1], in0=col("k_norm_g"), scalar=float(P) ** -0.5,
                                              in1=col("b_q_norm_g"), op0=ALU.mult, op1=ALU.mult))
            for dst, name in ((HG1, "ffn1_norm_post_2"), (HG2, "ffn2_norm_post_2")):
                own.done(dve.tensor_scalar(derived[:, dst:dst + KD], cols[:, COL[name]:COL[name] + KD], 0.5, None, ALU.mult))
            ada_block(ada_acc[1], ada_w, 1, 0, KD)
            low_part(0, 0)
            reciprocal_root(0)
            ada_columns(0, 16, 2)
            dve.wait_ge(ada_cols, 1)
            scale_columns(A_A, SHIFT_A + KD, "a_norm_g")
            apply(0, lambda k: derived_col(A_A + k), lambda k: ada_col(SHIFT_A + k), h_high, h_low)

            own.done(dve.memset(ada_acc[0][:, :], 0.0))
            with dve.Fori(0, 2) as i:
                for m in range(4):
                    next_low(2 * i + m // 2, m % 2)
                    dve.wait_ge(ada_landed[m], 16 * i + 80)
                    dve.wait_ge(ada_used, 4 * i + (2 * KD + m))
                    dve.scalar_tensor_tensor(out=ada_acc[0][:, :], in0=ada_w[m][:, :], scalar=seg(tiny, 4 * i + (64 + m), 1),
                                             in1=ada_acc[0][:, :], op0=ALU.mult, op1=ALU.add).then_inc(ada_used, 1)
                    for t in range(2):
                        n = 8 * i + (2 * m + t)
                        dve.wait_ge(v_turned, n + 1)
                        dve.tensor_copy(seg(v_tok, n * T, T), sc[1 + t][:, :]).then_inc(v_stored, 1)
            ada_columns(16, 24, 3)
            dve.wait_ge(v_sq, 1)
            dve.tensor_scalar(tiny[:, V_MS:V_MS + 4], tiny[:, V_SS:V_SS + 4], 1.0 / AW, EPS, ALU.mult, ALU.add).then_inc(v_ms, 1)
            dve.wait_ge(v_root, 1)
            dve.reciprocal(tiny[:, V_R:V_R + 4], tiny[:, V_RT:V_RT + 4]).then_inc(mix_taken, 1)
            dve.wait_ge(mix_taken, 1)
            dve.wait_ge(bsb_landed, 16)
            dve.wait_ge(wsT_ready, 1)

            q0, t0 = C0["uz"] // 2, T0["uz"] // 2
            with dve.Fori(0, 8) as i:
                own.enter(i, 2)
                for j in range(2):
                    n = 2 * i + j
                    if j == 0:
                        dve.wait_ge(mix_ready, n)
                        dve.tensor_copy(ws[:, :], seg(wsT, i * P, P)).then_inc(ws_ready, 1)
                    dve.tensor_tensor(vs[j][:, :].rearrange("p (c e) -> p c e", e=P),
                                      seg(v_tok, n * T, T).rearrange("p (c e) -> p c e", e=P),
                                      tiny[:, V_R:V_R + 4].rearrange("p (c e) -> p c e", e=1).broadcast_to([P, TT, P]),
                                      ALU.mult).then_inc(vs_ready, 1)
                    next_low(i + q0, j)
                    dve.wait_ge(mix_ready, n + 1)
                    dve.scalar_tensor_tensor(out=vs[j][:, :].rearrange("p (c e) -> p c e", e=P),
                                             in0=sc[1 + j][:, :].rearrange("p (c e) -> p c e", e=P),
                                             scalar=col("a_sgu_g", n),
                                             in1=seg(bsb, i * P, P)[:, None, :].broadcast_to([P, TT, P]),
                                             op0=ALU.mult, op1=ALU.add).then_inc(mix_taken, 1)
                    dve.wait_ge(mix_taken, n + 2)
                    dve.wait_ge(evac[0], n + (t0 + 1))
                    own.done(dve.tensor_tensor(vs[j][:, :], vs[j][:, :], ug[j][:, :], ALU.mult))
                    dve.wait_ge(evac[1], n + (t0 + 1))
                    dve.tensor_tensor(y32[j][:, :], vs[j][:, :], zs[j][:, :], ALU.mult).then_inc(y32_ready, 1)
                    low_of(y32[j][:, :], b_high, b_low, n, y_high_ready, n + 1, y_ready)
                own.leave(8)

            def residual(tq, s, m, gate):
                dve.wait_ge(tile_ready, tq)
                x_m = seg(xT, m * T, T)
                dve.scalar_tensor_tensor(out=x_m, in0=acc[s][:, :], scalar=seg(ada, m + gate, 1), in1=x_m,
                                         op0=ALU.mult, op1=ALU.add).then_inc(evac[s], 1)

            q0, t0 = C0["ao"] // 2, T0["ao"]
            clear_sum()
            dve.wait_ge(ada_cols, 2)
            with dve.Fori(0, 4) as i:
                for s in range(2):
                    next_low(i + q0, s)
                    ada_block(ada2_acc, ada2_w, i + 3, 4 * s, 4, i + 3)
                    residual(2 * i + (t0 + s + 1), s, 2 * i + s, GATE_A)
                    add_square(1, 2 * i + s, s)
            ada_columns(24, 56, 7)
            dve.wait_ge(ada_cols, 3)
            scale_columns(A_KV, SHIFT_KV + KD, "kv_norm_g")
            scale_columns(A_B, SHIFT_B + KD, "b_norm_g")
            reciprocal_root(1)
            dve.wait_ge(tile_ready, TILES_END["ao"])
            apply(KD, lambda k: derived_col(A_KV + k), lambda k: ada_col(SHIFT_KV + k), b_high, b_low)

            def kv_after(m):
                if m < 3:
                    for j in range(2):
                        dve.wait_ge(k_stat, 2 * m + j + 1)
                        dve.tensor_scalar(k_ms[j][:, :], (misc, tr[0])[j][:, :], 1.0 / P, EPS, ALU.mult, ALU.add)\
                           .then_inc(k_ms_ready, 1)
                    for j in range(2):
                        dve.wait_ge(k_root, 2 * m + j + 1)
                        own.done(dve.reciprocal(k_rt[j][:, :], k_rt[j][:, :]))
                        n = 2 * m + j
                        dve.scalar_tensor_tensor(out=kT[:, n * T:(n + 1) * T], in0=k_raw[j][:, :],
                                                 scalar=derived_col(SC_K), in1=k_rt[j][:, :],
                                                 op0=ALU.mult, op1=ALU.mult).then_inc(k_done, 1)
                else:
                    for j in range(2):
                        n = 2 * (m - 3) + j
                        dve.wait_ge(v1_turned, n + 1)
                        dve.tensor_copy(v1[:, :].rearrange("p (k h d) -> p k h d", h=KVH, d=P)[:, :, n, :],
                                        sc[1 + j][:, :].rearrange("p (k d) -> p k d", d=P)).then_inc(v1_stored, 1)

            for m in range(6):
                next_low(C0["kv"] // 2 + m // 2, m % 2)
                if m > 0:
                    kv_after(m - 1)
                if m < 4:
                    apply(2 * KD, lambda k: derived_col(A_B + k), lambda k: ada_col(SHIFT_B + k), h_high, h_low,
                          range(2 * m, 2 * m + 2))
            kv_after(5)
            ada_block(ada3_acc, ada3_w, 7, 0, KD, 7)
            ada_columns(56, 64, 8)

            dve.wait_ge(dist_int, 2)
            for g in (1, 2):
                part = slice(DIST_AT[g], DIST_AT[g] + DIST_W[g])
                i32 = mybir.dt.int32
                own.done(dve.tensor_scalar(dist[:, part].bitcast(i32), bias[:, part].bitcast(i32), DILATION[g] - 1, None,
                                           ALU.bitwise_and))
                own.done(dve.tensor_scalar(dist[:, part], dist[:, part].bitcast(i32), 0.0, MASKED, ALU.is_gt, ALU.mult))
                dve.scalar_tensor_tensor(out=dist[:, part], in0=bias[:, part].bitcast(i32), scalar=-1.0,
                                         in1=dist[:, part], op0=ALU.mult, op1=ALU.add).then_inc(dist_thinned, 1)

            q0, t0 = C0["qz"] // 2, T0["qz"]

            def store_01(a, r):
                qt = TT - 1 - r
                for g in range(2):
                    e = 3 * r + g
                    dve.wait_ge(p_turned, 12 * a + (e + 1))
                    if not isinstance(a, int) or a > 0:
                        dve.wait_ge(pv_ready, a)
                    n = min(2, qt + 1) if g == 0 else qt + 1
                    src = tr[e % 2][:, 0:n * P]
                    if g == 0:
                        o = (qt - 1) * 256 + P if qt > 0 else 0
                        dst = pT[:, o:o + n * P]
                    else:
                        dst = pT[:, D:D + 4 * T].rearrange("p (k i) -> p k i", i=T)[:, 0:n, qt * P:(qt + 1) * P]
                        src = src.rearrange("p (k i) -> p k i", i=P)
                    dve.tensor_copy(dst, src).then_inc(p_stored[e % 2], 1)

            def softmax(a, j, r):
                qt = TT - 1 - r
                b = r % 2
                dve.wait_ge(scores_ready, 4 * a + (r + 1))
                if r == 0:
                    dve.wait_ge(bias_ready, a + 1)
                at_ = 0
                for g in range(GROUPS):
                    w = (min(2, qt + 1) if g == 0 else qt + 1) * P
                    d0 = DIST_AT[g] + DIST_W[g] - w
                    qr = Q_R + 12 * j + g * TT + qt
                    ins = dve.scalar_tensor_tensor(out=s_row[b][:, at_:at_ + w], in0=sc[g][:, DIST_W[g] - w:DIST_W[g]],
                                                   scalar=tiny[:, qr:qr + 1], in1=bias[:, d0:d0 + w],
                                                   op0=ALU.mult, op1=ALU.add)
                    at_ += w
                ins.then_inc(scores_taken, 1)
                dve.wait_ge(scores_taken, 4 * a + (r + 1))
                own.done(dve.tensor_reduce(tiny[:, MX + b:MX + b + 1], s_row[b][:, 0:at_], AX, ALU.max))
                dve.tensor_scalar(tiny[:, NM + b:NM + b + 1], tiny[:, MX + b:MX + b + 1], -1.0, None, ALU.mult)\
                   .then_inc(top_ready, 1)
                dve.wait_ge(p_ready, 4 * a + (r + 1))
                own.done(dve.reciprocal(tiny[:, LI + b:LI + b + 1], tiny[:, LS + b:LS + b + 1]))
                dve.tensor_scalar(s_row[b][:, 0:at_], s_row[b][:, 0:at_], tiny[:, LI + b:LI + b + 1], None, ALU.mult)\
                   .then_inc(p_scaled, 1)

            def head_step(s, j, first=False, last=False):
                for n in range(4):
                    if not last and n % 2 == 0:
                        next_low(s + q0, n // 2)
                    if not first:
                        if n > 0:
                            store_01(s - 1, n - 1)
                        softmax(s - 1, 1 - j, n)
                if not last:
                    dve.wait_ge(qsq_summed, s + 1)
                    dve.tensor_scalar(tiny[:, Q_MS:Q_MS + 12], ob[:, 480:492], 1.0 / P, EPS, ALU.mult, ALU.add)\
                       .then_inc(qms_ready, 1)
                    dve.wait_ge(q_root, s + 1)
                    dve.reciprocal(tiny[:, Q_R + 12 * j:Q_R + 12 * j + 12], tiny[:, Q_RT:Q_RT + 12]).then_inc(qr_ready, 1)
                if not first:
                    store_01(s - 1, 3)
                    dve.wait_ge(pv_ready, s)
                    dve.tensor_tensor(seg(yb, (s - 1) * T, T), ob[:, :], zb[1 - j][:, :], ALU.mult).then_inc(o_taken, 1)

            head_step(0, 0, first=True)
            with dve.Fori(0, 2) as i:
                own.enter(i, 16)
                head_step(2 * i + 1, 1)
                head_step(2 * i + 2, 0)
                own.leave(2)
            for s in (5, 6, 7):
                head_step(s, s % 2)
            head_step(8, 0, last=True)
            for k in range(KD):
                low_of(yb[:, k * T:(k + 1) * T], h_high, h_low, k, h_high_ready, 3 * KD + k + 1, h_ready)

            q0, t0 = C0["bo"] // 2, T0["bo"]
            dve.wait_ge(ada_cols, 4)
            clear_sum()
            for m in range(4):
                next_low(q0 + m // 2, m % 2)
                for t in range(2):
                    residual(t0 + 2 * m + t + 1, t, 2 * m + t, GATE_B)
                    add_square(2, 2 * m + t, t)
            reciprocal_root(2)

            def ffn(l, nb):
                h0 = (l - 1) * (FFA + FFB)
                for part, nk in (("a", FFA), ("b", FFB)):
                    q0, t0 = C0[f"gu{l}{part}"] // 2, T0[f"gu{l}{part}"]
                    hb = h0 + (FFA if part == "b" else 0)
                    with dve.Fori(0, nk // 2) as i:
                        for s in range(2):
                            n = 2 * i + s
                            next_low(i + q0, s)
                            dve.wait_ge(tile_ready, 2 * n + (t0 + 2))
                            dve.wait_ge(evac[0], n + (t0 // 2 + 1))
                            dve.tensor_tensor(hd[s][:, :], sg[s][:, :], acc[1][:, :], ALU.mult).then_inc(evac[1], 1)
                            low_of(hd[s][:, :], b_high, b_low, n, hid_high_ready, n + (hb + 1), hid_ready)
                    q0, t0 = C0[f"dn{l}{part}"] // 2, T0[f"dn{l}{part}"]
                    if part == "a":
                        with dve.Fori(0, 4) as i:
                            for s in range(2):
                                next_low(i + q0, s)
                clear_sum()

                def down(i, last=False):
                    for s in range(2):
                        if not (last and s == 1):
                            next_low(i + q0, s)
                        dve.wait_ge(tile_ready, 2 * i + (t0 + s + 1))
                        f_m = seg(f, (2 * i + s) * T, T)
                        dve.tensor_tensor(f_m, f_m, acc[s][:, :], ALU.add).then_inc(evac[s], 1)
                        add_square(nb, 2 * i + s, s)

                with dve.Fori(0, 3) as i:
                    down(i)
                down(3, last=(l == 2))
                reciprocal_root(nb)

            def add_normed(gain, base, n=None):
                for k in range(KD):
                    x_k = xT[:, k * T:(k + 1) * T]
                    own.done(dve.scalar_tensor_tensor(out=n1[k % 2][:, :], in0=f[:, k * T:(k + 1) * T], scalar=gain(k),
                                                      in1=rstd[:, :], op0=ALU.mult, op1=ALU.mult))
                    dve.tensor_tensor(x_k, x_k, n1[k % 2][:, :], ALU.add).then_inc(x_updated, 1)
                dve.wait_ge(x_updated, base + KD)
                if n is not None:
                    reciprocal_root(n)

            apply(4 * KD, lambda k: col("ffn1_norm_pre_2", k), None, h_high, h_low)
            ffn(1, 3)
            add_normed(lambda k: derived_col(HG1 + k), 0, 4)
            apply(5 * KD, lambda k: col("mix_norm_pre_2", k), None, h_high, h_low)

            q0, t0 = C0["mix"] // 2, T0["mix"]
            dve.wait_ge(h_ready, 6 * KD)
            dve.memset(glu[:, :].rearrange("p (n t) -> p n t", t=GW)[:, :, 0:PAD], 0.0).then_inc(toep_free, 1)
            dve.wait_ge(toep_free, 1)
            for m in range(4):
                next_low(q0 + m // 2, m % 2)
                dve.wait_ge(evac[1], t0 // 2 + m + 1)
                dve.scalar_tensor_tensor(out=glu[:, m * GW + PAD:(m + 1) * GW], in0=acc[0][:, :],
                                         scalar=col("conv_glu_bias_2", m), in1=c_sig[m % 2][:, :],
                                         op0=ALU.add, op1=ALU.mult).then_inc(evac[0], 1)
            dve.wait_ge(evac[0], t0 // 2 + 4)

            def tap(i, n):
                cy_n = cy[:, n * T:(n + 1) * T]
                dve.scalar_tensor_tensor(out=cy_n, in0=seg(glu, i + n * GW, T), scalar=col("conv_dw_w_2", i * CT + n),
                                         in1=cy_n, op0=ALU.mult, op1=ALU.add).then_inc(conv_step, 1)

            for n in range(CT):
                dve.tensor_scalar(cy[:, n * T:(n + 1) * T], glu[:, n * GW:n * GW + T], col("conv_dw_w_2", n),
                                  col("conv_dw_b_2", n), ALU.mult, ALU.add).then_inc(conv_step, 1)
            taps = (CONV - 1) // 6
            for m in range(6):
                next_low(q0 + 2 + m // 2, m % 2)
                with dve.Fori(0, taps) as i:
                    for n in range(CT):
                        dve.wait_ge(conv_step, i * CT + (m * taps * CT + n + 1))
                        tap(i + (m * taps + 1), n)
            for n in range(4):
                dve.wait_ge(v2_turned, n + 1)
                dve.tensor_copy(v2[:, :].rearrange("p (k d) -> p k d", d=T)[:, :, n * P:(n + 1) * P],
                                sc[1 + n % 2][:, :].rearrange("p (k d) -> p k d", d=P)).then_inc(v2_stored, 1)

            dve.wait_ge(toep_landed, 16 * H2)
            own.done(dve.memset(toep[0:CH2, :].rearrange("p (h m) -> p h m", m=REL)[:, :, 1:1 + CH2], MASKED))

            def softmax2(n):
                h, qt = n // TT, n % TT
                b = n % 2
                w = (qt + 1) * P
                near = min(2, qt + 1) * P
                dve.wait_ge(s2_ready, n + 1)
                if n >= 2:
                    dve.wait_ge(p2_turned, n - 1)
                ins = dve.scalar_tensor_tensor(out=s2_row[b][:, w - near:w], in0=sc[b][:, w - near:w], scalar=HD2 ** -0.5,
                                               in1=toep[:, h * REL + near:h * REL:-1], op0=ALU.mult, op1=ALU.add)
                if w > near:
                    ins = dve.tensor_scalar(s2_row[b][:, 0:w - near], sc[b][:, 0:w - near], HD2 ** -0.5,
                                            toep[:, h * REL + 256:h * REL + 257], ALU.mult, ALU.add)
                ins.then_inc(s2_taken, 1)
                dve.wait_ge(s2_taken, n + 1)
                own.done(dve.tensor_reduce(tiny[:, MX + b:MX + b + 1], s2_row[b][:, 0:w], AX, ALU.max))
                dve.tensor_scalar(tiny[:, NM + b:NM + b + 1], tiny[:, MX + b:MX + b + 1], -1.0, None, ALU.mult)\
                   .then_inc(top2_ready, 1)

            def scale2(n):
                b = n % 2
                w = (n % TT + 1) * P
                dve.wait_ge(p2_ready, n + 1)
                own.done(dve.reciprocal(tiny[:, LI + b:LI + b + 1], tiny[:, LS + b:LS + b + 1]))
                dve.tensor_scalar(s2_row[b][:, 0:w], s2_row[b][:, 0:w], tiny[:, LI + b:LI + b + 1], None, ALU.mult)\
                   .then_inc(p2_scaled, 1)

            def output2(m):
                dve.wait_ge(o2_high, m + 1)
                dve.tensor_tensor(b_low[:, m * T:(m + 1) * T], (ob, sc[2])[m % 2][:, :],
                                  b_high[:, m * T:(m + 1) * T].bitcast(F32), ALU.subtract).then_inc(o2_ready, 1)

            q0 = C0["gates"] // 2
            for n in range(H2 * TT):
                softmax2(n)
                if n > 0:
                    scale2(n - 1)
                if n > 8 and n % 8 == 2:
                    output2(n // 8 - 1)
                if n % 4 == 0:
                    next_low(q0 + n // 8, n // 4 % 2)
            scale2(H2 * TT - 1)
            output2(H2 // 2 - 1)

            dve.wait_ge(ln_sum, 1)
            for n in range(CT):
                cy_n = cy[:, n * T:(n + 1) * T]
                dve.scalar_tensor_tensor(out=cy_n, in0=misc[:, :], scalar=-1.0 / (CT * P), in1=cy_n,
                                         op0=ALU.mult, op1=ALU.add).then_inc(ln_mean_ready, 1)
            dve.wait_ge(ln_sq_summed, CT)
            dve.tensor_scalar(ln[2][:, :], tr[0][:, :], 1.0 / (CT * P), EPS, ALU.mult, ALU.add).then_inc(ln_ms, 1)
            dve.wait_ge(ln_root, 1)
            own.done(dve.reciprocal(ln[1][:, :], ln[0][:, :]))
            for n in range(CT):
                cy_n = cy[:, n * T:(n + 1) * T]
                dve.scalar_tensor_tensor(out=cy_n, in0=cy_n, scalar=col("conv_ln_g_2", n), in1=ln[1][:, :],
                                         op0=ALU.mult, op1=ALU.mult).then_inc(ln_out, 1)
            for n in range(CT):
                low_of(cy[:, n * T:(n + 1) * T], b_high, b_low, 4 + n, conv_high, n + 1, conv_ready)

            q0, t0 = C0["outs"] // 2, T0["outs"]
            dve.wait_ge(gates_ready, 2)
            with dve.Fori(0, 2) as i:
                for s in range(2):
                    next_low(i + q0, s)
                    for j in range(2):
                        n = 4 * i + (2 * s + j)
                        for t in range(2):
                            dve.wait_ge(tile_ready, 2 * n + (t0 + 1 + t))
                            dve.tensor_tensor(branch[t][:, :], seg(gates[t], n * T, T), acc[t][:, :], ALU.mult)\
                               .then_inc(evac[t], 1)
                        for t in range(2):
                            dve.wait_ge(evac[t], n + (t0 // 2 + 1))
                        dve.tensor_tensor(m32[:, :], branch[0][:, :], branch[1][:, :], ALU.add).then_inc(m32_ready, 1)
                        low_of(m32[:, :], h_high, h_low, n, m_high, n + 1, m_ready)

            q0 = C0["wo"] // 2
            clear_sum()
            for m in range(4):
                next_low(q0 + m // 2, m % 2)
                for t in range(2):
                    add_square(5, 2 * m + t, t)
            reciprocal_root(5)
            for t in range(2):
                dve.wait_ge(evac[t], T0["wo"] // 2 + 4)
            add_normed(lambda k: col("mix_norm_post_2", k), KD, 6)
            apply(6 * KD, lambda k: col("ffn2_norm_pre_2", k), None, h_high, h_low)
            ffn(2, 7)
            add_normed(lambda k: derived_col(HG2 + k), 2 * KD)

            for t in range(TT):
                for b in range(2):
                    dve.wait_ge(out_turned, 2 * t + b + 1)
                    if t >= 2:
                        dve.wait_ge(out_stored[t % 2], 16)
                    dve.tensor_copy(o_tok[t % 2][:, b * T:(b + 1) * T], sc[b][:, :]).then_inc(out_copied, 1)

    return nc


NAMES = ["x", "c", "a_ada_w", "a_ada_b", "a_norm_g", "a_w_in", "a_sgu_g", "a_w_spatial", "a_b_spatial", "a_w_out",
         "kv_ada_w", "kv_ada_b", "kv_norm_g", "w_kv", "k_norm_g", "b_ada_w", "b_ada_b", "b_norm_g", "b_w_in",
         "b_q_norm_g", "b_w_out", "ffn1_norm_pre_2", "ffn1_w_gate_2", "ffn1_w_up_2", "ffn1_w_down_2",
         "ffn1_norm_post_2", "mix_norm_pre_2", "w_in_2", "gate_bias_2", "rel_table_2", "w_attn_out_2",
         "conv_glu_bias_2", "conv_dw_w_2", "conv_dw_b_2", "conv_ln_g_2", "conv_ln_b_2", "conv_w_out_2", "w_out_2",
         "mix_norm_post_2", "ffn2_norm_pre_2", "ffn2_w_gate_2", "ffn2_w_up_2", "ffn2_w_down_2", "ffn2_norm_post_2"]


def kernel(**inputs):
    import concourse.bacc as bacc
    from concourse.bass_utils import run_bass_kernel_spmd

    nc = bacc.Bacc("TRN2", target_bir_lowering=False, num_devices=1)
    arrays, args = {}, {}
    for name in NAMES:
        a = np.ascontiguousarray(inputs[name])
        arrays[f"in_{name}"] = a
        args[name] = nc.dram_tensor(f"in_{name}", a.shape, mybir.dt.from_np(a.dtype), kind="ExternalInput").ap()
    out = nc.dram_tensor("out_0", (1, T, D), F32, kind="ExternalOutput").ap()
    build(nc, out=out, **args)
    r = run_bass_kernel_spmd(nc, [arrays], core_ids=[0])
    return r.results[0]["out_0"]
```

```python
from contextlib import ExitStack

import numpy as np

import concourse.bass as bass
from concourse import mybir

ALU = mybir.AluOpType
ACT = mybir.ActivationFunctionType
AX = mybir.AxisListType.X
F32 = mybir.dt.float32
F32R = mybir.dt.float32r

P = 128
D = 1024
KD = D // P
T = 512
TT = T // P
EPS = 1e-6
AW = 2048
AG = 8
AN = AW // P
NQ = 8
NKV = 2
GROUPS = 3
DILATION = (1, 4, 16)
KVH = GROUPS * NKV
FFA, FFB = 12, 10
FF = (FFA + FFB) * P
H2, HD2 = 8, 64
CH2 = 64
CONV = 31
CT = 4
REL = 257
SLOT = 16 * P
MASKED = -1e30

PHASES = [("v", 8, 16), ("uz", 16, 32), ("ao", 8, 8), ("kv", 6, 12), ("qz", 16, 32), ("bo", 4, 8),
          ("gu1a", FFA, 2 * FFA), ("dn1a", 8, 8), ("gu1b", FFB, 2 * FFB), ("dn1b", 8, 8),
          ("mix", 10, 20), ("gates", 8, 16), ("outs", 4, 16), ("wo", 4, 8),
          ("gu2a", FFA, 2 * FFA), ("dn2a", 8, 8), ("gu2b", FFB, 2 * FFB), ("dn2b", 8, 8)]
C0, T0 = {}, {}
_c = _t = 0
for _name, _nc, _nt in PHASES:
    C0[_name], T0[_name] = _c, _t
    _c, _t = _c + _nc, _t + _nt
TILES_END = {name: T0[name] + nt for name, _, nt in PHASES}

ROWS_A = [("a_ada_b", 24), ("kv_ada_b", 16), ("b_ada_b", 24), ("a_norm_g", 8), ("a_sgu_g", 16),
          ("kv_norm_g", 8), ("b_norm_g", 8), ("k_norm_g", 1), ("b_q_norm_g", 1)]
ROWS_B = [("ffn1_norm_pre_2", 8), ("ffn1_norm_post_2", 8), ("mix_norm_pre_2", 8), ("gate_bias_2", 16),
          ("conv_glu_bias_2", 8), ("conv_dw_b_2", 4), ("conv_ln_g_2", 4), ("conv_ln_b_2", 4),
          ("mix_norm_post_2", 8), ("ffn2_norm_pre_2", 8), ("ffn2_norm_post_2", 8)]
COL = {}
for _rows, _base in ((ROWS_A, 0), (ROWS_B, P)):
    for _name, _n in _rows:
        COL[_name] = _base
        _base += _n
COL["conv_dw_w_2"] = 2 * P


class Chain:

    def __init__(self, eng, sem):
        self.eng, self.sem, self.base, self.n, self.i, self.per = eng, sem, 0, 0, None, 0

    def done(self, ins):
        ins.then_inc(self.sem, 1)
        self.n += 1
        at = self.base + self.n
        self.eng.wait_ge(self.sem, at if self.i is None else self.i * self.per + at)

    def enter(self, i, per):
        self.base, self.n, self.i, self.per = self.base + self.n, 0, i, per

    def leave(self, count):
        assert self.n == self.per, (self.n, self.per)
        self.base, self.n, self.i = self.base + count * self.per, 0, None


DIST_AT, DIST_W = (0, 256, 768), (256, T, T)
PE_NORMS = (0, 4, 6)


def stats_before(n):
    return sum(m not in PE_NORMS for m in range(n))


ROW_DMAS = len(ROWS_A) + len(ROWS_B) + 1
ROW_COUNTS = (sum(n for _, n in ROWS_A), sum(n for _, n in ROWS_B), CONV * CT)


def seg(t, start, n):
    if isinstance(start, int):
        return t[:, start:start + n]
    return t[:, bass.ds(start, n)]


def build(nc, x, c, a_ada_w, a_ada_b, a_norm_g, a_w_in, a_sgu_g, a_w_spatial, a_b_spatial, a_w_out,
          kv_ada_w, kv_ada_b, kv_norm_g, w_kv, k_norm_g, b_ada_w, b_ada_b, b_norm_g, b_w_in,
          b_q_norm_g, b_w_out, ffn1_norm_pre_2, ffn1_w_gate_2, ffn1_w_up_2, ffn1_w_down_2,
          ffn1_norm_post_2, mix_norm_pre_2, w_in_2, gate_bias_2, rel_table_2, w_attn_out_2,
          conv_glu_bias_2, conv_dw_w_2, conv_dw_b_2, conv_ln_g_2, conv_ln_b_2, conv_w_out_2, w_out_2,
          mix_norm_post_2, ffn2_norm_pre_2, ffn2_w_gate_2, ffn2_w_up_2, ffn2_w_down_2,
          ffn2_norm_post_2, out):
    vectors = {"c": c, "a_ada_b": a_ada_b, "kv_ada_b": kv_ada_b, "b_ada_b": b_ada_b, "a_norm_g": a_norm_g,
               "a_sgu_g": a_sgu_g, "kv_norm_g": kv_norm_g, "b_norm_g": b_norm_g, "k_norm_g": k_norm_g,
               "b_q_norm_g": b_q_norm_g, "ffn1_norm_pre_2": ffn1_norm_pre_2,
               "ffn1_norm_post_2": ffn1_norm_post_2, "mix_norm_pre_2": mix_norm_pre_2,
               "gate_bias_2": gate_bias_2, "conv_glu_bias_2": conv_glu_bias_2,
               "conv_dw_b_2": conv_dw_b_2, "conv_ln_g_2": conv_ln_g_2, "conv_ln_b_2": conv_ln_b_2,
               "mix_norm_post_2": mix_norm_post_2, "ffn2_norm_pre_2": ffn2_norm_pre_2,
               "ffn2_norm_post_2": ffn2_norm_post_2}
    ctx = ExitStack()
    with ctx:
        KB = 1024
        BASE = 16512
        W0, X0, HH, HL, BH, BL, U = (BASE + k * KB for k in (0, 48, 64, 80, 96, 128, 160))
        END = 229360
        SMALL = END - 3584 - (END - 3584) % 32
        TMP = SMALL - 16 * KB
        TILE = 4 * T

        def at(name, offset, cols, dt=F32, rows=P):
            return nc.alloc_sbuf_tensor_at("s_" + name, [rows, cols], dt, offset=offset)

        raw = at("raw", W0, 2 * SLOT)
        w_high = at("w_high", W0 + 16 * KB, 2 * SLOT, F32R)
        w_low = at("w_low", W0 + 32 * KB, 2 * SLOT, F32R)
        xT = at("xT", X0, KD * T)
        h_high = at("h_high", HH, KD * T, F32R)
        h_low = at("h_low", HL, KD * T, F32R)
        b_high = at("b_high", BH, 16 * T, F32R)
        b_low = at("b_low", BL, 16 * T, F32R)
        ident = at("ident", SMALL, P)
        ones = at("ones", SMALL + 512, P)
        cols = at("cols", SMALL + 1024, 3 * P)
        ada = at("ada", SMALL + 2560, 64)
        derived = at("derived", SMALL + 2816, 64)
        slopes = at("slopes", SMALL + 3072, 24)
        tiny = at("tiny", SMALL + 3168, 96)
        acc_sq = at("acc_sq", TMP, T)
        rstd = at("rstd", TMP + TILE, T)
        sq = [at(f"sq{j}", TMP + (2 + j) * TILE, T) for j in range(2)]
        n1 = [at(f"n1{j}", TMP + (4 + j) * TILE, T) for j in range(2)]
        n2 = [at(f"n2{j}", TMP + (6 + j) * TILE, T) for j in range(2)]
        xin = at("xin", BH, TT * D)
        ada_w = [at(f"ada_w{j}", BH + 16 * KB + 4 * KB * j, D) for j in range(4)]
        ada_acc = [at(f"ada_acc{j}", U + 8 * KB + 4 * KB * j, D) for j in range(2)]
        rows = [at(f"rows{j}", BL + 512 * j, P) for j in range(3)]
        c_row = at("c_row", BL + 2 * KB, P, rows=KD)
        wsp = at("wsp", BL + 4 * KB, AG * P)
        relrow = at("relrow", BL + 8 * KB, 3 * P, rows=H2)
        junk = [at(f"junk{j}", BH + 8 * KB * j, AW) for j in range(4)]
        v_tok = at("v_tok", BL, AN * T)
        wsT = at("wsT", U, AG * P)
        bsb = at("bsb", U + 4 * KB, AG * P)
        ug = [at(f"ug{j}", U + 8 * KB + j * TILE, T) for j in range(2)]
        zs = [at(f"zs{j}", U + 12 * KB + j * TILE, T) for j in range(2)]
        y32 = [at(f"y32{j}", U + 16 * KB + j * TILE, T) for j in range(2)]
        vs = [at(f"vs{j}", U + 20 * KB + j * TILE, T) for j in range(2)]
        v_gel = [at(f"v_gel{j}", U + 16 * KB + j * TILE, T) for j in range(2)]
        ws = at("ws", U + 24 * KB, P)
        ada2_w = [at(f"ada2_w{j}", TMP + 8 * KB + 4 * KB * j, D) for j in range(2)]
        ada2_acc = at("ada2_acc", TMP + 4 * KB, D)
        ada3_acc = at("ada3_acc", U + 16 * KB, D)
        kT = at("kT", U, KVH * T)
        v1 = at("v1", U + 12 * KB, TT * KVH * P)
        k_raw = [at(f"k_raw{j}", BH + 16 * KB + j * TILE, T) for j in range(2)]
        k_sq = [at(f"k_sq{j}", BH + 20 * KB + j * TILE, T) for j in range(2)]
        k_ms = [at(f"k_ms{j}", BH + 24 * KB + j * TILE, T) for j in range(2)]
        k_rt = [at(f"k_rt{j}", BH + 28 * KB + j * TILE, T) for j in range(2)]
        v_raw = [at(f"v_raw{j}", BL + 16 * KB + j * TILE, T) for j in range(2)]
        yb = at("yb", BH, KD * T)
        pT = at("pT", BH + 16 * KB, 4 * 256 + 8 * T)
        s_row = [at(f"s_row{j}", BH + 36 * KB + j * 5 * KB, 1280) for j in range(2)]
        qT = [[at(f"qT{j}{g}", BH + 46 * KB + (3 * j + g) * TILE, T) for g in range(GROUPS)] for j in range(2)]
        bias = at("bias", BH + 58 * KB, 1280)
        q_sq = [at(f"q_sq{g}", TMP + g * TILE, T) for g in range(GROUPS)]
        zb = [at(f"zb{j}", TMP + (3 + j) * TILE, T) for j in range(2)]
        dist = at("dist", TMP + 5 * TILE, 1280)
        f = at("f", U, KD * T)
        sg = [at(f"sg{j}", U + 16 * KB + j * TILE, T) for j in range(2)]
        hd = [at(f"hd{j}", U + 20 * KB + j * TILE, T) for j in range(2)]
        q2 = at("q2", U, 4 * T)
        k2 = at("k2", U + 8 * KB, 4 * T)
        v2 = at("v2", U + 16 * KB, 4 * T)
        c_sig = [at(f"c_sig{j}", U + 24 * KB + j * TILE, T) for j in range(2)]
        PAD = CONV - 1
        GW = T + PAD
        glu = at("glu", BL + 32 * KB - 4 * CT * GW, CT * GW)
        s2_row = [at(f"s2_row{j}", TMP + 8448 + j * TILE, T) for j in range(2)]
        p2T = at("p2T", BH + 8 * KB, 4 * T)
        cy = at("cy", BL + 8 * KB, CT * T)
        gates = [at(f"gates{j}", o + 16 * KB, KD * T) for j, o in enumerate((BH, BL))]
        v2_raw = [at(f"v2_raw{j}", BH + j * TILE, T) for j in range(2)]
        toep = at("toep", TMP, H2 * REL)
        ln = [at(f"ln{j}", TMP + 8448 + j * TILE, T) for j in range(3)]
        branch = [at(f"branch{j}", U + j * TILE, T) for j in range(2)]
        m32 = at("m32", U + 4 * TILE, T)
        o_tok = at("o_tok", BH, TT * D)

        rel_ext = nc.dram_tensor("rel_ext", [H2, 3 * P], F32).ap()

        def bank(name):
            return ctx.enter_context(nc.psum_tensor(name, [P, 512], F32))

        acc = [bank("acc0"), bank("acc1")]
        misc = bank("misc")
        sc = [bank("sc0"), bank("sc1"), bank("sc2")]
        tr = [bank("tr"), misc]
        xb = [sc[1], sc[2], tr[0]]
        ob = bank("ob")
        out_bank = [[acc[0], acc[1], sc[0], sc[1]], [sc[2], tr[0], misc, ob]]

        def sem(name):
            return ctx.enter_context(nc.semaphore(name))

        w_landed = [sem("w_landed0"), sem("w_landed1")]
        w_high_ready, w_ready = sem("w_high_ready"), sem("w_ready")
        tile_ready = sem("tile_ready")
        evac = [sem("evac0"), sem("evac1")]
        dve_own, pool_own = sem("dve_own"), sem("pool_own")
        x_landed, rows_landed, wsp_landed, rel_landed = sem("x_landed"), sem("rows_landed"), sem("wsp_landed"), sem("rel_landed")
        rel_padded, rel_stored, toep_landed = sem("rel_padded"), sem("rel_stored"), sem("toep_landed")
        toep_free = sem("toep_free")
        bsb_landed = sem("bsb_landed")
        ada_landed = [sem(f"ada_landed{j}") for j in range(4)]
        ada2_landed = [sem(f"ada2_landed{j}") for j in range(2)]
        ada_used, ada_read, ada_cols = sem("ada_used"), sem("ada_read"), sem("ada_cols")
        consts_ready = sem("consts_ready")
        rows_turned, cols_ready, c_ready = sem("rows_turned"), sem("cols_ready"), sem("c_ready")
        c_landed, c_turned = sem("c_landed"), sem("c_turned")
        x_turned, x_stored = sem("x_turned"), sem("x_stored")
        wsp_ready, wsp_turned, wsT_ready = sem("wsp_ready"), sem("wsp_turned"), sem("wsT_ready")
        sq_ready, sq_added = sem("sq_ready"), sem("sq_added")
        stat_ready, ms_ready, root_ready = sem("stat_ready"), sem("ms_ready"), sem("root_ready")
        h32_ready, h_high_ready, h_ready = sem("h32_ready"), sem("h_high_ready"), sem("h_ready")
        x_updated = sem("x_updated")
        v_turned, v_stored = sem("v_turned"), sem("v_stored")
        v_sq, v_ms, v_root = sem("v_sq"), sem("v_ms"), sem("v_root")
        vs_ready, ws_ready, mix_ready, mix_taken = sem("vs_ready"), sem("ws_ready"), sem("mix_ready"), sem("mix_taken")
        y32_ready, y_high_ready, y_ready = sem("y32_ready"), sem("y_high_ready"), sem("y_ready")
        k_stat, k_ms_ready, k_root, k_done = sem("k_stat"), sem("k_ms_ready"), sem("k_root"), sem("k_done")
        v1_turned, v1_stored = sem("v1_turned"), sem("v1_stored")
        dist_ready, bias_ready = sem("dist_ready"), sem("bias_ready")
        scores_ready, scores_taken, top_ready = sem("scores_ready"), sem("scores_taken"), sem("top_ready")
        p_ready, p_scaled, p_turned = sem("p_ready"), sem("p_scaled"), sem("p_turned")
        p_stored = [sem("p_stored0"), sem("p_stored1")]
        pv_ready, o_taken = sem("pv_ready"), sem("o_taken")
        qsq_summed, qms_ready, q_root = sem("qsq_summed"), sem("qms_ready"), sem("q_root")
        qr_ready = sem("qr_ready")
        silu_ready, hid32_ready = sem("silu_ready"), sem("hid32_ready")
        hid_high_ready, hid_ready = sem("hid_high_ready"), sem("hid_ready")
        conv_step, gates_ready = sem("conv_step"), sem("gates_ready")
        ln_sum, ln_mean_ready, ln_sq_ready, ln_sq_summed, ln_ms, ln_root = (
            sem(n) for n in ("ln_sum", "ln_mean_ready", "ln_sq_ready", "ln_sq_summed", "ln_ms", "ln_root"))
        ln_out, conv_silu, conv_high, conv_ready = sem("ln_out"), sem("conv_silu"), sem("conv_high"), sem("conv_ready")
        v2_turned, v2_stored = sem("v2_turned"), sem("v2_stored")
        s2_ready, s2_taken, top2_ready, p2_ready, p2_scaled = (
            sem(n) for n in ("s2_ready", "s2_taken", "top2_ready", "p2_ready", "p2_scaled"))
        p2_turned, p2_stored, pv2_ready, o2_high, o2_ready = (
            sem(n) for n in ("p2_turned", "p2_stored", "pv2_ready", "o2_high", "o2_ready"))
        m32_ready, m_high, m_ready = sem("m32_ready"), sem("m_high"), sem("m_ready")
        dist_int, dist_thinned = sem("dist_int"), sem("dist_thinned")
        out_turned, out_stored = sem("out_turned"), sem("out_stored")
        out_copied = [sem(f"out_copied{b}") for b in range(2)]

        A_A, A_KV, A_B, SC_K, HG1, HG2 = 0, 8, 16, 24, 25, 33
        V_SS, V_MS, V_RT, V_R = 0, 4, 8, 12
        MX, NM, LS, LI = 16, 18, 20, 22
        Q_MS, Q_RT, Q_R = 24, 36, 48
        SHIFT_A, GATE_A, SHIFT_KV, SHIFT_B, GATE_B = 0, 16, 24, 40, 56

        def col(name, n=0):
            if isinstance(n, int):
                return cols[:, COL[name] + n:COL[name] + n + 1]
            return cols[:, bass.ds(n + COL[name], 1)]

        def kview(w):
            return w.rearrange("(k p) n -> p k n", p=P)

        W = {"a_in": kview(a_w_in[0]), "a_out": kview(a_w_out[0]), "kv": kview(w_kv), "b_in": kview(b_w_in[0]),
             "b_out": kview(b_w_out[0]), "in2": kview(w_in_2[0]), "attn": kview(w_attn_out_2[0]),
             "conv": kview(conv_w_out_2[0]), "out2": kview(w_out_2[0]),
             "g1": kview(ffn1_w_gate_2[0]), "u1": kview(ffn1_w_up_2[0]), "d1": kview(ffn1_w_down_2[0]),
             "g2": kview(ffn2_w_gate_2[0]), "u2": kview(ffn2_w_up_2[0]), "d2": kview(ffn2_w_down_2[0])}

        def wide(k, t):
            return k * 2 * P + t * P

        def paired(k, t):
            return t * 8 * P + k * P

        def tall(k, t):
            return k * P

        block = ctx.enter_context(nc.Block())

        @block.sync
        def _(sp):
            def wait_slot(q, s):
                if not isinstance(q, int) or q > 0:
                    sp.wait_ge(x_landed, 16 * TT)
                    sp.wait_ge(w_ready, 2 * q + s - 1)

            def column(n0):
                return n0 if isinstance(n0, int) else sp.snap(n0)

            def put(s, off, w, k0, nk, n0, n):
                dst = raw[:, s * SLOT + off:s * SLOT + off + nk * n].rearrange("p (k n) -> p k n", k=nk)
                src = w[:, k0:k0 + nk, n0:n0 + n] if isinstance(n0, int) else w[:, k0:k0 + nk, bass.ds(n0, n)]
                sp.dma_start(dst, src).then_inc(w_landed[s], 16)

            def chunk_wide(q, s, w, n0):
                n0 = column(n0)
                wait_slot(q, s)
                put(s, 0, w, 0, 4, n0, 2 * P)
                put(s, 8 * P, w, 4, 4, n0, 2 * P)

            def chunk_paired(q, s, wa, na, wb, nb):
                na, nb = column(na), column(nb)
                wait_slot(q, s)
                put(s, 0, wa, 0, 8, na, P)
                put(s, 8 * P, wb, 0, 8, nb, P)

            def chunk_tall(q, s, w, k0, nk, n0):
                half = nk // 2
                n0 = column(n0)
                wait_slot(q, s)
                put(s, 0, w, k0, half, n0, P)
                put(s, half * P, w, k0 + half, half, n0, P)

            def chunk_outs(q, s, n0):
                n0 = column(n0)
                wait_slot(q, s)
                put(s, 0, W["attn"], 0, 4, n0, 2 * P)
                put(s, 8 * P, W["conv"], 0, 4, n0, 2 * P)

            sp.dma_start(c_row[:, :], c[0].rearrange("(k p) -> k p", p=P)).then_inc(c_landed, 16)
            for t in range(TT):
                sp.dma_start(xin[:, t * D:(t + 1) * D], x[0, t * P:(t + 1) * P, :]).then_inc(x_landed, 16)
            for s in range(2):
                chunk_wide(0, s, W["a_in"], AW + s * 2 * P)
            n = 0
            for table, names in ((0, ROWS_A), (1, ROWS_B)):
                r = 0
                for name, k in names:
                    v = vectors[name]
                    if len(v.shape) == 2:
                        v = v[0]
                    sp.dma_start(rows[table][r:r + k, :], v.rearrange("(k p) -> k p", p=P)).then_inc(rows_landed, 16)
                    r += k
                    n += 1
            sp.dma_start(rows[2][0:CONV * CT, :],
                           conv_dw_w_2[0, :, 0, :].rearrange("t (k p) -> (t k) p", p=P)).then_inc(rows_landed, 16)
            assert n + 1 == ROW_DMAS
            sp.dma_start(wsp[:, :].rearrange("t (g s) -> t g s", g=AG),
                         a_w_spatial[0].rearrange("g t s -> t g s")).then_inc(wsp_landed, 16)
            sp.dma_start(relrow[:, 0:REL], rel_table_2[0]).then_inc(rel_landed, 16)
            sp.dma_start(bsb[:, :].rearrange("p (g t) -> p g t", g=AG),
                         a_b_spatial[0][None, :, :].broadcast_to([P, AG, P])).then_inc(bsb_landed, 16)
            sp.wait_ge(rel_padded, 1)
            sp.dma_start(rel_ext, relrow[:, :]).then_inc(rel_stored, 16)

            with sp.Fori(1, 4) as i:
                for s in range(2):
                    chunk_wide(i, s, W["a_in"], i * 512 + (AW + s * 2 * P))
            q0 = C0["uz"] // 2
            with sp.Fori(0, 8) as i:
                for s in range(2):
                    chunk_paired(i + q0, s, W["a_in"], i * 256 + s * P, W["a_in"], i * 256 + (2 * AW + s * P))
            q0 = C0["ao"] // 2
            with sp.Fori(0, 4) as i:
                for s in range(2):
                    chunk_tall(i + q0, s, W["a_out"], 0, 16, i * 256 + s * P)
            q0 = C0["kv"] // 2
            with sp.Fori(0, 3) as i:
                for s in range(2):
                    chunk_wide(i + q0, s, W["kv"], i * 512 + s * 2 * P)
            q0 = C0["qz"] // 2
            with sp.Fori(0, 8) as i:
                for s in range(2):
                    chunk_paired(i + q0, s, W["b_in"], i * P + 2 * s * D, W["b_in"], i * P + (2 * s + 1) * D)
            q0 = C0["bo"] // 2
            with sp.Fori(0, 2) as i:
                for s in range(2):
                    chunk_wide(i + q0, s, W["b_out"], i * 512 + s * 2 * P)

            def ffn(l):
                for part, k0, nk in (("a", 0, FFA), ("b", FFA, FFB)):
                    q0 = C0[f"gu{l}{part}"] // 2
                    with sp.Fori(0, nk // 2) as i:
                        for s in range(2):
                            n0 = i * 256 + (k0 + s) * P
                            chunk_paired(i + q0, s, W[f"g{l}"], n0, W[f"u{l}"], n0)
                    q0 = C0[f"dn{l}{part}"] // 2
                    with sp.Fori(0, 4) as i:
                        for s in range(2):
                            chunk_tall(i + q0, s, W[f"d{l}"], k0, nk, i * 256 + s * P)

            ffn(1)
            q0 = C0["mix"] // 2
            with sp.Fori(0, 2) as i:
                for s in range(2):
                    n0 = i * 256 + (1536 + s * P)
                    chunk_paired(i + q0, s, W["in2"], n0, W["in2"], n0 + 512)
            with sp.Fori(0, 3) as i:
                for s in range(2):
                    chunk_wide(i + (q0 + 2), s, W["in2"], i * 512 + s * 2 * P)
            sp.wait_ge(rel_stored, 16)
            sp.wait_ge(toep_free, 1)
            for h in range(H2):
                src = bass.AP(tensor=rel_ext.tensor, offset=h * 3 * P, ap=[[1, P], [1, REL]])
                sp.dma_start(toep[:, h * REL:(h + 1) * REL], src).then_inc(toep_landed, 16)
            q0 = C0["gates"] // 2
            with sp.Fori(0, 4) as i:
                for s in range(2):
                    n0 = i * 256 + (2560 + s * P)
                    chunk_paired(i + q0, s, W["in2"], n0, W["in2"], n0 + D)
            q0 = C0["outs"] // 2
            with sp.Fori(0, 2) as i:
                for s in range(2):
                    chunk_outs(i + q0, s, i * 512 + s * 2 * P)
            q0 = C0["wo"] // 2
            with sp.Fori(0, 2) as i:
                for s in range(2):
                    chunk_wide(i + q0, s, W["out2"], i * 512 + s * 2 * P)
            ffn(2)
            for h in range(2):
                for t in range(TT):
                    if h == 0:
                        sp.wait_ge(out_copied[0], t + 1)
                    else:
                        sp.wait_ge(out_copied[t % 2], TT * (1 - t % 2) + t // 2 + 1)
                    sp.dma_start(out[0, t * P:(t + 1) * P, h * T:(h + 1) * T],
                                 o_tok[:, t * D + h * T:t * D + (h + 1) * T]).then_inc(out_stored, 16)
            sp.wait_ge(out_stored, 16 * 2 * TT)
            sp.wait_ge(toep_landed, 16 * H2)

        @block.gpsimd
        def _(pool):
            own = Chain(pool, pool_own)
            own.done(pool.memset(ident[:, :], 0.0))
            pool.memset(ones[:, :], 1.0).then_inc(consts_ready, 1)
            pool.affine_select(out=ident[:, :], in_=ident[:, :], compare_op=ALU.not_equal, fill=1.0, base=0,
                               pattern=[[-1, P]], channel_multiplier=1).then_inc(consts_ready, 1)
            aw = a_ada_w[0].rearrange("(k p) n -> p k n", p=P)

            def load_block(b):
                for k in range(KD):
                    m = b * KD + k
                    if m >= 4:
                        pool.wait_ge(ada_used, m - 3)
                    pool.dma_start(ada_w[m % 4][:, :], aw[:, k, b * D:(b + 1) * D]).then_inc(ada_landed[m % 4], 16)

            load_block(0)
            load_block(1)

            pool.wait_ge(wsp_landed, 16)
            pool.affine_select(out=wsp[:, :].rearrange("t (g s) -> t g s", g=AG),
                               in_=wsp[:, :].rearrange("t (g s) -> t g s", g=AG), compare_op=ALU.is_ge, fill=0.0,
                               base=0, pattern=[[0, AG], [-1, P]], channel_multiplier=1).then_inc(wsp_ready, 1)

            load_block(2)
            for g in range(GROUPS):
                for h in range(NQ):
                    n = g * NQ + h
                    own.done(pool.memset(slopes[:, n:n + 1], float(np.exp2(np.float32(-8.0 * (n + 1) / (GROUPS * NQ))))))

            pool.wait_ge(h_ready, KD)
            for w, blocks, b0 in ((kv_ada_w, 2, 3), (b_ada_w[0], 3, 5)):
                wv = w.rearrange("(k p) n -> p k n", p=P)
                with pool.Fori(0, blocks) as i:
                    for k in range(KD):
                        pool.wait_ge(ada_used, (i + b0) * KD + (k - 1))
                        pool.dma_start(ada2_w[k % 2][:, :], wv[:, k, bass.ds(i * D, D)]).then_inc(ada2_landed[k % 2], 16)

            pool.wait_ge(ada_used, 8 * KD)
            for g in range(GROUPS):
                off, w = DIST_AT[g], DIST_W[g]
                part = dist[:, off:off + w]
                if g == 0:
                    pool.wait_ge(h_ready, 3 * KD)
                    own.done(pool.iota(part, pattern=[[1, w]], base=P - w, channel_multiplier=-1,
                                       allow_small_or_imprecise_dtypes=True))
                    own.done(pool.affine_select(out=part, in_=part, compare_op=ALU.is_ge, fill=MASKED, base=0,
                                                pattern=[[1, w]], channel_multiplier=-1))
                else:
                    pool.iota(bias[:, off:off + w].bitcast(mybir.dt.int32), pattern=[[-1, w]], base=w - P,
                              channel_multiplier=1).then_inc(dist_int, 1)
            for g in range(GROUPS):
                off, w = DIST_AT[g], DIST_W[g]
                part = dist[:, off:off + w]
                if g == 1:
                    pool.wait_ge(dist_thinned, 2)
                pool.affine_select(out=part, in_=part, compare_op=ALU.is_ge, fill=MASKED, base=w - P,
                                   pattern=[[-1, w]], channel_multiplier=1).then_inc(dist_ready, 1)

        @block.tensor
        def _(pe):
            def product(b, tq, s, where, t, high, low, k0, nk, ready=None, base=0, between=None):
                if not isinstance(tq, int) or tq > 0:
                    pe.wait_ge(evac[b], tq)
                for k in range(nk):
                    if ready is not None:
                        pe.wait_ge(ready, base + k + 1)
                    o = s * SLOT + where(k, t)
                    hi = high[:, (k0 + k) * T:(k0 + k + 1) * T]
                    lo = low[:, (k0 + k) * T:(k0 + k + 1) * T]
                    grouped = between is not None
                    pe.matmul(acc[b][:, :], w_high[:, o:o + P], hi, start=(k == 0), stop=False, skip_group_check=grouped)
                    pe.matmul(acc[b][:, :], w_high[:, o:o + P], lo, start=False, stop=False, skip_group_check=grouped)
                    mm = pe.matmul(acc[b][:, :], w_low[:, o:o + P], hi, start=False, stop=(k == nk - 1),
                                   skip_group_check=grouped)
                    if k == nk - 1:
                        mm.then_inc(tile_ready, 1)
                    if between is not None:
                        between(k)

            def chunk(c):
                pe.wait_ge(w_ready, c + 1)

            def sum_square(n, k):
                pe.wait_ge(sq_ready, KD * n + k + 1)
                pe.matmul(misc[:, :], ones[:, :], sq[k % 2][:, :], start=(k == 0), stop=(k == KD - 1))\
                  .then_inc(sq_added, 1)

            def sums(n):
                if n > 0:
                    pe.wait_ge(ms_ready, n)
                if n in PE_NORMS:
                    for k in range(KD):
                        sum_square(n, k)
                else:
                    pe.wait_ge(sq_added, KD * (n + 1))
                    pe.matmul(misc[:, :], ones[:, :], acc_sq[:, :], start=True, stop=True).then_inc(stat_ready, 1)

            def ada_sum(table, b):
                pe.wait_ge(ada_used, b * KD + KD)
                for n in range(KD):
                    o = ob[:, KD * b + n:KD * b + n + 1] if isinstance(b, int) else ob[:, bass.ds(b * KD + n, 1)]
                    mm = pe.matmul(o, table[:, n * P:(n + 1) * P], ones[:, 0:1], start=True, stop=True)
                mm.then_inc(ada_read, 1)

            pe.wait_ge(consts_ready, 2)
            pe.wait_ge(c_landed, 16)
            pe.transpose(sc[0][:, 0:KD], c_row[:, :], ident[0:KD, 0:KD]).then_inc(c_turned, 1)
            pe.wait_ge(x_landed, 16 * TT)
            for k in range(KD):
                if k >= 3:
                    pe.wait_ge(x_stored, k - 2)
                for t in range(TT):
                    mm = pe.transpose(xb[k % 3][:, t * P:(t + 1) * P], xin[:, t * D + k * P:t * D + (k + 1) * P], ident[:, :])
                mm.then_inc(x_turned, 1)
                if k >= 2:
                    sum_square(0, k - 2)
            sum_square(0, KD - 2)
            sum_square(0, KD - 1)
            pe.wait_ge(rows_landed, 16 * ROW_DMAS)
            pe.wait_ge(c_ready, 1)
            for j, n in enumerate(ROW_COUNTS):
                mm = pe.transpose(sc[0][:, j * P:j * P + n], rows[j][0:n, :], ident[0:n, 0:n])
            mm.then_inc(rows_turned, 1)
            for b in range(2):
                ada_sum(ada_acc[b], b)
            pe.wait_ge(wsp_ready, 1)
            pe.wait_ge(x_stored, KD)
            for g in range(AG):
                mm = pe.transpose(sc[1 + g // 4][:, g % 4 * P:(g % 4 + 1) * P], wsp[:, g * P:(g + 1) * P], ident[:, :])
            mm.then_inc(wsp_turned, 1)

            def v_turn(n, j, tq):
                pe.wait_ge(evac[j], tq + 1)
                if not isinstance(n, int) or n >= 2:
                    pe.wait_ge(v_stored, n - 1)
                else:
                    pe.wait_ge(wsT_ready, 1)
                for t in range(TT):
                    mm = pe.transpose(sc[1 + j][:, t * P:(t + 1) * P], v_gel[j][:, t * P:(t + 1) * P], ident[:, :])
                mm.then_inc(v_turned, 1)

            def v_pair(i, first, ready=None):
                for s in range(2):
                    chunk(2 * i + s)
                    for t in range(2):
                        product(t, 2 * i + s, s, wide, t, h_high, h_low, 0, KD,
                                *((h_ready, 0) if first and s == t == 0 else ()))
                        if not (first and s == t == 0):
                            v_turn(4 * i + 2 * s + t - 1, 1 - t, 2 * i + s - (1 - t))

            v_pair(0, True)
            with pe.Fori(1, 4) as i:
                v_pair(i, False)
            v_turn(15, 1, 7)
            ada_sum(ada_acc[0], 2)

            q0, t0 = C0["uz"], T0["uz"] // 2
            with pe.Fori(0, 4) as i:
                for m in range(4):
                    j = m % 2
                    chunk(4 * i + (q0 + m))
                    product(0, 4 * i + (t0 + m), j, paired, 0, h_high, h_low, 0, KD)
                    pe.wait_ge(vs_ready, 4 * i + (m + 1))
                    pe.wait_ge(ws_ready, 2 * i + (m // 2 + 1))
                    if m == 0:
                        pe.wait_ge(v_stored, 2 * AG)
                    pe.wait_ge(mix_taken, 4 * i + (m + 1))
                    for t in range(TT):
                        mm = pe.matmul(sc[1 + j][:, t * P:(t + 1) * P], vs[j][:, t * P:(t + 1) * P], ws[:, :],
                                       start=True, stop=True)
                    mm.then_inc(mix_ready, 1)
                    product(1, 4 * i + (t0 + m), j, paired, 1, h_high, h_low, 0, KD)
                ada_sum(ada2_acc, i + 3)

            q0, t0 = C0["ao"], T0["ao"] // 2
            for s in range(2):
                chunk(q0 + s)
                product(s, t0, s, tall, 0, b_high, b_low, 0, AN, *((y_ready, 0) if s == 0 else ()))
            with pe.Fori(1, 4) as i:
                for s in range(2):
                    chunk(2 * i + (q0 + s))
                    product(s, i + t0, s, tall, 0, b_high, b_low, 0, AN)
            sums(1)
            ada_sum(ada3_acc, 7)

            def kv_after(m):
                if m < 3:
                    pe.wait_ge(evac[1], T0["kv"] // 2 + m + 1)
                    if m > 0:
                        pe.wait_ge(k_ms_ready, 2 * m)
                    else:
                        pe.wait_ge(ms_ready, 2)
                    for j in range(2):
                        pe.matmul((misc, tr[0])[j][:, :], ones[:, :], k_sq[j][:, :], start=True, stop=True)\
                            .then_inc(k_stat, 1)
                else:
                    for j in range(2):
                        n = 2 * (m - 3) + j
                        pe.wait_ge(evac[j], T0["kv"] // 2 + m + 1)
                        if n >= 2:
                            pe.wait_ge(v1_stored, n - 1)
                        for t in range(TT):
                            mm = pe.transpose(sc[1 + j][:, t * P:(t + 1) * P], v_raw[j][:, t * P:(t + 1) * P], ident[:, :])
                        mm.then_inc(v1_turned, 1)

            for m in range(6):
                chunk(C0["kv"] + m)
                product(0, T0["kv"] // 2 + m, m % 2, wide, 0, b_high, b_low, 0, KD,
                        *((h_ready, KD) if m == 0 else ()))
                if m > 0:
                    kv_after(m - 1)
                product(1, T0["kv"] // 2 + m, m % 2, wide, 1, b_high, b_low, 0, KD)
            kv_after(5)

            TQ = T0["qz"] // 2

            def q_half(s, n, h):
                b = n % 2
                if n % 2 == h == 0:
                    chunk(2 * s + (C0["qz"] + n // 2))
                if h == 0:
                    pe.wait_ge(evac[b], 2 * s + (TQ + n // 2))
                for k in range(4 * h, 4 * h + 4):
                    if s == n == 0:
                        pe.wait_ge(h_ready, 2 * KD + k + 1)
                    o = n // 2 * SLOT + paired(k, b)
                    hi, lo = h_high[:, k * T:(k + 1) * T], h_low[:, k * T:(k + 1) * T]
                    pe.matmul(acc[b][:, :], w_high[:, o:o + P], hi, start=(k == 0), stop=False, skip_group_check=True)
                    pe.matmul(acc[b][:, :], w_high[:, o:o + P], lo, start=False, stop=False, skip_group_check=True)
                    mm = pe.matmul(acc[b][:, :], w_low[:, o:o + P], hi, start=False, stop=(k == KD - 1),
                                   skip_group_check=True)
                if h == 1:
                    mm.then_inc(tile_ready, 1)

            def scores(a, j, kv, r):
                qt = TT - 1 - r
                if r == 0:
                    pe.wait_ge(qr_ready, a + 1)
                if not isinstance(a, int) or 4 * a + r > 0:
                    pe.wait_ge(scores_taken, 4 * a + r)
                for g in range(GROUPS):
                    w = (min(2, qt + 1) if g == 0 else qt + 1) * P
                    k = (g * NKV + kv) * T
                    mm = pe.matmul(sc[g][:, DIST_W[g] - w:DIST_W[g]], qT[j][g][:, qt * P:(qt + 1) * P],
                                   kT[:, k + (qt + 1) * P - w:k + (qt + 1) * P], start=True, stop=True)
                mm.then_inc(scores_ready, 1)

            def turn(a, r):
                qt = TT - 1 - r
                pe.wait_ge(p_scaled, 4 * a + (r + 1))
                at_ = 0
                for g in range(GROUPS):
                    e = 3 * r + g
                    if not isinstance(a, int) or 6 * a + e // 2 > 0:
                        pe.wait_ge(p_stored[e % 2], 6 * a + e // 2)
                    for m in range(min(2, qt + 1) if g == 0 else qt + 1):
                        mm = pe.transpose(tr[e % 2][:, m * P:(m + 1) * P], s_row[r % 2][:, at_:at_ + P], ident[:, :])
                        at_ += P
                    mm.then_inc(p_turned, 1)

            def square_sums(s):
                if not isinstance(s, int) or s > 1:
                    pe.wait_ge(o_taken, s - 1)
                pe.wait_ge(evac[0], 2 * s + (TQ + 2))
                for g in range(GROUPS):
                    for t in range(TT):
                        mm = pe.matmul(ob[:, 480 + g * TT + t:481 + g * TT + t], q_sq[g][:, t * P:(t + 1) * P],
                                       ones[:, 0:1], start=True, stop=True)
                mm.then_inc(qsq_summed, 1)

            def weighted(a, kv, last=False):
                for b in range(2):
                    pe.wait_ge(p_stored[b], 6 * a + 6)
                if last:
                    pe.wait_ge(o_taken, a)
                else:
                    pe.wait_ge(qms_ready, a + 2)
                order = [(1, k) for k in range(TT)] + [(2, k) for k in range(TT)] + [(0, k) for k in range(TT)]
                for n, (g, k) in enumerate(order):
                    end = min(k + 2, TT) if g == 0 else TT
                    src = k * 256 if g == 0 else D + (g - 1) * 4 * T + k * T + k * P
                    v = k * KVH * P + (g * NKV + kv) * P
                    mm = pe.matmul(ob[:, k * P:end * P], v1[:, v:v + P], pT[:, src:src + (end - k) * P],
                                   start=(n == 0), stop=(n == len(order) - 1), skip_group_check=True)
                mm.then_inc(pv_ready, 1)

            pe.wait_ge(v1_stored, KVH)
            pe.wait_ge(k_done, KVH)
            pe.wait_ge(ada_cols, 4)
            for s in range(NQ + 1):
                for n in range(4):
                    if s < NQ:
                        q_half(s, n, 0)
                        if n == 3:
                            square_sums(s)
                    if s > 1 and n == 1:
                        weighted(s - 2, (s - 2) // 4)
                    if s > 0:
                        scores(s - 1, (s - 1) % 2, (s - 1) // 4, n)
                    if s < NQ:
                        q_half(s, n, 1)
                    if s > 0 and n > 0:
                        turn(s - 1, n - 1)
                    elif s > 1:
                        turn(s - 2, 3)
            turn(NQ - 1, 3)
            weighted(NQ - 1, 1, last=True)

            def out_wide(name, high, low, k0, ready=None, base=0):
                q0, t0 = C0[name], T0[name] // 2
                for s in range(2):
                    chunk(q0 + s)
                    for t in range(2):
                        product(t, t0 + s, s, wide, t, high, low, k0, KD,
                                *((ready, base) if ready is not None and s == t == 0 else ()))
                for s in range(2):
                    chunk(q0 + 2 + s)
                    for t in range(2):
                        product(t, t0 + 2 + s, s, wide, t, high, low, k0, KD)

            out_wide("bo", h_high, h_low, 0, h_ready, 3 * KD)

            def ffn(l, hb, nb):
                for part, nk in (("a", FFA), ("b", FFB)):
                    q0, t0 = C0[f"gu{l}{part}"], T0[f"gu{l}{part}"] // 2
                    for s in range(2):
                        chunk(q0 + s)
                        for t in range(2):
                            first = part == "a" and s == t == 0
                            if first and l == 2:
                                pe.wait_ge(ms_ready, 6)
                            product(t, t0 + s, s, paired, t, h_high, h_low, 0, KD,
                                    *((h_ready, hb) if first else ()),
                                    between=(lambda k: sum_square(6, k)) if first and l == 2 else None)
                            if first and l == 1:
                                sums(2)
                    with pe.Fori(1, nk // 2) as i:
                        for s in range(2):
                            chunk(2 * i + (q0 + s))
                            for t in range(2):
                                product(t, 2 * i + (t0 + s), s, paired, t, h_high, h_low, 0, KD)
                    q0, t0 = C0[f"dn{l}{part}"], T0[f"dn{l}{part}"] // 2
                    for s in range(2):
                        chunk(q0 + s)
                        product(s, t0, s, tall, 0, b_high, b_low, 0, nk,
                                *((hid_ready, (l - 1) * (FFA + FFB) + (0 if part == "a" else FFA)) if s == 0 else ()))
                    with pe.Fori(1, 4) as i:
                        for s in range(2):
                            chunk(2 * i + (q0 + s))
                            product(s, i + t0, s, tall, 0, b_high, b_low, 0, nk)
                sums(nb)
                if l == 1:
                    sums(nb + 1)

            ffn(1, 4 * KD, 3)

            q0, t0 = C0["mix"], T0["mix"] // 2
            for m in range(4):
                chunk(q0 + m)
                for t in range(2):
                    product(t, t0 + m, m % 2, paired, t, h_high, h_low, 0, KD,
                            *((h_ready, 5 * KD) if m == t == 0 else ()))

            def v2_turn(n):
                pe.wait_ge(evac[n % 2], t0 + 8 + n // 2 + 1)
                if n >= 2:
                    pe.wait_ge(v2_stored, n - 1)
                for t in range(TT):
                    mm = pe.transpose(sc[1 + n % 2][:, t * P:(t + 1) * P], v2_raw[n % 2][:, t * P:(t + 1) * P], ident[:, :])
                mm.then_inc(v2_turned, 1)

            for m in range(6):
                chunk(q0 + 4 + m)
                for t in range(2):
                    product(t, t0 + 4 + m, m % 2, wide, t, h_high, h_low, 0, KD)
                    if m == 5 and t == 0:
                        v2_turn(0)
                        v2_turn(1)
            v2_turn(2)
            v2_turn(3)

            def scores2(n):
                h, qt = n // TT, n % TT
                r0 = h % 2 * HD2
                if n >= 2:
                    pe.wait_ge(s2_taken, n - 1)
                w = (qt + 1) * P
                pe.matmul(sc[n % 2][:, 0:w], q2[r0:r0 + HD2, h // 2 * T + qt * P:h // 2 * T + (qt + 1) * P],
                          k2[r0:r0 + HD2, h // 2 * T:h // 2 * T + w], start=True, stop=True).then_inc(s2_ready, 1)

            def turn2(n):
                h, qt = n // TT, n % TT
                pe.wait_ge(p2_scaled, n + 1)
                if n >= 2:
                    pe.wait_ge(p2_stored, n - 1)
                for k in range(qt + 1):
                    mm = pe.transpose(tr[n % 2][:, k * P:(k + 1) * P], s2_row[n % 2][:, k * P:(k + 1) * P], ident[:, :])
                mm.then_inc(p2_turned, 1)

            def weighted2(h):
                pe.wait_ge(p2_stored, TT * (h + 1))
                r0 = h % 2 * HD2
                bank2 = (ob, sc[2])[h // 2 % 2]
                if h >= 4:
                    pe.wait_ge(o2_ready, h // 2 - 1)
                for k in range(TT):
                    mm = pe.matmul(bank2[r0:r0 + HD2, k * P:T], v2[:, k * T + h * HD2:k * T + (h + 1) * HD2],
                                   p2T[:, k * T + k * P:(k + 1) * T], start=(k == 0), stop=(k == TT - 1),
                                   skip_group_check=True)
                mm.then_inc(pv2_ready, 1)

            for b in range(2):
                pe.wait_ge(evac[b], t0 + 8)
            pe.wait_ge(v2_stored, 4)
            q0, t0 = C0["gates"], T0["gates"] // 2

            def gate_half(n):
                p = n // 2
                m, b = p // 2, p % 2
                if n % 4 == 0:
                    chunk(q0 + m)
                if n % 2 == 0:
                    pe.wait_ge(evac[b], t0 + m)
                for k in range(n % 2 * 4, n % 2 * 4 + 4):
                    o = m % 2 * SLOT + paired(k, b)
                    hi, lo = h_high[:, k * T:(k + 1) * T], h_low[:, k * T:(k + 1) * T]
                    pe.matmul(acc[b][:, :], w_high[:, o:o + P], hi, start=(k == 0), stop=False, skip_group_check=True)
                    pe.matmul(acc[b][:, :], w_high[:, o:o + P], lo, start=False, stop=False, skip_group_check=True)
                    mm = pe.matmul(acc[b][:, :], w_low[:, o:o + P], hi, start=False, stop=(k == KD - 1),
                                   skip_group_check=True)
                if n % 2 == 1:
                    mm.then_inc(tile_ready, 1)

            for n in range(H2 * TT):
                scores2(n)
                gate_half(n)
                if n >= 1:
                    turn2(n - 1)
                if n % TT == 0 and n > 0:
                    weighted2(n // TT - 1)
            turn2(H2 * TT - 1)
            weighted2(H2 - 1)

            pe.wait_ge(conv_step, CONV * CT)
            pe.wait_ge(p2_stored, H2 * TT)
            for n in range(CT):
                mm = pe.matmul(misc[:, :], ones[:, :], cy[:, n * T:(n + 1) * T], start=(n == 0), stop=(n == CT - 1))
            mm.then_inc(ln_sum, 1)
            for n in range(CT):
                pe.wait_ge(ln_sq_ready, n + 1)
                pe.matmul(tr[0][:, :], ones[:, :], ln[n % 2][:, :], start=(n == 0), stop=(n == CT - 1))\
                    .then_inc(ln_sq_summed, 1)

            q0, t0 = C0["outs"], T0["outs"] // 2
            pe.wait_ge(o2_ready, H2 // 2)
            for m in range(4):
                chunk(q0 + m)
                for j in range(2):
                    for t in range(2):
                        product(t, t0 + 2 * m + j, m % 2, lambda k, t, j=j: (8 * t + 2 * k + j) * P, t,
                                b_high, b_low, 4 * t, 4, *((conv_ready, 0) if m == j == 0 and t == 1 else ()))
            out_wide("wo", h_high, h_low, 0, m_ready, 0)
            sums(5)
            ffn(2, 6 * KD, 7)

            for k in range(KD):
                pe.wait_ge(x_updated, 2 * KD + k + 1)
                for t in range(TT):
                    mm = pe.transpose(out_bank[k // 4][t][:, k % 4 * P:(k % 4 + 1) * P],
                                      xT[:, k * T + t * P:k * T + (t + 1) * P], ident[:, :])
                    if k % 4 == 3:
                        mm.then_inc(out_turned, 1)

        @block.scalar
        def _(act):
            def high_part(q, s, tiles):
                act.wait_ge(w_landed[s], 32 * q + 32)
                if not isinstance(tiles, int) or tiles > 0:
                    act.wait_ge(tile_ready, tiles)
                act.activation(w_high[:, s * SLOT:(s + 1) * SLOT], raw[:, s * SLOT:(s + 1) * SLOT], ACT.Copy)\
                   .then_inc(w_high_ready, 1)

            def next_high(q, s, tiles):
                if s == 0:
                    high_part(q, 1, tiles)
                else:
                    high_part(q + 1, 0, tiles)

            def root(n):
                act.wait_ge(ms_ready, n + 1)
                act.activation(n1[1][:, :], n1[0][:, :], ACT.Sqrt).then_inc(root_ready, 1)

            def square(src, j, n, m):
                if not isinstance(m, int) or KD * n + m >= 2:
                    act.wait_ge(sq_added, m + (KD * n - 1))
                act.activation(sq[j][:, :], src, ACT.Square).then_inc(sq_ready, 1)

            def high_of(src, dst, k, ready, at_least, done):
                act.wait_ge(ready, at_least)
                act.activation(seg(dst, k * T, T), src, ACT.Copy).then_inc(done, 1)


            act.wait_ge(c_turned, 1)
            act.activation(tiny[:, 64:72], sc[0][:, 0:KD], ACT.Silu).then_inc(c_ready, 1)

            for k in range(KD):
                act.wait_ge(x_turned, k + 1)
                act.activation(xT[:, k * T:(k + 1) * T], xb[k % 3][:, :], ACT.Copy).then_inc(x_stored, 1)
                act.wait_ge(x_stored, k + 1)
                square(xT[:, k * T:(k + 1) * T], k % 2, 0, k)
            act.wait_ge(cols_ready, 1)
            high_part(0, 0, 0)
            root(0)
            act.wait_ge(wsp_turned, 1)
            act.activation(wsT[:, 0:512], sc[1][:, :], ACT.Copy)
            act.activation(wsT[:, 512:1024], sc[2][:, :], ACT.Copy).then_inc(wsT_ready, 1)
            for k in range(KD):
                high_of(n2[k % 2][:, :], h_high, k, h32_ready, k + 1, h_high_ready)

            def v_pair(i, first):
                for s in range(2):
                    next_high(i, s, 4 * i + 2 * s)
                    for t in range(2):
                        act.wait_ge(tile_ready, 4 * i + (2 * s + t + 1))
                        if not (first and s == 0):
                            act.wait_ge(v_turned, 4 * i + (2 * s + t - 1))
                        act.activation(v_gel[t][:, :], acc[t][:, :], ACT.Gelu_apprx_tanh).then_inc(evac[t], 1)

            v_pair(0, True)
            with act.Fori(1, 4) as i:
                v_pair(i, False)
            act.wait_ge(v_stored, AN)
            act.wait_ge(ada_used, 3 * KD)
            for t in range(TT):
                ins = act.activation(junk[t][:, :].rearrange("p (n e) -> p n e", e=P),
                                     v_tok[:, :].rearrange("p (n c e) -> p n c e", c=TT, e=P)[:, :, t, :],
                                     ACT.Square, accum_out=tiny[:, V_SS + t:V_SS + t + 1])
            ins.then_inc(v_sq, 1)
            act.wait_ge(v_ms, 1)
            act.activation(tiny[:, V_RT:V_RT + 4], tiny[:, V_MS:V_MS + 4], ACT.Sqrt).then_inc(v_root, 1)

            q0, t0 = C0["uz"] // 2, T0["uz"]
            with act.Fori(0, 8) as i:
                for j in range(2):
                    next_high(i + q0, j, 4 * i + (t0 + 2 * j))
                    act.wait_ge(tile_ready, 4 * i + (t0 + 2 * j + 1))
                    act.activation(ug[j][:, :], acc[0][:, :], ACT.Gelu_apprx_tanh).then_inc(evac[0], 1)
                    act.wait_ge(tile_ready, 4 * i + (t0 + 2 * j + 2))
                    act.activation(zs[j][:, :], acc[1][:, :], ACT.Silu).then_inc(evac[1], 1)
                    high_of(y32[j][:, :], b_high, 2 * i + j, y32_ready, 2 * i + (j + 1), y_high_ready)

            q0, t0 = C0["ao"] // 2, T0["ao"]
            with act.Fori(0, 4) as i:
                for s in range(2):
                    next_high(i + q0, s, 2 * i + (t0 + s))
                    act.wait_ge(evac[s], i + (t0 // 2 + 1))
                    square(seg(xT, (2 * i + s) * T, T), s, 1, 2 * i + s)
            root(1)
            act.wait_ge(tile_ready, TILES_END["ao"])
            for k in range(KD):
                high_of(n2[k % 2][:, :], b_high, k, h32_ready, KD + k + 1, h_high_ready)

            for m in range(6):
                next_high(C0["kv"] // 2 + m // 2, m % 2, T0["kv"] + 2 * m)
                if 1 <= m <= 3:
                    for j in range(2):
                        act.wait_ge(k_ms_ready, 2 * (m - 1) + j + 1)
                        act.activation(k_rt[j][:, :], k_ms[j][:, :], ACT.Sqrt).then_inc(k_root, 1)
                for t in range(2):
                    act.wait_ge(tile_ready, T0["kv"] + 2 * m + t + 1)
                    if m < 3:
                        if m > 0:
                            act.wait_ge(k_done, 2 * (m - 1) + t + 1)
                        act.activation(k_raw[t][:, :], acc[t][:, :], ACT.Copy)
                        act.activation(k_sq[t][:, :], acc[t][:, :], ACT.Square).then_inc(evac[t], 1)
                    else:
                        n = 2 * (m - 3) + t
                        if n >= 2:
                            act.wait_ge(v1_turned, n - 1)
                        act.activation(v_raw[t][:, :], acc[t][:, :], ACT.Copy).then_inc(evac[t], 1)
                if m < 4:
                    for k in (2 * m, 2 * m + 1):
                        high_of(n2[k % 2][:, :], h_high, k, h32_ready, 2 * KD + k + 1, h_high_ready)

            q0, t0 = C0["qz"] // 2, T0["qz"]

            def head_bias(a):
                if not isinstance(a, int) or a > 0:
                    act.wait_ge(scores_taken, 4 * a)
                for g in range(GROUPS):
                    part = slice(DIST_AT[g], DIST_AT[g] + DIST_W[g])
                    ins = act.activation(bias[:, part], dist[:, part], ACT.Identity, scale=seg(slopes, a + g * NQ, 1))
                ins.then_inc(bias_ready, 1)

            def store_g0(a, r):
                qt = TT - 1 - r
                n = min(2, qt + 1)
                act.wait_ge(p_turned, 12 * a + (3 * r + 1))
                if a > 0:
                    act.wait_ge(pv_ready, a)
                o = (qt - 1) * 256 + P if qt > 0 else 0
                act.activation(pT[:, o:o + n * P], tr[3 * r % 2][:, 0:n * P], ACT.Copy).then_inc(p_stored[3 * r % 2], 1)

            def store_g2(a, r):
                qt = TT - 1 - r
                e = 3 * r + 2
                act.wait_ge(p_turned, 12 * a + (e + 1))
                if not isinstance(a, int) or a > 0:
                    act.wait_ge(pv_ready, a)
                dst = pT[:, D + 4 * T:D + 8 * T].rearrange("p (k i) -> p k i", i=T)[:, 0:qt + 1, qt * P:(qt + 1) * P]
                act.activation(dst, tr[e % 2][:, 0:(qt + 1) * P].rearrange("p (k i) -> p k i", i=P), ACT.Copy)\
                   .then_inc(p_stored[e % 2], 1)

            def leave(s, n):
                j = s % 2
                act.wait_ge(tile_ready, 4 * s + (t0 + n + 1))
                if n == 0 and s > 0:
                    act.wait_ge(scores_ready, 4 * s - 4)
                    act.wait_ge(qsq_summed, s)
                if n < 3:
                    act.activation(qT[j][n][:, :], acc[n % 2][:, :], ACT.Copy)
                    act.activation(q_sq[n][:, :], acc[n % 2][:, :], ACT.Square).then_inc(evac[n % 2], 1)
                else:
                    if s > 1:
                        act.wait_ge(o_taken, s - 1)
                    act.activation(zb[j][:, :], acc[1][:, :], ACT.Silu).then_inc(evac[1], 1)

            for s in range(NQ + 1):
                for n in range(4):
                    if s < NQ and n == 3:
                        act.wait_ge(qms_ready, s + 1)
                        act.activation(tiny[:, Q_RT:Q_RT + 12], tiny[:, Q_MS:Q_MS + 12], ACT.Sqrt).then_inc(q_root, 1)
                    if s > 0 and n > 0:
                        store_g0(s - 1, n - 1)
                    elif s > 1:
                        store_g0(s - 2, 3)
                    if s > 0:
                        w = (min(2, TT - n) + 2 * (TT - n)) * P
                        act.wait_ge(top_ready, 4 * (s - 1) + (n + 1))
                        act.activation(s_row[n % 2][:, 0:w], s_row[n % 2][:, 0:w], ACT.Exp,
                                       bias=tiny[:, NM + n % 2:NM + n % 2 + 1],
                                       accum_out=tiny[:, LS + n % 2:LS + n % 2 + 1]).then_inc(p_ready, 1)
                    if s < NQ:
                        leave(s, n)
                    if s > 0 and n > 0:
                        store_g2(s - 1, n - 1)
                    elif s > 1:
                        store_g2(s - 2, 3)
                    if s < NQ and n % 2 == 0:
                        next_high(s + q0, n // 2, 4 * s + (t0 + n))
                if s < NQ:
                    if s == 0:
                        act.wait_ge(dist_ready, GROUPS)
                    head_bias(s)
            store_g0(NQ - 1, 3)
            store_g2(NQ - 1, 3)
            for k in range(KD):
                high_of(yb[:, k * T:(k + 1) * T], h_high, k, o_taken, k + 1, h_high_ready)

            q0, t0 = C0["bo"] // 2, T0["bo"]
            for m in range(4):
                next_high(q0 + m // 2, m % 2, t0 + 2 * m)
                for t in range(2):
                    n = 2 * m + t
                    act.wait_ge(evac[t], t0 // 2 + m + 1)
                    square(xT[:, n * T:(n + 1) * T], t, 2, n)

            def apply(base, hbase):
                for k in range(KD):
                    high_of(n2[k % 2][:, :], h_high, k, h32_ready, base + k + 1, h_high_ready)

            def squares_of_x(n, base):
                for k in range(KD):
                    act.wait_ge(x_updated, base + k + 1)
                    square(xT[:, k * T:(k + 1) * T], k % 2, n, k)

            def highs_of_x(gain, group, wait, n=None):
                for k in range(KD):
                    x_k = xT[:, k * T:(k + 1) * T]
                    wait(k)
                    act.activation(h_high[:, k * T:(k + 1) * T], x_k, ACT.Copy, scale=col(gain, k)).then_inc(h_high_ready, 1)
                    if n is not None:
                        square(x_k, k % 2, n, k)

            def ffn(l, nb, n_in):
                h0 = (l - 1) * (FFA + FFB)
                for part, nk in (("a", FFA), ("b", FFB)):
                    q0, t0 = C0[f"gu{l}{part}"] // 2, T0[f"gu{l}{part}"]
                    hb = h0 + (FFA if part == "b" else 0)

                    def hidden(i, first=False):
                        for s in range(2):
                            next_high(i + q0, s, 4 * i + (t0 + 2 * s))
                            if first and s == 0:
                                root(n_in)
                            act.wait_ge(evac[0], 2 * i + (t0 // 2 + s + 1))
                            act.activation(sg[s][:, :], sg[s][:, :], ACT.Silu).then_inc(silu_ready, 1)
                            high_of(hd[s][:, :], b_high, 2 * i + s, hid32_ready, 2 * i + (hb + s + 1), hid_high_ready)

                    if part == "a":
                        hidden(0, first=True)
                    with act.Fori(1 if part == "a" else 0, nk // 2) as i:
                        hidden(i)
                    q0, t0 = C0[f"dn{l}{part}"] // 2, T0[f"dn{l}{part}"]
                    if part == "a":
                        with act.Fori(0, 4) as i:
                            for s in range(2):
                                next_high(i + q0, s, 2 * i + (t0 + s))
                                act.wait_ge(tile_ready, 2 * i + (t0 + s + 1))
                                act.activation(seg(f, (2 * i + s) * T, T), acc[s][:, :], ACT.Copy).then_inc(evac[s], 1)

                def down(i, last=False):
                    for s in range(2):
                        if not (last and s == 1):
                            next_high(i + q0, s, 2 * i + (t0 + s))
                        act.wait_ge(evac[s], i + (t0 // 2 + 1))
                        square(seg(f, (2 * i + s) * T, T), s, nb, 2 * i + s)

                with act.Fori(0, 3) as i:
                    down(i)
                down(3, last=(l == 2))
                root(nb)

            highs_of_x("ffn1_norm_pre_2", 4, lambda k: act.wait_ge(tile_ready, TILES_END["bo"]))
            ffn(1, 3, 2)
            squares_of_x(4, 0)
            root(4)
            apply(3 * KD, 5 * KD)

            q0, t0 = C0["mix"] // 2, T0["mix"]
            for m in range(4):
                next_high(q0 + m // 2, m % 2, t0 + 2 * m)
                act.wait_ge(tile_ready, t0 + 2 * m + 2)
                if m >= 2:
                    act.wait_ge(evac[0], t0 // 2 + m - 1)
                act.activation(c_sig[m % 2][:, :], acc[1][:, :], ACT.Sigmoid, bias=col("conv_glu_bias_2", 4 + m))\
                   .then_inc(evac[1], 1)
            for m in range(6):
                next_high(q0 + 2 + m // 2, m % 2, t0 + 8 + 2 * m)
                for t in range(2):
                    act.wait_ge(tile_ready, t0 + 8 + 2 * m + t + 1)
                    n = 2 * m + t
                    if n < 8:
                        dst = (q2, k2)[n // 4][:, n % 4 * T:(n % 4 + 1) * T]
                    else:
                        dst = v2_raw[t][:, :]
                        if n >= 10:
                            act.wait_ge(v2_turned, n - 9)
                    act.activation(dst, acc[t][:, :], ACT.Copy).then_inc(evac[t], 1)

            def store2(n):
                h, qt = n // TT, n % TT
                act.wait_ge(p2_turned, n + 1)
                if h > 0:
                    act.wait_ge(pv2_ready, h)
                dst = p2T[:, :].rearrange("p (k i) -> p k i", i=T)[:, 0:qt + 1, qt * P:(qt + 1) * P]
                act.activation(dst, tr[n % 2][:, 0:(qt + 1) * P].rearrange("p (k i) -> p k i", i=P), ACT.Copy)\
                   .then_inc(p2_stored, 1)

            def output2(m):
                act.wait_ge(pv2_ready, 2 * m + 2)
                act.activation(b_high[:, m * T:(m + 1) * T], (ob, sc[2])[m % 2][:, :], ACT.Copy).then_inc(o2_high, 1)

            q0, t0 = C0["gates"] // 2, T0["gates"]

            def gate(p):
                act.wait_ge(tile_ready, t0 + p + 1)
                if p == 7:
                    act.wait_ge(conv_step, CONV * CT)
                act.activation(gates[p % 2][:, p // 2 * T:(p // 2 + 1) * T], acc[p % 2][:, :], ACT.Identity,
                               bias=col("gate_bias_2", p // 2 + 8 * (p % 2))).then_inc(evac[p % 2], 1)

            for n in range(H2 * TT):
                w = (n % TT + 1) * P
                act.wait_ge(top2_ready, n + 1)
                act.activation(s2_row[n % 2][:, 0:w], s2_row[n % 2][:, 0:w], ACT.Exp,
                               bias=tiny[:, NM + n % 2:NM + n % 2 + 1],
                               accum_out=tiny[:, LS + n % 2:LS + n % 2 + 1]).then_inc(p2_ready, 1)
                if n > 0:
                    store2(n - 1)
                if n > 8 and n % 8 == 1:
                    output2(n // 8 - 1)
                if n % 2 == 0 and n > 0:
                    gate(n // 2 - 1)
                if n % 4 == 0:
                    next_high(q0 + n // 8, n // 4 % 2, t0 + n // 2)
            store2(H2 * TT - 1)
            gate(15)
            output2(H2 // 2 - 1)

            for n in range(CT):
                act.wait_ge(ln_mean_ready, n + 1)
                if n >= 2:
                    act.wait_ge(ln_sq_summed, n - 1)
                act.activation(ln[n % 2][:, :], cy[:, n * T:(n + 1) * T], ACT.Square).then_inc(ln_sq_ready, 1)
            act.wait_ge(ln_ms, 1)
            act.activation(ln[0][:, :], ln[2][:, :], ACT.Sqrt).then_inc(ln_root, 1)
            for n in range(CT):
                act.wait_ge(ln_out, n + 1)
                cy_n = cy[:, n * T:(n + 1) * T]
                act.activation(cy_n, cy_n, ACT.Silu, bias=col("conv_ln_b_2", n)).then_inc(conv_silu, 1)
                high_of(cy_n, b_high, 4 + n, conv_silu, n + 1, conv_high)

            for b in range(2):
                act.wait_ge(evac[b], T0["gates"] // 2 + KD)
                act.activation(gates[b][:, :], gates[b][:, :], ACT.Sigmoid).then_inc(gates_ready, 1)
            q0, t0 = C0["outs"] // 2, T0["outs"]
            with act.Fori(0, 2) as i:
                for s in range(2):
                    next_high(i + q0, s, 8 * i + (t0 + 4 * s))
                    for j in range(2):
                        n = 4 * i + (2 * s + j)
                        high_of(m32[:, :], h_high, n, m32_ready, n + 1, m_high)

            q0, t0 = C0["wo"] // 2, T0["wo"]
            for m in range(4):
                next_high(q0 + m // 2, m % 2, t0 + 2 * m)
                for t in range(2):
                    n = 2 * m + t
                    act.wait_ge(tile_ready, t0 + n + 1)
                    square(acc[t][:, :], t, 5, n)
                    act.activation(f[:, n * T:(n + 1) * T], acc[t][:, :], ACT.Copy).then_inc(evac[t], 1)
            root(5)
            highs_of_x("ffn2_norm_pre_2", 6, lambda k: act.wait_ge(x_updated, KD + k + 1), n=6)
            ffn(2, 7, 6)
            for h, t in [(0, t) for t in range(TT)] + [(1, 0), (1, 2)]:
                act.wait_ge(out_turned, TT * h + t + 1)
                act.activation(o_tok[:, t * D + h * T:t * D + (h + 1) * T], out_bank[h][t][:, :], ACT.Copy)\
                   .then_inc(out_copied[0], 1)

        @block.vector
        def _(dve):
            own = Chain(dve, dve_own)

            def low_part(q, s):
                dve.wait_ge(w_high_ready, 2 * q + (s + 1))
                w = slice(s * SLOT, (s + 1) * SLOT)
                dve.tensor_tensor(w_low[:, w], raw[:, w], w_high[:, w].bitcast(F32), ALU.subtract).then_inc(w_ready, 1)

            def next_low(q, s):
                if s == 0:
                    low_part(q, 1)
                else:
                    low_part(q + 1, 0)

            def low_of(src, high, low, k, ready, at_least, done):
                dve.wait_ge(ready, at_least)
                dve.tensor_tensor(seg(low, k * T, T), src, seg(high, k * T, T).bitcast(F32), ALU.subtract)\
                   .then_inc(done, 1)

            def clear_sum():
                own.done(dve.memset(acc_sq[:, :], 0.0))

            def add_square(n, m, j):
                dve.wait_ge(sq_ready, m + (KD * n + 1))
                if not isinstance(m, int) or KD * n + m > 0:
                    dve.wait_ge(sq_added, m + KD * n)
                dve.tensor_tensor(acc_sq[:, :], acc_sq[:, :], sq[j][:, :], ALU.add).then_inc(sq_added, 1)

            def mean_square(n):
                if n in PE_NORMS:
                    dve.wait_ge(sq_added, KD * (n + 1))
                else:
                    dve.wait_ge(stat_ready, stats_before(n) + 1)
                dve.tensor_scalar(n1[0][:, :], misc[:, :], 1.0 / D, EPS, ALU.mult, ALU.add).then_inc(ms_ready, 1)

            def reciprocal_root(n):
                mean_square(n)
                rstd_of(n)

            def rstd_of(n):
                dve.wait_ge(root_ready, n + 1)
                own.done(dve.reciprocal(rstd[:, :], n1[1][:, :]))

            def apply(hbase, scale, shift, high, low, tiles=range(KD)):
                for k in tiles:
                    if k >= 2:
                        dve.wait_ge(h_high_ready, hbase + k - 1)
                        dve.wait_ge(h_ready, hbase + k - 1)
                    x_k = xT[:, k * T:(k + 1) * T]
                    if shift is None:
                        dve.scalar_tensor_tensor(out=n2[k % 2][:, :], in0=x_k, scalar=scale(k), in1=rstd[:, :],
                                                 op0=ALU.mult, op1=ALU.mult).then_inc(h32_ready, 1)
                    else:
                        own.done(dve.scalar_tensor_tensor(out=n1[k % 2][:, :], in0=x_k, scalar=scale(k), in1=rstd[:, :],
                                                          op0=ALU.mult, op1=ALU.mult))
                        dve.tensor_scalar(n2[k % 2][:, :], n1[k % 2][:, :], shift(k), None, ALU.add).then_inc(h32_ready, 1)
                    if k > tiles[0]:
                        low_of(n2[(k - 1) % 2][:, :], high, low, k - 1, h_high_ready, hbase + k, h_ready)
                k = tiles[-1]
                low_of(n2[k % 2][:, :], high, low, k, h_high_ready, hbase + k + 1, h_ready)

            def ada_block(table, bufs, b, k0, nk, sums_taken=None):
                for k in range(k0, k0 + nk):
                    dve.wait_ge(ada_landed[k % 4], b * 32 + 16 * (k // 4 + 1))
                    ck = tiny[:, 64 + k:65 + k]
                    if k == 0:
                        if sums_taken is not None:
                            dve.wait_ge(ada_read, sums_taken)
                        dve.tensor_scalar(table[:, :], bufs[0][:, :], ck, None, ALU.mult).then_inc(ada_used, 1)
                    else:
                        dve.wait_ge(ada_used, b * KD + k)
                        dve.scalar_tensor_tensor(out=table[:, :], in0=bufs[k % 4][:, :], scalar=ck, in1=table[:, :],
                                                 op0=ALU.mult, op1=ALU.add).then_inc(ada_used, 1)

            def ada_columns(n0, n1_, read):
                dve.wait_ge(ada_read, read)
                b0 = COL["a_ada_b"]
                dve.tensor_tensor(ada[:, n0:n1_], ob[:, n0:n1_], cols[:, b0 + n0:b0 + n1_], ALU.add).then_inc(ada_cols, 1)

            def scale_columns(dst, scale0, norm):
                own.done(dve.scalar_tensor_tensor(out=derived[:, dst:dst + KD], in0=ada[:, scale0:scale0 + KD], scalar=1.0,
                                                  in1=cols[:, COL[norm]:COL[norm] + KD], op0=ALU.add, op1=ALU.mult))

            def derived_col(n):
                return derived[:, n:n + 1]

            def ada_col(n):
                return ada[:, n:n + 1]

            dve.wait_ge(c_ready, 1)
            ada_block(ada_acc[0], ada_w, 0, 0, KD)
            dve.wait_ge(rows_turned, 1)
            for j, n in enumerate(ROW_COUNTS):
                ins = dve.tensor_copy(cols[:, j * P:j * P + n], sc[0][:, j * P:j * P + n])
            ins.then_inc(cols_ready, 1)
            dve.wait_ge(rel_landed, 16)
            dve.tensor_copy(relrow[:, REL:3 * P], relrow[:, REL - 1:REL].broadcast_to([H2, 3 * P - REL])).then_inc(rel_padded, 1)
            dve.wait_ge(cols_ready, 1)
            own.done(dve.scalar_tensor_tensor(out=derived[:, SC_K:SC_K + 1], in0=col("k_norm_g"), scalar=float(P) ** -0.5,
                                              in1=col("b_q_norm_g"), op0=ALU.mult, op1=ALU.mult))
            for dst, name in ((HG1, "ffn1_norm_post_2"), (HG2, "ffn2_norm_post_2")):
                own.done(dve.tensor_scalar(derived[:, dst:dst + KD], cols[:, COL[name]:COL[name] + KD], 0.5, None, ALU.mult))
            ada_block(ada_acc[1], ada_w, 1, 0, KD)
            low_part(0, 0)
            reciprocal_root(0)
            ada_columns(0, 16, 2)
            dve.wait_ge(ada_cols, 1)
            scale_columns(A_A, SHIFT_A + KD, "a_norm_g")
            apply(0, lambda k: derived_col(A_A + k), lambda k: ada_col(SHIFT_A + k), h_high, h_low)

            own.done(dve.memset(ada_acc[0][:, :], 0.0))
            with dve.Fori(0, 2) as i:
                for m in range(4):
                    next_low(2 * i + m // 2, m % 2)
                    dve.wait_ge(ada_landed[m], 16 * i + 80)
                    dve.wait_ge(ada_used, 4 * i + (2 * KD + m))
                    dve.scalar_tensor_tensor(out=ada_acc[0][:, :], in0=ada_w[m][:, :], scalar=seg(tiny, 4 * i + (64 + m), 1),
                                             in1=ada_acc[0][:, :], op0=ALU.mult, op1=ALU.add).then_inc(ada_used, 1)
                    for t in range(2):
                        n = 8 * i + (2 * m + t)
                        dve.wait_ge(v_turned, n + 1)
                        dve.tensor_copy(seg(v_tok, n * T, T), sc[1 + t][:, :]).then_inc(v_stored, 1)
            ada_columns(16, 24, 3)
            dve.wait_ge(v_sq, 1)
            dve.tensor_scalar(tiny[:, V_MS:V_MS + 4], tiny[:, V_SS:V_SS + 4], 1.0 / AW, EPS, ALU.mult, ALU.add).then_inc(v_ms, 1)
            dve.wait_ge(v_root, 1)
            dve.reciprocal(tiny[:, V_R:V_R + 4], tiny[:, V_RT:V_RT + 4]).then_inc(mix_taken, 1)
            dve.wait_ge(mix_taken, 1)
            dve.wait_ge(bsb_landed, 16)
            dve.wait_ge(wsT_ready, 1)

            def ada_tile(b, k):
                ck = tiny[:, 64 + k:65 + k]
                dve.wait_ge(ada2_landed[k % 2], b * 64 + (16 * (k // 2 + 1) - 3 * 64))
                if k == 0:
                    dve.wait_ge(ada_read, b)
                    dve.tensor_scalar(ada2_acc[:, :], ada2_w[0][:, :], ck, None, ALU.mult).then_inc(ada_used, 1)
                else:
                    dve.wait_ge(ada_used, b * KD + k)
                    dve.scalar_tensor_tensor(out=ada2_acc[:, :], in0=ada2_w[k % 2][:, :], scalar=ck, in1=ada2_acc[:, :],
                                             op0=ALU.mult, op1=ALU.add).then_inc(ada_used, 1)

            q0, t0 = C0["uz"] // 2, T0["uz"] // 2
            def normed(n, i, m):
                if m % 2 == 0:
                    dve.wait_ge(mix_taken, n + 1)
                    dve.tensor_copy(ws[:, :], seg(wsT, i * 256 + m // 2 * P, P)).then_inc(ws_ready, 1)
                dve.tensor_tensor(vs[m % 2][:, :].rearrange("p (c e) -> p c e", e=P),
                                  seg(v_tok, n * T, T).rearrange("p (c e) -> p c e", e=P),
                                  tiny[:, V_R:V_R + 4].rearrange("p (c e) -> p c e", e=1).broadcast_to([P, TT, P]),
                                  ALU.mult).then_inc(vs_ready, 1)

            with dve.Fori(0, 4) as i:
                own.enter(i, 4)
                for m in range(4):
                    j, n = m % 2, 4 * i + m
                    if m == 0:
                        normed(n, i, m)
                    if m == 3:
                        ada_tile(i + 3, 6)
                    next_low(2 * i + (q0 + m // 2), j)
                    if m == 3:
                        ada_tile(i + 3, 7)
                    dve.wait_ge(mix_ready, n + 1)
                    dve.scalar_tensor_tensor(out=vs[j][:, :].rearrange("p (c e) -> p c e", e=P),
                                             in0=sc[1 + j][:, :].rearrange("p (c e) -> p c e", e=P),
                                             scalar=col("a_sgu_g", n),
                                             in1=seg(bsb, i * 256 + m // 2 * P, P)[:, None, :].broadcast_to([P, TT, P]),
                                             op0=ALU.mult, op1=ALU.add).then_inc(mix_taken, 1)
                    dve.wait_ge(mix_taken, n + 2)
                    if m < 3:
                        normed(n + 1, i, m + 1)
                    dve.wait_ge(evac[0], n + (t0 + 1))
                    own.done(dve.tensor_tensor(vs[j][:, :], vs[j][:, :], ug[j][:, :], ALU.mult))
                    if m < 3:
                        ada_tile(i + 3, 2 * m)
                    dve.wait_ge(evac[1], n + (t0 + 1))
                    dve.tensor_tensor(y32[j][:, :], vs[j][:, :], zs[j][:, :], ALU.mult).then_inc(y32_ready, 1)
                    low_of(y32[j][:, :], b_high, b_low, n, y_high_ready, n + 1, y_ready)
                    if m < 3:
                        ada_tile(i + 3, 2 * m + 1)
                own.leave(4)

            def residual(tq, s, m, gate):
                dve.wait_ge(tile_ready, tq)
                x_m = seg(xT, m * T, T)
                dve.scalar_tensor_tensor(out=x_m, in0=acc[s][:, :], scalar=seg(ada, m + gate, 1), in1=x_m,
                                         op0=ALU.mult, op1=ALU.add).then_inc(evac[s], 1)

            ada_columns(24, 56, 7)
            dve.wait_ge(ada_cols, 3)
            scale_columns(A_KV, SHIFT_KV + KD, "kv_norm_g")
            scale_columns(A_B, SHIFT_B + KD, "b_norm_g")

            q0, t0 = C0["ao"] // 2, T0["ao"]
            clear_sum()
            own.done(dve.memset(ada3_acc[:, :], 0.0))
            with dve.Fori(0, 4) as i:
                for s in range(2):
                    next_low(i + q0, s)
                    dve.wait_ge(ada2_landed[s], 16 * i + (4 * 64 + 16))
                    dve.wait_ge(ada_used, 2 * i + (7 * KD + s))
                    dve.scalar_tensor_tensor(out=ada3_acc[:, :], in0=ada2_w[s][:, :], scalar=seg(tiny, 2 * i + (64 + s), 1),
                                             in1=ada3_acc[:, :], op0=ALU.mult, op1=ALU.add).then_inc(ada_used, 1)
                    residual(2 * i + (t0 + s + 1), s, 2 * i + s, GATE_A)
                    add_square(1, 2 * i + s, s)
            reciprocal_root(1)
            dve.wait_ge(tile_ready, TILES_END["ao"])
            apply(KD, lambda k: derived_col(A_KV + k), lambda k: ada_col(SHIFT_KV + k), b_high, b_low)
            ada_columns(56, 64, 8)

            def kv_after(m):
                if m < 3:
                    for j in range(2):
                        dve.wait_ge(k_stat, 2 * m + j + 1)
                        dve.tensor_scalar(k_ms[j][:, :], (misc, tr[0])[j][:, :], 1.0 / P, EPS, ALU.mult, ALU.add)\
                           .then_inc(k_ms_ready, 1)
                    for j in range(2):
                        dve.wait_ge(k_root, 2 * m + j + 1)
                        own.done(dve.reciprocal(k_rt[j][:, :], k_rt[j][:, :]))
                        n = 2 * m + j
                        dve.scalar_tensor_tensor(out=kT[:, n * T:(n + 1) * T], in0=k_raw[j][:, :],
                                                 scalar=derived_col(SC_K), in1=k_rt[j][:, :],
                                                 op0=ALU.mult, op1=ALU.mult).then_inc(k_done, 1)
                else:
                    for j in range(2):
                        n = 2 * (m - 3) + j
                        dve.wait_ge(v1_turned, n + 1)
                        dve.tensor_copy(v1[:, :].rearrange("p (k h d) -> p k h d", h=KVH, d=P)[:, :, n, :],
                                        sc[1 + j][:, :].rearrange("p (k d) -> p k d", d=P)).then_inc(v1_stored, 1)

            for m in range(6):
                next_low(C0["kv"] // 2 + m // 2, m % 2)
                if m > 0:
                    kv_after(m - 1)
                if m < 4:
                    apply(2 * KD, lambda k: derived_col(A_B + k), lambda k: ada_col(SHIFT_B + k), h_high, h_low,
                          range(2 * m, 2 * m + 2))
            kv_after(5)

            dve.wait_ge(dist_int, 2)
            for g in (1, 2):
                part = slice(DIST_AT[g], DIST_AT[g] + DIST_W[g])
                i32 = mybir.dt.int32
                own.done(dve.tensor_scalar(dist[:, part].bitcast(i32), bias[:, part].bitcast(i32), DILATION[g] - 1, None,
                                           ALU.bitwise_and))
                own.done(dve.tensor_scalar(dist[:, part], dist[:, part].bitcast(i32), 0.0, MASKED, ALU.is_gt, ALU.mult))
                dve.scalar_tensor_tensor(out=dist[:, part], in0=bias[:, part].bitcast(i32), scalar=-1.0,
                                         in1=dist[:, part], op0=ALU.mult, op1=ALU.add).then_inc(dist_thinned, 1)

            q0, t0 = C0["qz"] // 2, T0["qz"]

            def store_g1(a, r):
                qt = TT - 1 - r
                e = 3 * r + 1
                dve.wait_ge(p_turned, 12 * a + (e + 1))
                if a > 0:
                    dve.wait_ge(pv_ready, a)
                dst = pT[:, D:D + 4 * T].rearrange("p (k i) -> p k i", i=T)[:, 0:qt + 1, qt * P:(qt + 1) * P]
                dve.tensor_copy(dst, tr[e % 2][:, 0:(qt + 1) * P].rearrange("p (k i) -> p k i", i=P))\
                   .then_inc(p_stored[e % 2], 1)

            def tops(a, j, r):
                qt = TT - 1 - r
                b = r % 2
                dve.wait_ge(scores_ready, 4 * a + (r + 1))
                if 4 * a + r >= 2:
                    dve.wait_ge(p_turned, 3 * (4 * a + r - 1))
                if r == 0:
                    dve.wait_ge(bias_ready, a + 1)
                at_ = 0
                for g in range(GROUPS):
                    w = (min(2, qt + 1) if g == 0 else qt + 1) * P
                    d0 = DIST_AT[g] + DIST_W[g] - w
                    qr = Q_R + 12 * j + g * TT + qt
                    ins = dve.scalar_tensor_tensor(out=s_row[b][:, at_:at_ + w], in0=sc[g][:, DIST_W[g] - w:DIST_W[g]],
                                                   scalar=tiny[:, qr:qr + 1], in1=bias[:, d0:d0 + w],
                                                   op0=ALU.mult, op1=ALU.add)
                    at_ += w
                ins.then_inc(scores_taken, 1)
                dve.wait_ge(scores_taken, 4 * a + (r + 1))
                own.done(dve.tensor_reduce(tiny[:, MX + b:MX + b + 1], s_row[b][:, 0:at_], AX, ALU.max))
                dve.tensor_scalar(tiny[:, NM + b:NM + b + 1], tiny[:, MX + b:MX + b + 1], -1.0, None, ALU.mult)\
                   .then_inc(top_ready, 1)

            def scale(a, r):
                b = r % 2
                at_ = (min(2, TT - r) + 2 * (TT - r)) * P
                dve.wait_ge(p_ready, 4 * a + (r + 1))
                own.done(dve.reciprocal(tiny[:, LI + b:LI + b + 1], tiny[:, LS + b:LS + b + 1]))
                dve.tensor_scalar(s_row[b][:, 0:at_], s_row[b][:, 0:at_], tiny[:, LI + b:LI + b + 1], None, ALU.mult)\
                   .then_inc(p_scaled, 1)

            def output(a):
                dve.wait_ge(pv_ready, a + 1)
                dve.tensor_tensor(yb[:, a * T:(a + 1) * T], ob[:, :], zb[a % 2][:, :], ALU.mult).then_inc(o_taken, 1)

            for s in range(NQ + 1):
                for n in range(4):
                    before = (s - 1, n - 1) if n > 0 else (s - 2, 3)
                    if before[0] >= 0:
                        scale(*before)
                    if s < NQ and n == 3:
                        dve.wait_ge(qsq_summed, s + 1)
                        dve.tensor_scalar(tiny[:, Q_MS:Q_MS + 12], ob[:, 480:492], 1.0 / P, EPS, ALU.mult, ALU.add)\
                           .then_inc(qms_ready, 1)
                    if s > 1 and n == 1:
                        output(s - 2)
                    if s > 0:
                        tops(s - 1, (s - 1) % 2, n)
                    if before[0] >= 0:
                        store_g1(*before)
                    if s < NQ and n == 3:
                        dve.wait_ge(q_root, s + 1)
                        dve.reciprocal(tiny[:, Q_R + 12 * (s % 2):Q_R + 12 * (s % 2) + 12], tiny[:, Q_RT:Q_RT + 12])\
                           .then_inc(qr_ready, 1)
                    if s < NQ and n % 2 == 0:
                        next_low(s + q0, n // 2)
            scale(NQ - 1, 3)
            store_g1(NQ - 1, 3)
            output(NQ - 1)
            for k in range(KD):
                low_of(yb[:, k * T:(k + 1) * T], h_high, h_low, k, h_high_ready, 3 * KD + k + 1, h_ready)

            q0, t0 = C0["bo"] // 2, T0["bo"]
            dve.wait_ge(ada_cols, 4)
            clear_sum()
            for m in range(4):
                next_low(q0 + m // 2, m % 2)
                for t in range(2):
                    residual(t0 + 2 * m + t + 1, t, 2 * m + t, GATE_B)
                    add_square(2, 2 * m + t, t)

            def low_of_x(gain, group, k):
                dve.wait_ge(h_high_ready, group * KD + k + 1)
                dve.scalar_tensor_tensor(out=h_low[:, k * T:(k + 1) * T], in0=xT[:, k * T:(k + 1) * T], scalar=col(gain, k),
                                         in1=h_high[:, k * T:(k + 1) * T].bitcast(F32), op0=ALU.mult, op1=ALU.subtract)\
                   .then_inc(h_ready, 1)

            def ffn(l, nb, n_in):
                h0 = (l - 1) * (FFA + FFB)
                for part, nk in (("a", FFA), ("b", FFB)):
                    q0, t0 = C0[f"gu{l}{part}"] // 2, T0[f"gu{l}{part}"]
                    hb = h0 + (FFA if part == "b" else 0)

                    def hidden(i, first=False):
                        for s in range(2):
                            n = 2 * i + s
                            if first and s == 0:
                                mean_square(n_in)
                                next_low(i + q0, s)
                                rstd_of(n_in)
                            else:
                                next_low(i + q0, s)
                            dve.wait_ge(tile_ready, 2 * n + (t0 + 1))
                            dve.tensor_tensor(sg[s][:, :], rstd[:, :], acc[0][:, :], ALU.mult).then_inc(evac[0], 1)
                            dve.wait_ge(tile_ready, 2 * n + (t0 + 2))
                            dve.tensor_tensor(hd[s][:, :], rstd[:, :], acc[1][:, :], ALU.mult).then_inc(evac[1], 1)
                            dve.wait_ge(evac[1], n + (t0 // 2 + 1))
                            dve.wait_ge(silu_ready, n + (hb + 1))
                            dve.tensor_tensor(hd[s][:, :], sg[s][:, :], hd[s][:, :], ALU.mult).then_inc(hid32_ready, 1)
                            low_of(hd[s][:, :], b_high, b_low, n, hid_high_ready, n + (hb + 1), hid_ready)

                    if part == "a":
                        hidden(0, first=True)
                    with dve.Fori(1 if part == "a" else 0, nk // 2) as i:
                        hidden(i)
                    q0, t0 = C0[f"dn{l}{part}"] // 2, T0[f"dn{l}{part}"]
                    if part == "a":
                        with dve.Fori(0, 4) as i:
                            for s in range(2):
                                next_low(i + q0, s)
                clear_sum()

                def down(i, last=False):
                    for s in range(2):
                        if not (last and s == 1):
                            next_low(i + q0, s)
                        dve.wait_ge(tile_ready, 2 * i + (t0 + s + 1))
                        f_m = seg(f, (2 * i + s) * T, T)
                        dve.tensor_tensor(f_m, f_m, acc[s][:, :], ALU.add).then_inc(evac[s], 1)
                        add_square(nb, 2 * i + s, s)

                with dve.Fori(0, 3) as i:
                    down(i)
                down(3, last=(l == 2))
                reciprocal_root(nb)

            def add_normed(gain, base, n=None, low=None):
                for k in range(KD):
                    x_k = xT[:, k * T:(k + 1) * T]
                    own.done(dve.scalar_tensor_tensor(out=n1[k % 2][:, :], in0=f[:, k * T:(k + 1) * T], scalar=gain(k),
                                                      in1=rstd[:, :], op0=ALU.mult, op1=ALU.mult))
                    dve.tensor_tensor(x_k, x_k, n1[k % 2][:, :], ALU.add).then_inc(x_updated, 1)
                    if low is not None and k > 0:
                        low(k - 1)
                dve.wait_ge(x_updated, base + KD)
                if low is not None:
                    low(KD - 1)
                if n is not None:
                    reciprocal_root(n)

            for k in range(KD):
                low_of_x("ffn1_norm_pre_2", 4, k)
            ffn(1, 3, 2)
            add_normed(lambda k: derived_col(HG1 + k), 0, 4)
            apply(5 * KD, lambda k: col("mix_norm_pre_2", k), None, h_high, h_low)

            q0, t0 = C0["mix"] // 2, T0["mix"]
            dve.wait_ge(h_ready, 6 * KD)
            dve.memset(glu[:, :].rearrange("p (n t) -> p n t", t=GW)[:, :, 0:PAD], 0.0).then_inc(toep_free, 1)
            dve.wait_ge(toep_free, 1)
            for m in range(4):
                next_low(q0 + m // 2, m % 2)
                dve.wait_ge(evac[1], t0 // 2 + m + 1)
                dve.scalar_tensor_tensor(out=glu[:, m * GW + PAD:(m + 1) * GW], in0=acc[0][:, :],
                                         scalar=col("conv_glu_bias_2", m), in1=c_sig[m % 2][:, :],
                                         op0=ALU.add, op1=ALU.mult).then_inc(evac[0], 1)
            dve.wait_ge(evac[0], t0 // 2 + 4)

            def tap(i, n):
                cy_n = cy[:, n * T:(n + 1) * T]
                dve.scalar_tensor_tensor(out=cy_n, in0=seg(glu, i + n * GW, T), scalar=col("conv_dw_w_2", i * CT + n),
                                         in1=cy_n, op0=ALU.mult, op1=ALU.add).then_inc(conv_step, 1)

            for n in range(CT):
                dve.tensor_scalar(cy[:, n * T:(n + 1) * T], glu[:, n * GW:n * GW + T], col("conv_dw_w_2", n),
                                  col("conv_dw_b_2", n), ALU.mult, ALU.add).then_inc(conv_step, 1)
            taps = 3
            for m in range(6):
                next_low(q0 + 2 + m // 2, m % 2)
                with dve.Fori(0, taps) as i:
                    for n in range(CT):
                        dve.wait_ge(conv_step, i * CT + (m * taps * CT + n + 1))
                        tap(i + (m * taps + 1), n)
            for n in range(4):
                dve.wait_ge(v2_turned, n + 1)
                dve.tensor_copy(v2[:, :].rearrange("p (k d) -> p k d", d=T)[:, :, n * P:(n + 1) * P],
                                sc[1 + n % 2][:, :].rearrange("p (k d) -> p k d", d=P)).then_inc(v2_stored, 1)

            dve.wait_ge(toep_landed, 16 * H2)
            own.done(dve.memset(toep[0:CH2, :].rearrange("p (h m) -> p h m", m=REL)[:, :, 1:1 + CH2], MASKED))

            def softmax2(n):
                h, qt = n // TT, n % TT
                b = n % 2
                w = (qt + 1) * P
                near = min(2, qt + 1) * P
                dve.wait_ge(s2_ready, n + 1)
                if n >= 2:
                    dve.wait_ge(p2_turned, n - 1)
                ins = dve.scalar_tensor_tensor(out=s2_row[b][:, w - near:w], in0=sc[b][:, w - near:w], scalar=HD2 ** -0.5,
                                               in1=toep[:, h * REL + near:h * REL:-1], op0=ALU.mult, op1=ALU.add)
                if w > near:
                    ins = dve.tensor_scalar(s2_row[b][:, 0:w - near], sc[b][:, 0:w - near], HD2 ** -0.5,
                                            toep[:, h * REL + 256:h * REL + 257], ALU.mult, ALU.add)
                ins.then_inc(s2_taken, 1)
                dve.wait_ge(s2_taken, n + 1)
                own.done(dve.tensor_reduce(tiny[:, MX + b:MX + b + 1], s2_row[b][:, 0:w], AX, ALU.max))
                dve.tensor_scalar(tiny[:, NM + b:NM + b + 1], tiny[:, MX + b:MX + b + 1], -1.0, None, ALU.mult)\
                   .then_inc(top2_ready, 1)

            def scale2(n):
                b = n % 2
                w = (n % TT + 1) * P
                dve.wait_ge(p2_ready, n + 1)
                own.done(dve.reciprocal(tiny[:, LI + b:LI + b + 1], tiny[:, LS + b:LS + b + 1]))
                dve.tensor_scalar(s2_row[b][:, 0:w], s2_row[b][:, 0:w], tiny[:, LI + b:LI + b + 1], None, ALU.mult)\
                   .then_inc(p2_scaled, 1)

            def output2(m):
                dve.wait_ge(o2_high, m + 1)
                dve.tensor_tensor(b_low[:, m * T:(m + 1) * T], (ob, sc[2])[m % 2][:, :],
                                  b_high[:, m * T:(m + 1) * T].bitcast(F32), ALU.subtract).then_inc(o2_ready, 1)

            q0 = C0["gates"] // 2
            for n in range(H2 * TT):
                softmax2(n)
                if n > 0:
                    scale2(n - 1)
                if n > 8 and n % 8 == 2:
                    output2(n // 8 - 1)
                for e in range(CT * (6 * taps + 1) + 3 * n, min(CT * (6 * taps + 1) + 3 * n + 3, CT * CONV)):
                    dve.wait_ge(conv_step, e - CT + 1)
                    tap(e // CT, e % CT)
                if n % 4 == 0:
                    next_low(q0 + n // 8, n // 4 % 2)
            scale2(H2 * TT - 1)
            output2(H2 // 2 - 1)

            dve.wait_ge(ln_sum, 1)
            for n in range(CT):
                cy_n = cy[:, n * T:(n + 1) * T]
                dve.scalar_tensor_tensor(out=cy_n, in0=misc[:, :], scalar=-1.0 / (CT * P), in1=cy_n,
                                         op0=ALU.mult, op1=ALU.add).then_inc(ln_mean_ready, 1)
            dve.wait_ge(ln_sq_summed, CT)
            dve.tensor_scalar(ln[2][:, :], tr[0][:, :], 1.0 / (CT * P), EPS, ALU.mult, ALU.add).then_inc(ln_ms, 1)
            dve.wait_ge(ln_root, 1)
            own.done(dve.reciprocal(ln[1][:, :], ln[0][:, :]))
            for n in range(CT):
                cy_n = cy[:, n * T:(n + 1) * T]
                dve.scalar_tensor_tensor(out=cy_n, in0=cy_n, scalar=col("conv_ln_g_2", n), in1=ln[1][:, :],
                                         op0=ALU.mult, op1=ALU.mult).then_inc(ln_out, 1)
            for n in range(CT):
                low_of(cy[:, n * T:(n + 1) * T], b_high, b_low, 4 + n, conv_high, n + 1, conv_ready)

            q0, t0 = C0["outs"] // 2, T0["outs"]
            dve.wait_ge(gates_ready, 2)
            with dve.Fori(0, 2) as i:
                for s in range(2):
                    next_low(i + q0, s)
                    for j in range(2):
                        n = 4 * i + (2 * s + j)
                        for t in range(2):
                            dve.wait_ge(tile_ready, 2 * n + (t0 + 1 + t))
                            dve.tensor_tensor(branch[t][:, :], seg(gates[t], n * T, T), acc[t][:, :], ALU.mult)\
                               .then_inc(evac[t], 1)
                        for t in range(2):
                            dve.wait_ge(evac[t], n + (t0 // 2 + 1))
                        dve.tensor_tensor(m32[:, :], branch[0][:, :], branch[1][:, :], ALU.add).then_inc(m32_ready, 1)
                        low_of(m32[:, :], h_high, h_low, n, m_high, n + 1, m_ready)

            q0 = C0["wo"] // 2
            clear_sum()
            for m in range(4):
                next_low(q0 + m // 2, m % 2)
                for t in range(2):
                    add_square(5, 2 * m + t, t)
            reciprocal_root(5)
            for t in range(2):
                dve.wait_ge(evac[t], T0["wo"] // 2 + 4)
            add_normed(lambda k: col("mix_norm_post_2", k), KD, low=lambda k: low_of_x("ffn2_norm_pre_2", 6, k))
            ffn(2, 7, 6)
            add_normed(lambda k: derived_col(HG2 + k), 2 * KD)

            for t in (1, 3):
                dve.wait_ge(out_turned, TT + t + 1)
                dve.tensor_copy(o_tok[:, t * D + T:(t + 1) * D], out_bank[1][t][:, :]).then_inc(out_copied[1], 1)

    return nc


NAMES = ["x", "c", "a_ada_w", "a_ada_b", "a_norm_g", "a_w_in", "a_sgu_g", "a_w_spatial", "a_b_spatial", "a_w_out",
         "kv_ada_w", "kv_ada_b", "kv_norm_g", "w_kv", "k_norm_g", "b_ada_w", "b_ada_b", "b_norm_g", "b_w_in",
         "b_q_norm_g", "b_w_out", "ffn1_norm_pre_2", "ffn1_w_gate_2", "ffn1_w_up_2", "ffn1_w_down_2",
         "ffn1_norm_post_2", "mix_norm_pre_2", "w_in_2", "gate_bias_2", "rel_table_2", "w_attn_out_2",
         "conv_glu_bias_2", "conv_dw_w_2", "conv_dw_b_2", "conv_ln_g_2", "conv_ln_b_2", "conv_w_out_2", "w_out_2",
         "mix_norm_post_2", "ffn2_norm_pre_2", "ffn2_w_gate_2", "ffn2_w_up_2", "ffn2_w_down_2", "ffn2_norm_post_2"]


def kernel(**inputs):
    import concourse.bacc as bacc
    from concourse.bass_utils import run_bass_kernel_spmd

    nc = bacc.Bacc("TRN2", target_bir_lowering=False, num_devices=1)
    arrays, args = {}, {}
    for name in NAMES:
        a = np.ascontiguousarray(inputs[name])
        arrays[f"in_{name}"] = a
        args[name] = nc.dram_tensor(f"in_{name}", a.shape, mybir.dt.from_np(a.dtype), kind="ExternalInput").ap()
    out = nc.dram_tensor("out_0", (1, T, D), F32, kind="ExternalOutput").ap()
    build(nc, out=out, **args)
    r = run_bass_kernel_spmd(nc, [arrays], core_ids=[0])
    return r.results[0]["out_0"]
```
